# Optimizing a Trainium2 kernel written in Bass

```python
import math
import jax, jax.numpy as jnp
from jax import lax
import numpy as np

D_MODEL = 2048
BATCH = 1
SEQ = 512
DEPTH = 1

HEAD_DIM = 128
NSA_HEADS = 8
NSA_KV_GROUPS = 2
NSA_HPG = NSA_HEADS // NSA_KV_GROUPS
CMP_LEN = 32
CMP_STRIDE = 16
SEL_LEN = 64
SEL_TOPK = 16
WINDOW = 512
CMP_HIDDEN = 256
NSA_Q_BLOCK = 64
NSA_WIDTH = NSA_HEADS * HEAD_DIM
DIFF_HEADS = 4
DIFF_V_DIM = 2 * HEAD_DIM
DIFF_Q_BLOCK = 128
DIFF_WIDTH = DIFF_HEADS * DIFF_V_DIM
REL_BUCKETS = 32
REL_MAX_EXACT = 16
REL_MAX_DIST = 128
N_BIAS_HEADS = NSA_HEADS + DIFF_HEADS
D_FF = -(-8 * D_MODEL // (3 * 256)) * 256

EPS = 1e-6
NEG = -1e30
BIG = 1e30

SPLIT_SIZES = (
    NSA_HEADS * HEAD_DIM,
    NSA_KV_GROUPS * HEAD_DIM,
    NSA_KV_GROUPS * HEAD_DIM,
    NSA_KV_GROUPS * HEAD_DIM,
    NSA_KV_GROUPS * HEAD_DIM,
    NSA_KV_GROUPS * HEAD_DIM,
    NSA_KV_GROUPS * HEAD_DIM,
    NSA_HEADS * 3,
    DIFF_HEADS * 2 * HEAD_DIM,
    DIFF_HEADS * 2 * HEAD_DIM,
    DIFF_HEADS * DIFF_V_DIM,
    2 * D_MODEL,
)
D_IN_PROJ = int(sum(SPLIT_SIZES))
SPLIT_POINTS = tuple(int(v) for v in np.cumsum(SPLIT_SIZES)[:-1])

kernel_name = 'hybrid_nsa_diffattn_gated_block'

def rms_norm(x, g):
    xf = x.astype(jnp.float32)
    y = xf * lax.rsqrt(jnp.mean(xf * xf, axis=-1, keepdims=True) + EPS)
    return (y * g.astype(jnp.float32)).astype(x.dtype)

def masked_softmax(logits, mask):
    z = jnp.where(mask, logits, NEG)
    m = jnp.max(z, axis=-1, keepdims=True)
    e = jnp.where(mask, jnp.exp(z - m), 0.0)
    return e / jnp.maximum(jnp.sum(e, axis=-1, keepdims=True), 1e-30)

def t5_bucket(rel):
    n = jnp.maximum(rel, 0)
    nf = jnp.maximum(n, 1).astype(jnp.float32)
    large = REL_MAX_EXACT + (jnp.log(nf / REL_MAX_EXACT) / math.log(REL_MAX_DIST / REL_MAX_EXACT)
                             * (REL_BUCKETS - REL_MAX_EXACT)).astype(jnp.int32)
    large = jnp.minimum(large, REL_BUCKETS - 1)
    return jnp.where(n < REL_MAX_EXACT, n, large)

def compress_blocks(kv, pe, w1, w2):
    B, G, S, D = kv.shape
    halves = kv.reshape(B, G, S // CMP_STRIDE, CMP_STRIDE, D)
    nxt = jnp.pad(halves[:, :, 1:], ((0, 0), (0, 0), (0, 1), (0, 0), (0, 0)))
    blocks = jnp.concatenate([halves, nxt], axis=3) + pe
    hid = jax.nn.gelu(blocks.reshape(B, G, S // CMP_STRIDE, CMP_LEN * D) @ w1)
    return hid @ w2

def nsa_mixer(q, k_cmp, v_cmp, k_slc, v_slc, k_win, v_win, gates, table_nsa):
    B, G, P, S, D = q.shape
    scale = D ** -0.5
    n_cmp = S // CMP_STRIDE
    n_sel = S // SEL_LEN
    top_n = min(SEL_TOPK, n_sel)
    r_m = SEL_LEN // CMP_STRIDE
    r_n = CMP_LEN // CMP_STRIDE
    overlap = [sum(1 for m in range(r_m) for n in range(r_n) if m + n == s)
               for s in range(r_m + r_n - 1)]
    k_blk = k_slc.reshape(B, G, n_sel, SEL_LEN, D)
    v_blk = v_slc.reshape(B, G, n_sel, SEL_LEN, D)
    wpad = ((0, 0), (0, 0), (WINDOW, 0), (0, 0))
    k_wp = jnp.pad(k_win, wpad)
    v_wp = jnp.pad(v_win, wpad)
    c_end = jnp.arange(n_cmp, dtype=jnp.int32) * CMP_STRIDE + CMP_LEN - 1
    blk_ids = jnp.arange(n_sel, dtype=jnp.int32)
    sel_off = jnp.arange(SEL_LEN, dtype=jnp.int32)
    bi = jnp.arange(B)[:, None, None, None]
    gi = jnp.arange(G)[None, :, None, None]
    gi5 = gi[..., None]
    span = NSA_Q_BLOCK + WINDOW

    def block(i):
        t0 = i * NSA_Q_BLOCK
        tpos = t0 + jnp.arange(NSA_Q_BLOCK, dtype=jnp.int32)
        qb = lax.dynamic_slice_in_dim(q, t0, NSA_Q_BLOCK, axis=3)
        gb = lax.dynamic_slice_in_dim(gates, t0, NSA_Q_BLOCK, axis=3)
        rel_c = tpos[:, None] - c_end[None, :]
        bias_c = jnp.transpose(table_nsa[t5_bucket(rel_c)], (2, 3, 0, 1)).astype(jnp.float32)
        s_c = jnp.einsum('bgpqd,bgcd->bgpqc', qb, k_cmp).astype(jnp.float32) * scale + bias_c
        p_c = masked_softmax(s_c, rel_c >= 0)
        o_c = jnp.einsum('bgpqc,bgcd->bgpqd', p_c.astype(v_cmp.dtype), v_cmp)
        imp = jnp.pad(p_c.sum(axis=2), ((0, 0), (0, 0), (0, 0), (0, len(overlap) - 1)))
        p_slc = sum(w * imp[..., s: s + n_cmp: r_m] for s, w in enumerate(overlap))
        j_t = (tpos // SEL_LEN)[:, None]
        forced = (blk_ids == 0) | (blk_ids == j_t) | (blk_ids == j_t - 1)
        score = jnp.where(forced, BIG, jnp.where(blk_ids > j_t, NEG, p_slc))
        _, idx = lax.top_k(score, top_n)
        ks = k_blk[bi, gi, idx]
        vs = v_blk[bi, gi, idx]
        spos = idx[..., None] * SEL_LEN + sel_off
        rel_s = tpos[:, None, None] - spos
        bias_s = jnp.moveaxis(table_nsa[t5_bucket(rel_s), gi5], -1, 2).astype(jnp.float32)
        s_s = jnp.einsum('bgpqd,bgqnld->bgpqnl', qb, ks).astype(jnp.float32) * scale + bias_s
        m_sel = top_n * SEL_LEN
        p_s = masked_softmax(s_s.reshape(B, G, P, NSA_Q_BLOCK, m_sel),
                             (rel_s >= 0).reshape(B, G, 1, NSA_Q_BLOCK, m_sel))
        o_s = jnp.einsum('bgpqm,bgqmd->bgpqd', p_s.astype(vs.dtype),
                         vs.reshape(B, G, NSA_Q_BLOCK, m_sel, D))
        kwb = lax.dynamic_slice_in_dim(k_wp, t0, span, axis=2)
        vwb = lax.dynamic_slice_in_dim(v_wp, t0, span, axis=2)
        wpos = t0 - WINDOW + jnp.arange(span, dtype=jnp.int32)
        rel_w = tpos[:, None] - wpos[None, :]
        mask_w = (rel_w >= 0) & (rel_w < WINDOW) & (wpos[None, :] >= 0)
        bias_w = jnp.transpose(table_nsa[t5_bucket(rel_w)], (2, 3, 0, 1)).astype(jnp.float32)
        s_w = jnp.einsum('bgpqd,bgkd->bgpqk', qb, kwb).astype(jnp.float32) * scale + bias_w
        p_w = masked_softmax(s_w, mask_w)
        o_w = jnp.einsum('bgpqk,bgkd->bgpqd', p_w.astype(vwb.dtype), vwb)
        return gb[..., 0:1] * o_c + gb[..., 1:2] * o_s + gb[..., 2:3] * o_w

    out = lax.map(block, jnp.arange(S // NSA_Q_BLOCK, dtype=jnp.int32))
    return out.transpose(1, 0, 4, 2, 3, 5).reshape(B, S, G * P * D)

def diff_mixer(q1, q2, k1, k2, v, lam, table_diff):
    B, H, S, D = q1.shape
    scale = D ** -0.5
    kpos = jnp.arange(S, dtype=jnp.int32)

    def block(i):
        t0 = i * DIFF_Q_BLOCK
        tpos = t0 + jnp.arange(DIFF_Q_BLOCK, dtype=jnp.int32)
        rel = tpos[:, None] - kpos[None, :]
        mask = rel >= 0
        bias = jnp.transpose(table_diff[t5_bucket(rel)], (2, 0, 1)).astype(jnp.float32)
        q1b = lax.dynamic_slice_in_dim(q1, t0, DIFF_Q_BLOCK, axis=2)
        q2b = lax.dynamic_slice_in_dim(q2, t0, DIFF_Q_BLOCK, axis=2)
        a1 = masked_softmax(jnp.einsum('bhqd,bhkd->bhqk', q1b, k1).astype(jnp.float32) * scale + bias, mask)
        a2 = masked_softmax(jnp.einsum('bhqd,bhkd->bhqk', q2b, k2).astype(jnp.float32) * scale + bias, mask)
        a = a1 - lam * a2
        return jnp.einsum('bhqk,bhkd->bhqd', a.astype(v.dtype), v)

    out = lax.map(block, jnp.arange(S // DIFF_Q_BLOCK, dtype=jnp.int32))
    return out.transpose(1, 2, 0, 3, 4).reshape(B, H, S, v.shape[-1])

def setup_inputs(seed: int = 0) -> dict:
    key = jax.random.key(seed)
    ks = jax.random.split(key, 24)

    def nrm(k, shape, scale):
        return jax.random.normal(k, shape, jnp.float32) * scale

    kvin = CMP_LEN * HEAD_DIM
    return {
        'x': nrm(ks[0], (BATCH, SEQ, D_MODEL), 1.0),
        'norm_mix_g': 1.0 + nrm(ks[1], (DEPTH, D_MODEL), 0.02),
        'w_in': nrm(ks[2], (DEPTH, D_MODEL, D_IN_PROJ), D_MODEL ** -0.5),
        'cmp_pe_k': nrm(ks[3], (DEPTH, CMP_LEN, HEAD_DIM), 0.1),
        'cmp_pe_v': nrm(ks[4], (DEPTH, CMP_LEN, HEAD_DIM), 0.1),
        'cmp_w1_k': nrm(ks[5], (DEPTH, kvin, CMP_HIDDEN), kvin ** -0.5),
        'cmp_w2_k': nrm(ks[6], (DEPTH, CMP_HIDDEN, HEAD_DIM), CMP_HIDDEN ** -0.5),
        'cmp_w1_v': nrm(ks[7], (DEPTH, kvin, CMP_HIDDEN), kvin ** -0.5),
        'cmp_w2_v': nrm(ks[8], (DEPTH, CMP_HIDDEN, HEAD_DIM), CMP_HIDDEN ** -0.5),
        'diff_lq1': nrm(ks[9], (DEPTH, HEAD_DIM), 0.1),
        'diff_lk1': nrm(ks[10], (DEPTH, HEAD_DIM), 0.1),
        'diff_lq2': nrm(ks[11], (DEPTH, HEAD_DIM), 0.1),
        'diff_lk2': nrm(ks[12], (DEPTH, HEAD_DIM), 0.1),
        'diff_head_g': 1.0 + nrm(ks[13], (DEPTH, DIFF_HEADS, DIFF_V_DIM), 0.02),
        'w_up_nsa': nrm(ks[14], (DEPTH, NSA_WIDTH, D_MODEL), NSA_WIDTH ** -0.5),
        'w_up_diff': nrm(ks[15], (DEPTH, DIFF_WIDTH, D_MODEL), DIFF_WIDTH ** -0.5),
        'w_out': nrm(ks[16], (DEPTH, D_MODEL, D_MODEL), D_MODEL ** -0.5),
        'norm_ff_g': 1.0 + nrm(ks[17], (DEPTH, D_MODEL), 0.02),
        'w_ff_in': nrm(ks[18], (DEPTH, D_MODEL, 2 * D_FF), D_MODEL ** -0.5),
        'w_ff_out': nrm(ks[19], (DEPTH, D_FF, D_MODEL), D_FF ** -0.5),
        'rel_bias_table': nrm(ks[20], (REL_BUCKETS, N_BIAS_HEADS), 0.1),
        'norm_final_g': 1.0 + nrm(ks[21], (D_MODEL,), 0.02),
    }

def reference(x, norm_mix_g, w_in, cmp_pe_k, cmp_pe_v, cmp_w1_k, cmp_w2_k, cmp_w1_v, cmp_w2_v,
              diff_lq1, diff_lk1, diff_lq2, diff_lk2, diff_head_g, w_up_nsa, w_up_diff, w_out,
              norm_ff_g, w_ff_in, w_ff_out, rel_bias_table, norm_final_g):
    B, S, _ = x.shape
    G, P, HD = NSA_KV_GROUPS, NSA_HPG, HEAD_DIM
    table_nsa = rel_bias_table[:, :NSA_HEADS].reshape(REL_BUCKETS, G, P)
    table_diff = rel_bias_table[:, NSA_HEADS:]

    def groups(t, n):
        return t.reshape(B, S, n, -1).transpose(0, 2, 1, 3)

    for l in range(DEPTH):
        h = rms_norm(x, norm_mix_g[l])
        proj = h @ w_in[l]
        (q_n, kc, vc, ksl, vsl, kw, vw, g_n, q_d, k_d, v_d, g_m) = jnp.split(proj, SPLIT_POINTS, axis=-1)
        q_n = q_n.reshape(B, S, G, P, HD).transpose(0, 2, 3, 1, 4)
        k_cmp = compress_blocks(groups(kc, G), cmp_pe_k[l], cmp_w1_k[l], cmp_w2_k[l])
        v_cmp = compress_blocks(groups(vc, G), cmp_pe_v[l], cmp_w1_v[l], cmp_w2_v[l])
        nsa_gates = jax.nn.sigmoid(g_n.reshape(B, S, G, P, 3).transpose(0, 2, 3, 1, 4))
        o_nsa = nsa_mixer(q_n, k_cmp, v_cmp, groups(ksl, G), groups(vsl, G),
                          groups(kw, G), groups(vw, G), nsa_gates, table_nsa)
        q_d = q_d.reshape(B, S, DIFF_HEADS, 2, HD)
        k_d = k_d.reshape(B, S, DIFF_HEADS, 2, HD)
        q1 = q_d[:, :, :, 0].transpose(0, 2, 1, 3)
        q2 = q_d[:, :, :, 1].transpose(0, 2, 1, 3)
        k1 = k_d[:, :, :, 0].transpose(0, 2, 1, 3)
        k2 = k_d[:, :, :, 1].transpose(0, 2, 1, 3)
        lam_init = 0.8 - 0.6 * math.exp(-0.3 * l)
        lam = (jnp.exp(jnp.sum(diff_lq1[l].astype(jnp.float32) * diff_lk1[l].astype(jnp.float32)))
               - jnp.exp(jnp.sum(diff_lq2[l].astype(jnp.float32) * diff_lk2[l].astype(jnp.float32)))
               + lam_init)
        o_d = diff_mixer(q1, q2, k1, k2, groups(v_d, DIFF_HEADS), lam, table_diff)
        o_d = rms_norm(o_d, diff_head_g[l][:, None, :]) * (1.0 - lam_init)
        o_d = o_d.transpose(0, 2, 1, 3).reshape(B, S, DIFF_WIDTH)
        g_a, g_b = jnp.split(jax.nn.sigmoid(g_m), 2, axis=-1)
        mixed = (g_a * (o_nsa @ w_up_nsa[l]) + g_b * (o_d @ w_up_diff[l])) @ w_out[l]
        x = x + mixed
        h = rms_norm(x, norm_ff_g[l])
        a, b = jnp.split(h @ w_ff_in[l], 2, axis=-1)
        x = x + (jax.nn.silu(a) * b) @ w_ff_out[l]
    return rms_norm(x, norm_final_g)


_drawn_inputs = setup_inputs


def setup_inputs(seed=0):
    import zlib

    import numpy as np

    out = dict(_drawn_inputs(seed))
    spreads = {}
    factors = {'norm_mix_g': 3.22,
     'cmp_pe_k': 8.0,
     'cmp_pe_v': 3.677,
     'diff_lq1': 3.66,
     'diff_head_g': 6.222,
     'norm_ff_g': 4.102,
     'norm_final_g': 2.766}
    for name, (base, spread) in spreads.items():
        noise = np.random.default_rng([zlib.crc32(name.encode()), seed]).standard_normal(out[name].shape)
        drawn = base * np.exp(spread * noise) if base else spread * noise
        out[name] = __import__('jax').numpy.asarray(drawn.astype(out[name].dtype))
    for name, factor in factors.items():
        out[name] = (out[name] * factor).astype(out[name].dtype)
    return out
```

```python
import math
from contextlib import ExitStack

import numpy as np

import concourse.bass as bass
from concourse import mybir

F32 = mybir.dt.float32
F32R = mybir.dt.float32r
ALU = mybir.AluOpType
ACT = mybir.ActivationFunctionType
AX = mybir.AxisListType

P = 128
S = 512
DM = 2048
HD = 128
NT = S // P
KT = DM // P
NH, NG, DH = 8, 2, 4
DV = 2 * HD
CL, CS = 32, 16
NC_ = S // CS
CH = 256
DFF = 5632
BUCKETS, MAX_EXACT, MAX_DIST = 32, 16, 128
EPS = 1e-6
SCALE = HD ** -0.5
LAM_INIT = 0.8 - 0.6 * math.exp(0.0)
MASKED = 1e30
FLOOR = 1e29
COLS = 512
PAIRS = KT // 2
RAW = 4
HL = 4
AHEAD = 2

T_JOBS = 8
G_JOBS = 8
N_JOBS = 3
N_COL0 = (T_JOBS + G_JOBS) * COLS
GN_COL0 = N_COL0 + N_JOBS * COLS
GN = 3 * NH
C_TILE, K_TILE, QD_TILE, KD_TILE, G_TILE = 8, 12, 16, 24, 32
REV = 640
FWD = 1024
FWD0 = S + CL // 2 - 1
ROW = REV + FWD
FF_CHUNK = 4
CHUNKS = DFF // (FF_CHUNK * P)
FF_PAIRS = 3 * PAIRS
PAIR_N = T_JOBS * PAIRS
PAIR_C = PAIR_N + N_JOBS * PAIRS
PAIR_G = PAIR_C + 2 * PAIRS
PAIR_UP = PAIR_G + G_JOBS * PAIRS
PAIR_OUT = PAIR_UP + NT * PAIRS
PAIR_FF = PAIR_OUT + NT * PAIRS
PAIR_END = PAIR_FF + CHUNKS * FF_PAIRS
JOB_N = T_JOBS
JOB_C = JOB_N + N_JOBS
JOB_G = JOB_C + 1
JOB_UP = JOB_G + G_JOBS
JOB_OUT = JOB_UP + 2 * NT
JOB_FF = JOB_OUT + NT
FF_JOBS = 6
FREE_AHEAD = 3
ITERS = DH
ORDER = (0, 2, 1, 3)
BANK_END = {0: 1, 2: 1, 1: 2, 3: 3}
U_PT = (0, 4, 7, 11, 14, 17)
AT = {3: [("S", 0)], 6: [("T", 0)], 7: [("V", 0), ("S", 1)], 10: [("T", 1)], 11: [("V", 1), ("S", 2)],
      14: [("T", 2)], 15: [("V", 2), ("S", 3)], 18: [("T", 3)], 19: [("V", 3), ("S", 4)],
      21: [("S", 5)], 25: [("T", 4)], 26: [("V", 4)], 29: [("O", 0)]}


def bucket_onehot():
    n = np.arange(S)
    large = MAX_EXACT + (np.log(np.maximum(n, 1) / MAX_EXACT) / math.log(MAX_DIST / MAX_EXACT)
                         * (BUCKETS - MAX_EXACT)).astype(np.int32)
    bucket = np.where(n < MAX_EXACT, n, np.minimum(large, BUCKETS - 1))
    rel = np.concatenate([S - 1 - np.arange(REV), np.arange(FWD) - FWD0])
    row = np.where((rel < 0) | (rel >= S), BUCKETS, bucket[np.clip(rel, 0, S - 1)])
    return (np.arange(BUCKETS + 1)[:, None] == row[None, :]).astype(np.float32)


def build(nc, x, w_proj, pe_k, pe_v, cw1, cw2, lq1, lk1, lq2, lk2, head_g, mix_g, ff_g, final_g,
          w_up, w_out, w_ff_in, w_ff_out, table, onehot, out):
    ctx = ExitStack()
    with ctx:
        proj_t = nc.dram_tensor("proj_t", [(T_JOBS + G_JOBS) * NT, P, S], F32).ap()
        proj_n = nc.dram_tensor("proj_n", [NT, P, N_JOBS * COLS], F32).ap()
        o_hi_d = nc.dram_tensor("o_hi_d", [KT, P, S], F32).ap()
        o_lo_d = nc.dram_tensor("o_lo_d", [KT, P, S], F32).ap()
        bias_d = nc.dram_tensor("bias_d", [NH + DH, ROW], F32).ap()

        skew_d = nc.dram_tensor("skew_d", [NH + DH, P * (REV + 1)], F32).ap()
        cskew_d = nc.dram_tensor("cskew_d", [NH, NC_ * (FWD + CS)], F32).ap()
        skew_w = skew_d.rearrange("h (p r) -> h p r", p=P)
        cskew_w = cskew_d.rearrange("h (c r) -> h c r", c=NC_)
        skew_r = skew_d[:, 0:P * REV].rearrange("h (p r) -> h p r", p=P)
        cskew_r = cskew_d[:, 0:NC_ * FWD].rearrange("h (c r) -> h c r", c=NC_)

        base = (nc.sbuf_base + 63) // 64 * 64
        KB = 1024
        R1, R2 = base, base + 64 * KB
        RING = base + 128 * KB
        MISC = RING + 48 * KB

        def at(name, shape, offset, dt=F32):
            return nc.alloc_sbuf_tensor_at(name, shape, dt, offset=offset)

        h_hi = at("h_hi", [P, KT, S], R1, F32R)
        h_lo = at("h_lo", [P, KT, S], R1 + 32 * KB, F32R)
        o_hi = at("o_hi", [P, KT, S], R1, F32R)
        o_lo = at("o_lo", [P, KT, S], R1 + 32 * KB, F32R)
        res = at("res", [P, NT, DM], R1)
        res_s = at("res_s", [P, NT, DM], R1 + 32 * KB)
        silu = at("silu", [P, FF_CHUNK, S], R1 + 32 * KB)
        f_hi = at("f_hi", [P, FF_CHUNK, S], R1 + 40 * KB, F32R)
        f_lo = at("f_lo", [P, FF_CHUNK, S], R1 + 48 * KB, F32R)
        fg = at("fg", [P, DM], R1 + 56 * KB)
        x_in = at("x_in", [P, NT, DM], R2)
        x_s = at("x_s", [P, NT, DM], R2 + 32 * KB)
        m_hi = at("m_hi", [P, KT, S], R2, F32R)
        m_lo = at("m_lo", [P, KT, S], R2 + 32 * KB, F32R)
        h2_hi = at("h2_hi", [P, KT, S], R2, F32R)
        h2_lo = at("h2_lo", [P, KT, S], R2 + 32 * KB, F32R)
        fin = at("fin", [P, NT, DM], R2)
        fin_s = at("fin_s", [P, NT, DM], R2 + 32 * KB)
        c_in = at("c_in", [P, 4, S], R2)
        blk = at("blk", [P, 2, CL, NG * NC_], R2 + 8 * KB)
        blk_hi = at("blk_hi", [P, 2, CL, NG * NC_], R2 + 24 * KB, F32R)
        blk_lo = at("blk_lo", [P, 2, CL, NG * NC_], R2 + 40 * KB, F32R)
        hid = at("hid", [P, 2, 2, NG * NC_], R2 + 56 * KB)
        w2 = at("w2", [P, 2, 2, HD], R2 + 57 * KB)
        q2 = at("q2", [P, 2, S], R2)
        k2 = at("k2", [P, 2, S], R2 + 4 * KB)
        v2 = at("v2", [P, NT, 2, HD], R2 + 8 * KB)
        qd = at("qd", [P, 2, S], R2 + 12 * KB)
        kd = at("kd", [P, 2, S], R2 + 16 * KB)
        vd = at("vd", [P, NT, DV], R2 + 20 * KB)
        bias = at("bias", [P, 3, S], R2 + 24 * KB)
        cbias = at("cbias", [NC_, 2, S], R2 + 30 * KB)
        z = at("z", [P, 1280], R2 + 34 * KB)
        p_a = at("p_a", [P, 1280], R2 + 39 * KB)
        p_b = at("p_b", [P, 1280], R2 + 44 * KB)
        pt = at("pt", [P, 1280], R2 + 49 * KB)
        zc = at("zc", [P, NT, NC_], R2 + 54 * KB)
        pc = at("pc", [P, NT, NC_], R2 + 54 * KB + 512)
        pct = at("pct", [NC_, S], R2 + 55 * KB)
        on = at("on", [P, NT, DV], R2 + 57 * KB)
        raw = [at(f"raw{s}", [P, 2, COLS], RING + 4 * KB * s) for s in range(RAW)]
        w_hi = [at(f"w_hi{s}", [P, 2, COLS], RING + 16 * KB + 4 * KB * s, F32R) for s in range(HL)]
        w_lo = [at(f"w_lo{s}", [P, 2, COLS], RING + 32 * KB + 4 * KB * s, F32R) for s in range(HL)]
        stage = [at(f"stage{b}", [P, S], MISC + 2 * KB * b) for b in range(4)]
        oh = at("oh", [BUCKETS + 1, ROW], MISC + 8 * KB)
        brow = at("brow", [NH + DH, ROW], MISC + 15 * KB)
        s_hi = [at(f"s_hi{k}", [P, S], MISC + 8 * KB + 2 * KB * k, F32R) for k in range(4)]
        s_lo = [at(f"s_lo{k}", [P, S], MISC + 16 * KB + 2 * KB * k, F32R) for k in range(4)]
        ga = at("ga", [P, NT, S], MISC + 8 * KB)
        gb = at("gb", [P, NT, S], MISC + 16 * KB)
        top = [MISC + 24 * KB]

        def small(name, shape, dt=F32):
            n = int(np.prod(shape[1:])) * 4
            t = at(name, shape, top[0], dt)
            top[0] += (n + 31) // 32 * 32
            return t

        ident = small("ident", [P, P])
        rows = at("rows", [108, P], MISC + 22 * KB)
        cols = small("cols", [P, 108])
        tab = small("tab", [BUCKETS + 1, NH + DH])
        wg_hi = small("wg_hi", [P, KT, GN], F32R)
        wg_lo = small("wg_lo", [P, KT, GN], F32R)
        wg = stage[3][:, 0:KT * GN].rearrange("p (k n) -> p k n", k=KT)
        gates = small("gates", [P, NT, GN])
        gcur = small("gcur", [P, NT, 6])
        ones = small("ones", [P, P])
        kct = small("kct", [P, NG * NC_])
        kcur = small("kcur", [P, NC_])
        vc = small("vc", [NC_, NG, HD])
        vcur = small("vcur", [NC_, HD])
        hg = small("hg", [P, 2 * DH])
        hgcur = small("hgcur", [P, 2])
        lprod = small("lprod", [P, 2])
        lexp = small("lexp", [P, 2])
        neglam = small("neglam", [P, 1])
        ss = small("ss", [P, NT])
        ms = small("ms", [P, NT])
        rstd = small("rstd", [P, NT])
        inv = small("inv", [P, NT])
        m = small("m", [P, NT])
        l1 = small("l1", [P, NT])
        l2 = small("l2", [P, NT])
        r1 = small("r1", [P, NT])
        r2 = small("r2", [P, NT])
        cm = small("cm", [P, NT])
        cl = small("cl", [P, NT])
        cr = small("cr", [P, NT])
        assert top[0] <= nc.sbuf_usable_end, (top[0], nc.sbuf_usable_end)

        def bank(name):
            return ctx.enter_context(nc.psum_tensor(name, [P, 512], F32))

        acc = [bank(f"acc{b}") for b in range(4)]
        e = [bank(f"e{b}") for b in range(3)]
        ob = bank("ob")
        nbanks = e + [ob] + acc

        SEG = [(0, 0), (1, 0), (0, 128), (2, 0)]
        CSEG = 256
        ZOFF = [0, 128, 384, 768]
        TSEG = [(0, 0), (1, 0), (2, 0), (1, 384)]

        def sem(name):
            return ctx.enter_context(nc.semaphore(name))

        pool_waited, dve_waited = sem("pool_waited"), sem("dve_waited")
        x_landed = [sem(f"x_landed{i}") for i in range(NT)]
        w_landed = [sem(f"w_landed{s}") for s in range(RAW)]
        hi_ready = sem("hi_ready")
        lo_ready = sem("lo_ready")
        pair_done = sem("pair_done")
        acc_done = sem("acc_done")
        acc_free = [sem(f"acc_free{b}") for b in range(4)]
        spilled = [sem(f"spilled{b}") for b in range(4)]
        rows_landed, tab_landed, oh_landed, wg_landed = sem("rows_landed"), sem("tab_landed"), sem("oh_landed"), sem("wg_landed")
        tab_masked = sem("tab_masked")
        ident_ready, ones_ready = sem("ident_ready"), sem("ones_ready")
        cols_turned, cols_ready = sem("cols_turned"), sem("cols_ready")
        brow_done, brow_ready, brow_spilled = sem("brow_done"), sem("brow_ready"), sem("brow_spilled")
        skewed = sem("skewed")
        lprod_ready, lam_sum, lam_exp = sem("lprod_ready"), sem("lam_sum"), sem("lam_exp")
        dve = sem("dve")
        sq_ready, ms_ready, rstd_ready, xs_ready = sem("sq_ready"), sem("ms_ready"), sem("rstd_ready"), sem("xs_ready")
        turned, n_hi, n_lo = sem("turned"), sem("n_hi"), sem("n_lo")
        wg_hi_ready, wg_lo_ready, gn_done, gates_ready = sem("wg_hi_ready"), sem("wg_lo_ready"), sem("gn_done"), sem("gates_ready")
        c_landed, w2_landed = sem("c_landed"), sem("w2_landed")
        blk_ready, blk_hi_ready, blk_lo_ready = sem("blk_ready"), sem("blk_hi_ready"), sem("blk_lo_ready")
        hid_done, kvc_done, kvc_ready = sem("hid_done"), sem("kvc_done"), sem("kvc_ready")
        nsa_loaded, diff_loaded = sem("nsa_loaded"), sem("diff_loaded")
        cur_ready = sem("cur_ready")
        scores_done, z_ready, p_exp, p_scaled = sem("scores_done"), sem("z_ready"), sem("p_exp"), sem("p_scaled")
        zc_ready, pc_exp, pc_scaled = sem("zc_ready"), sem("pc_exp"), sem("pc_scaled")
        pt_done, pt_ready, pv_done = sem("pt_done"), sem("pt_ready"), sem("pv_done")
        o_hi_ready, o_lo_ready = sem("o_hi_ready"), sem("o_lo_ready")
        o_spilled = [sem(f"o_spilled{k}") for k in range(4)]
        on_ready, on_sq, on_ms, on_rstd, on_scaled, ot_done = (sem("on_ready"), sem("on_sq"), sem("on_ms"),
                                                               sem("on_rstd"), sem("on_scaled"), sem("ot_done"))
        chain = sem("chain")
        o_landed = [sem(f"o_landed{k}") for k in range(PAIRS)]
        g_landed, sig_ready, mix_part, mix_sum, mix_hi, mix_lo = (sem("g_landed"), sem("sig_ready"), sem("mix_part"),
                                                                  sem("mix_sum"), sem("mix_hi"), sem("mix_lo"))
        res_landed = sem("res_landed")
        f_hi_ready, f_lo_ready = sem("f_hi_ready"), sem("f_lo_ready")
        fg_landed, fin_ready, out_stored = sem("fg_landed"), sem("fin_ready"), sem("out_stored")

        w_proj_v = w_proj.rearrange("(k p) n -> p k n", p=P)
        w_up_v = w_up.rearrange("(k p) n -> p k n", p=P)
        w_out_v = w_out.rearrange("(k p) n -> p k n", p=P)
        w_ff_in_v = w_ff_in.rearrange("(k p) n -> p k n", p=P)
        w_ff_out_v = w_ff_out.rearrange("(c k p) n -> p c k n", p=P, k=FF_CHUNK)
        cw1_v = cw1.rearrange("s (j p) n -> s p j n", p=P)
        x_v = x.rearrange("(i p) n -> p i n", p=P)
        out_v = out.rearrange("(i p) n -> p i n", p=P)
        pt_v = proj_t.rearrange("f p s -> p f s")
        pn_v = proj_n.rearrange("i p n -> p i n")

        block = ctx.enter_context(nc.Block())

        @block.sync
        def _(sp):
            for i in range(NT):
                sp.dma_start(x_in[:, i, :], x_v[:, i, :]).then_inc(x_landed[i], 16)

            def load(pair, k, source):
                if not isinstance(pair, int) or pair >= RAW:
                    sp.wait_ge(lo_ready, pair - RAW + 1)
                sp.dma_start(raw[k % RAW][:, :, :], source).then_inc(w_landed[k % RAW], 16)

            def job(pair, weights, col):
                for k in range(PAIRS):
                    load(pair + k, k, weights[:, 2 * k:2 * k + 2, bass.ds(col, COLS)])

            job(0, w_proj_v, 0)
            with sp.Fori(1, T_JOBS) as j:
                job(j * PAIRS, w_proj_v, j * COLS)
            with sp.Fori(0, N_JOBS) as j:
                job(j * PAIRS + PAIR_N, w_proj_v, j * COLS + N_COL0)
            for s in range(2):
                for k in range(PAIRS):
                    load(PAIR_C + PAIRS * s + k, k,
                         cw1_v[s, :, 4 * k:4 * k + 4, :])
            with sp.Fori(0, G_JOBS) as j:
                job(j * PAIRS + PAIR_G, w_proj_v, (j + T_JOBS) * COLS)
            with sp.Fori(0, NT) as c:
                job(c * PAIRS + PAIR_UP, w_up_v, c * COLS)
            with sp.Fori(0, NT) as c:
                job(c * PAIRS + PAIR_OUT, w_out_v, c * COLS)
            def ff_out(pair, c):
                for n in range(NT):
                    for k in range(2):
                        load(pair + 2 * n + k, 2 * n + k,
                             w_ff_out_v[:, bass.ds(c, 1), 2 * k:2 * k + 2, n * COLS:(n + 1) * COLS].rearrange("p c k n -> p (c k) n"))
            job(PAIR_FF, w_ff_in_v, 0)
            with sp.Fori(0, CHUNKS - 1) as c:
                job(c * FF_PAIRS + PAIR_FF + PAIRS, w_ff_in_v, c * COLS + DFF)
                job(c * FF_PAIRS + PAIR_FF + 2 * PAIRS, w_ff_in_v, c * COLS + COLS)
                ff_out(c * FF_PAIRS + PAIR_FF + 3 * PAIRS, c)
            job(PAIR_END - 2 * PAIRS, w_ff_in_v, (CHUNKS - 1) * COLS + DFF)
            ff_out(PAIR_END - PAIRS, CHUNKS - 1)
            for i in range(NT):
                sp.wait_ge(fin_ready, i + 1)
                sp.dma_start(out_v[:, i, :], fin[:, i, :]).then_inc(out_stored, 16)
            sp.wait_ge(out_stored, 16 * NT)

        @block.gpsimd
        def _(pool):
            pool.dma_start(rows[0:16, :], mix_g.rearrange("(k p) -> k p", p=P)).then_inc(rows_landed, 16)
            pool.dma_start(rows[16:32, :], ff_g.rearrange("(k p) -> k p", p=P)).then_inc(rows_landed, 16)
            pool.dma_start(rows[32:40, :], head_g.rearrange("h (k p) -> (h k) p", p=P)).then_inc(rows_landed, 16)
            for n, v in enumerate((lq1, lk1, lq2, lk2)):
                pool.dma_start(rows[40 + n:41 + n, :], v.rearrange("(a p) -> a p", a=1)).then_inc(rows_landed, 16)
            pool.dma_start(rows[44:76, :], pe_k).then_inc(rows_landed, 16)
            pool.dma_start(rows[76:108, :], pe_v).then_inc(rows_landed, 16)
            pool.dma_start(tab[0:BUCKETS, :], table).then_inc(tab_landed, 16)
            pool.dma_start(oh[:, :], onehot).then_inc(oh_landed, 16)
            pool.dma_start(wg, w_proj_v[:, :, GN_COL0:GN_COL0 + GN]).then_inc(wg_landed, 16)
            pool.memset(ones[:, :], 1.0).then_inc(ones_ready, 1)
            pool.memset(ident[:, :], 0.0).then_inc(ident_ready, 1)
            pool.wait_ge(ident_ready, 1)
            pool.affine_select(out=ident[:, :], in_=ident[:, :], compare_op=ALU.not_equal, fill=1.0, base=0,
                               pattern=[[-1, P]], channel_multiplier=1).then_inc(ident_ready, 1)
            pool.wait_ge(brow_ready, 4)
            pool.dma_start(bias_d, brow[:, :]).then_inc(brow_spilled, 16)
            pool.wait_ge(brow_spilled, 16)
            for h in range(NH + DH):
                pool.dma_start(skew_w[h, :, 0:REV], bias_d[h:h + 1, 0:REV].to_broadcast([P, REV])).then_inc(skewed, 16)
            for h in range(NH):
                pool.dma_start(cskew_w[h, :, 0:FWD], bias_d[h:h + 1, REV:ROW].to_broadcast([NC_, FWD])).then_inc(skewed, 16)

            def spill_t(j, tile0, job):
                for b in range(4):
                    pool.wait_ge(acc_free[b], job + 2).then_inc(pool_waited, 1)
                    pool.dma_start(pt_v[:, bass.ds(tile0 + b, 1), :].rearrange("p f s -> p (f s)"),
                                   stage[b][:, :]).then_inc(spilled[b], 16)

            with pool.Fori(0, T_JOBS) as j:
                spill_t(j, j * NT, j)
            with pool.Fori(0, N_JOBS) as j:
                for b in range(4):
                    pool.wait_ge(acc_free[b], j + (JOB_N + 2)).then_inc(pool_waited, 1)
                    pool.dma_start(proj_n[b, :, bass.ds(j * COLS, COLS)], stage[b][:, :]).then_inc(spilled[b], 16)
            for b in range(4):
                pool.wait_ge(spilled[b], 16 * (T_JOBS + N_JOBS))
            pool.wait_ge(xs_ready, NT)
            pool.dma_start(c_in[:, :, :], pt_v[:, C_TILE:C_TILE + 4, :]).then_inc(c_landed, 16)
            pool.dma_start(w2[:, :, :, :], cw2.rearrange("s (k p) n -> p s k n", p=P)).then_inc(w2_landed, 16)
            pool.wait_ge(kvc_ready, 2)
            pool.wait_ge(skewed, 16 * (2 * NH + DH))
            with pool.Fori(0, ITERS) as t:
                g = t // 2
                pool.dma_start(q2[:, :, :], pt_v[:, bass.ds(2 * t, 2), :]).then_inc(nsa_loaded, 16)
                for n in range(2):
                    pool.dma_start(k2[:, n, :], pt_v[:, bass.ds(g + (K_TILE + 2 * n), 1), :].rearrange("p f s -> p (f s)"))\
                        .then_inc(nsa_loaded, 16)
                pool.dma_start(bias[:, 0:2, :], skew_r[bass.ds(2 * t, 2), :, P - 1:P - 1 + S].rearrange("h p s -> p h s"))\
                    .then_inc(nsa_loaded, 16)
                pool.dma_start(cbias[:, :, :], cskew_r[bass.ds(2 * t, 2), :, FWD0 - CL + 1:FWD0 - CL + 1 + S].rearrange("h c s -> c h s")).then_inc(nsa_loaded, 16)
                for n in range(2):
                    pool.dma_start(v2[:, :, n, :], pn_v[:, :, bass.ds(g * HD + n * DV, HD)]).then_inc(nsa_loaded, 16)
                pool.dma_start(qd[:, :, :], pt_v[:, bass.ds(2 * t + QD_TILE, 2), :]).then_inc(diff_loaded, 16)
                pool.dma_start(kd[:, :, :], pt_v[:, bass.ds(2 * t + KD_TILE, 2), :]).then_inc(diff_loaded, 16)
                pool.dma_start(bias[:, 2, :], skew_r[bass.ds(t + NH, 1), :, P - 1:P - 1 + S].rearrange("h p s -> p (h s)"))\
                    .then_inc(diff_loaded, 16)
                pool.dma_start(vd[:, :, :], pn_v[:, :, bass.ds(t * DV + COLS, DV)]).then_inc(diff_loaded, 16)

                def spill_o(slot, ready, tile):
                    pool.wait_ge(o_lo_ready, ready).then_inc(pool_waited, 1)
                    pool.dma_start(o_hi_d[bass.ds(tile, 1), :, :].rearrange("f p s -> (f p) s"),
                                   s_hi[slot][:, :].bitcast(F32)).then_inc(o_spilled[slot], 16)
                    pool.dma_start(o_lo_d[bass.ds(tile, 1), :, :].rearrange("f p s -> (f p) s"),
                                   s_lo[slot][:, :].bitcast(F32)).then_inc(o_spilled[slot], 16)

                spill_o(0, 4 * t + 1, 2 * t)
                spill_t(0, 8 * t + G_TILE, 2 * t + JOB_G)
                spill_o(1, 4 * t + 2, 2 * t + 1)
                spill_o(2, 4 * t + 3, 2 * t + NH)
                spill_o(3, 4 * t + 4, 2 * t + (NH + 1))
                spill_t(0, 8 * t + (G_TILE + 4), 2 * t + (JOB_G + 1))
            for k in range(4):
                pool.wait_ge(o_spilled[k], 32 * ITERS)
            pool.wait_ge(pair_done, PAIR_UP)
            for k in range(PAIRS):
                for d, t in ((o_hi_d, o_hi), (o_lo_d, o_lo)):
                    pool.dma_start(t[:, 2 * k:2 * k + 2, :].bitcast(F32),
                                   d[2 * k:2 * k + 2].rearrange("f p s -> p f s")).then_inc(o_landed[k], 16)
                if k == 0:
                    for b in range(4):
                        pool.wait_ge(spilled[b], 16 * (T_JOBS + N_JOBS + G_JOBS))
                    for n, t in enumerate((ga, gb)):
                        pool.dma_start(t[:, :, :], pt_v[:, G_TILE + KT * n:G_TILE + KT * n + NT, :]).then_inc(g_landed, 16)
            with pool.Fori(1, NT) as c:
                pool.wait_ge(mix_lo, c * NT).then_inc(pool_waited, 1)
                for n, t in enumerate((ga, gb)):
                    pool.dma_start(t[:, :, :], pt_v[:, bass.ds(c * NT + (G_TILE + KT * n), NT), :]).then_inc(g_landed, 16)
            pool.wait_ge(pair_done, PAIR_OUT)
            for i in range(NT):
                pool.dma_start(res[:, i, :], x_v[:, i, :]).then_inc(res_landed, 16)
            pool.wait_ge(turned, 2 * KT)
            pool.dma_start(fg[:, :], bass.AP(final_g.tensor, 0, [[0, P], [1, DM]])).then_inc(fg_landed, 16)

        @block.tensor
        def _(pe):
            mm = nc.tensor.matmul

            pe.wait_ge(ident_ready, 2)
            pe.wait_ge(rows_landed, 16 * 9)
            nc.tensor.transpose(ob[:, 0:108], rows[:, :], ident[0:108, 0:108]).then_inc(cols_turned, 1)
            pe.wait_ge(tab_landed, 16)
            pe.wait_ge(tab_masked, 1)
            pe.wait_ge(oh_landed, 16)
            for n in range(4):
                w = min(512, ROW - 512 * n)
                mm(acc[n][0:NH + DH, 0:w], tab[:, :], oh[:, 512 * n:512 * n + w], start=True, stop=True).then_inc(brow_done, 1)
            pe.wait_ge(ones_ready, 1)
            pe.wait_ge(lprod_ready, 2)
            mm(e[0][:, 0:2], ones[:, :], lprod[:, :], start=True, stop=True).then_inc(lam_sum, 1)

            def turn(src, norm, free):
                pe.wait_ge(xs_ready, NT * (norm + 1))
                for k in range(KT):
                    if k >= 8:
                        pe.wait_ge(n_lo, 12 * norm + k - 7)
                    elif k >= 4:
                        free(k)
                    for i in range(NT):
                        t = nc.tensor.transpose(nbanks[k % 8][:, i * P:(i + 1) * P], src[:, i, k * P:(k + 1) * P], ident[:, :])
                    t.then_inc(turned, 1)

            pe.wait_ge(lam_exp, 1)
            pe.wait_ge(cols_ready, 1)
            pe.wait_ge(brow_ready, 4)
            turn(x_s, 0, lambda k: None)
            pe.wait_ge(n_lo, 12)

            def tile(slot, i, a_hi, a_lo, a, natural, first, last, done, job, width=COLS):
                wh, wl = w_hi[slot], w_lo[slot]
                for b in range(4):
                    if first:
                        pe.wait_ge(acc_free[b], job + 1)
                    bl = slice(b * P, (b + 1) * P)
                    for n, (w, h) in enumerate(((wl, a_hi), (wh, a_lo), (wh, a_hi))):
                        lhs, rhs = (h[:, a, bl], w[:, i, :]) if natural else (w[:, i, bl], h[:, a, :])
                        t = mm(acc[b][:, :], lhs, rhs, start=first and n == 0, stop=last and n == 2)
                    if last and b < 3:
                        t.then_inc(acc_done, 1)
                if done:
                    t.then_inc(pair_done, 1)

            def job(pair, number, a_hi, a_lo, natural, k0=0, k1=PAIRS, before=None, a0=0):
                for k in range(k0, k1):
                    pe.wait_ge(lo_ready, pair + (k - k0 + 1))
                    for i in range(2):
                        if before:
                            before(2 * k + i)
                        tile(k % HL, i, a_hi, a_lo, a0 + 2 * k + i, natural, k == k0 and i == 0,
                             k == k1 - 1 and i == 1, i == 1, number)

            with pe.Fori(0, T_JOBS) as j:
                job(j * PAIRS, j, h_hi, h_lo, False)
            with pe.Fori(0, N_JOBS) as j:
                job(j * PAIRS + PAIR_N, j + JOB_N, h_hi, h_lo, True)

            pe.wait_ge(wg_lo_ready, 1)
            for i in range(NT):
                for k in range(KT):
                    for n, (w, h) in enumerate(((wg_lo, h_hi), (wg_hi, h_lo), (wg_hi, h_hi))):
                        t = mm(ob[:, i * GN:(i + 1) * GN], h[:, k, i * P:(i + 1) * P], w[:, k, :],
                               start=k == 0 and n == 0, stop=k == KT - 1 and n == 2)
            t.then_inc(gn_done, 1)

            for s in range(2):
                pe.wait_ge(blk_lo_ready, s + 1)
                for u in range(2):
                    pe.wait_ge(acc_free[2 * s + u], JOB_C + 1)
                for k in range(PAIRS):
                    pe.wait_ge(lo_ready, PAIR_C + PAIRS * s + k + 1)
                    wh = w_hi[k % HL][:, :, :].rearrange("p a (b n) -> p (a b) n", b=2)
                    wl = w_lo[k % HL][:, :, :].rearrange("p a (b n) -> p (a b) n", b=2)
                    for jj in range(4):
                        j = 4 * k + jj
                        for u in range(2):
                            for n, (w, a) in enumerate(((wl, blk_hi), (wh, blk_lo), (wh, blk_hi))):
                                t = mm(acc[2 * s + u][:, 0:NG * NC_], w[:, jj, u * P:(u + 1) * P], a[:, s, j, :],
                                       start=j == 0 and n == 0, stop=j == CL - 1 and n == 2)
                            if j == CL - 1 and u == 0:
                                t.then_inc(hid_done, 1)
                    t.then_inc(pair_done, 1)
            pe.wait_ge(w2_landed, 16)
            for b in range(4):
                pe.wait_ge(acc_free[b], JOB_C + 2)
            for u in range(2):
                t = mm(e[0][:, 0:NG * NC_], w2[:, 0, u, :], hid[:, 0, u, :], start=u == 0, stop=u == 1)
            t.then_inc(kvc_done, 1)
            for g in range(NG):
                for u in range(2):
                    t = mm(e[1][0:NC_, g * HD:(g + 1) * HD], hid[:, 1, u, g * NC_:(g + 1) * NC_], w2[:, 1, u, :],
                           start=u == 0, stop=u == 1)
            t.then_inc(kvc_done, 1)
            pe.wait_ge(kvc_ready, 2)
            pe.wait_ge(gates_ready, 1)

            with pe.Fori(0, ITERS) as t:
                def scores(u):
                    q, k = (q2, k2) if u < 4 else (qd, kd)
                    qs, ks = (u // 2, u % 2) if u < 4 else (u - 4, u - 4)
                    if u == 0:
                        pe.wait_ge(nsa_loaded, 16 * 7 * (t + 1))
                        pe.wait_ge(cur_ready, 4 * t + 4)
                    if u == 4:
                        pe.wait_ge(diff_loaded, 16 * 4 * (t + 1))
                    if u == 5:
                        pe.wait_ge(z_ready, 24 * t + 20)
                    for i in ORDER:
                        b, c = SEG[i]
                        n = (i + 1) * P
                        s = mm(e[b][:, c:c + n], q[:, qs, i * P:(i + 1) * P], k[:, ks, 0:n], start=True, stop=True)
                        if i == 1 and u in (0, 2):
                            for j in range(NT):
                                c = CSEG + j * NC_
                                mm(e[1][:, c:c + NC_], q[:, qs, j * P:(j + 1) * P], kcur[:, :], start=True, stop=False)
                                s = mm(e[1][:, c:c + NC_], cbias[:, qs, j * P:(j + 1) * P], ident[0:NC_, 0:NC_],
                                       start=False, stop=True)
                        if i > 0:
                            s.then_inc(scores_done, 1)

                def transposes(u):
                    p = p_a if u < 4 else p_b
                    pe.wait_ge(p_scaled, 20 * t + 4 * (u + 1))
                    for kt in (0, 1, 3, 2):
                        b, c = TSEG[kt]
                        for i in range(kt, NT):
                            s = nc.tensor.transpose(e[b][:, c + (i - kt) * P:c + (i - kt + 1) * P],
                                                    p[:, ZOFF[i] + kt * P:ZOFF[i] + (kt + 1) * P], ident[:, :])
                        if kt != 1:
                            s.then_inc(pt_done, 1)
                    if u in (0, 2):
                        if u == 2:
                            pe.wait_ge(o_lo_ready, 4 * t + 1)
                        pe.wait_ge(pc_scaled, 2 * t + (1 + u // 2))
                        for i in range(NT):
                            s = mm(ob[0:NC_, i * P:(i + 1) * P], pc[:, i, :], ident[:, :], start=True, stop=True)
                        s.then_inc(pt_done, 1)

                def values(u):
                    pe.wait_ge(pt_ready, 17 * t + U_PT[u + 1])
                    if u < 4:
                        if u % 2 == 0:
                            mm(ob[:, :], vcur[:, :], pct[:, :], start=True, stop=False)
                        for kt in range(NT):
                            b, c = TSEG[kt]
                            n = (NT - kt) * P
                            s = mm(ob[:, kt * P:S], v2[:, kt, u % 2, :], pt[:, 512 * b + c:512 * b + c + n],
                                   start=False, stop=u % 2 == 1 and kt == NT - 1)
                    else:
                        pe.wait_ge(o_lo_ready, 4 * t + 2)
                        for i in range(NT):
                            o, c = (ob, i * DV) if i < 2 else (e[0], (i - 2) * DV)
                            for kt in range(i + 1):
                                b, c0 = TSEG[kt]
                                c1 = 512 * b + c0 + (i - kt) * P
                                s = mm(o[:, c:c + DV], pt[:, c1:c1 + P], vd[:, kt, :], start=kt == 0, stop=kt == i)
                    s.then_inc(pv_done, 1)

                def turn_o(_):
                    pe.wait_ge(on_scaled, t + 1)
                    for h in range(2):
                        for i in range(NT):
                            s = nc.tensor.transpose(e[1 + h][:, i * P:(i + 1) * P], on[:, i, h * P:(h + 1) * P], ident[:, :])
                        s.then_inc(ot_done, 1)

                def pieces(first):
                    def before(tile):
                        for kind, u in AT.get(first + tile, ()):
                            {"S": scores, "T": transposes, "V": values, "O": turn_o}[kind](u)
                    return before

                for n in range(2):
                    job(t * (2 * PAIRS) + (PAIR_G + n * PAIRS), 2 * t + (JOB_G + n), h_hi, h_lo, False, before=pieces(16 * n))
                pe.wait_ge(o_lo_ready, 4 * t + 4)

            def up(c, landed):
                for n in range(2):
                    k0 = 4 * n
                    for k in range(k0, k0 + 4):
                        pe.wait_ge(lo_ready, c * PAIRS + (PAIR_UP + k + 1))
                        if landed:
                            pe.wait_ge(o_landed[k], 32)
                        for i in range(2):
                            tile(k % HL, i, o_hi, o_lo, 2 * k + i, False, k == k0 and i == 0, k == k0 + 3 and i == 1,
                                 i == 1, 2 * c + (JOB_UP + n))
            up(0, True)
            with pe.Fori(1, NT) as c:
                up(c, False)

            with pe.Fori(0, NT) as c:
                job(c * PAIRS + PAIR_OUT, c + JOB_OUT, m_hi, m_lo, True,
                    before=lambda k: pe.wait_ge(mix_lo, k + 1))

            turn(res_s, 1, lambda k: pe.wait_ge(acc_free[k - 4], JOB_FF + 1))
            pe.wait_ge(n_lo, 24)

            def ff_out(pair, number, c):
                pe.wait_ge(f_lo_ready, 4 * (c + 1))
                for n in range(NT):
                    for k in range(2):
                        pe.wait_ge(lo_ready, pair + (2 * n + k + 1))
                        for i in range(2):
                            tile((2 * n + k) % HL, i, f_hi, f_lo, 2 * k + i, True, k == 0 and i == 0,
                                 k == 1 and i == 1, i == 1, number + n)

            FJ = JOB_FF + 1
            job(PAIR_FF, FJ, h2_hi, h2_lo, False)
            with pe.Fori(0, CHUNKS - 1) as c:
                job(c * FF_PAIRS + (PAIR_FF + PAIRS), c * FF_JOBS + (FJ + 1), h2_hi, h2_lo, False)
                job(c * FF_PAIRS + (PAIR_FF + 2 * PAIRS), c * FF_JOBS + (FJ + 2), h2_hi, h2_lo, False)
                ff_out(c * FF_PAIRS + (PAIR_FF + 3 * PAIRS), c * FF_JOBS + (FJ + 3), c)
            last = FJ + (CHUNKS - 1) * FF_JOBS
            job(PAIR_END - 2 * PAIRS, last + 1, h2_hi, h2_lo, False)
            ff_out(PAIR_END - PAIRS, last + 2, CHUNKS - 1)

        @block.scalar
        def _(act):
            A = nc.scalar.activation

            act.wait_ge(lam_sum, 1)
            A(lexp[:, :], e[0][:, 0:2], ACT.Exp).then_inc(lam_exp, 1)

            def norm(src, scratch, norm_no, g0, dst, landed):
                for i in range(NT):
                    landed(i)
                    A(scratch[:, i, :], src[:, i, :], ACT.Square, accum_out=ss[:, i:i + 1]).then_inc(sq_ready, 1)
                    act.wait_ge(ms_ready, NT * norm_no + i + 1)
                    A(rstd[:, i:i + 1], ms[:, i:i + 1], ACT.Sqrt).then_inc(rstd_ready, 1)
                for k in range(KT):
                    act.wait_ge(turned, KT * norm_no + k + 1)
                    A(dst[:, k, :], nbanks[k % 8][:, :], ACT.Copy, scale=cols[:, g0 + k:g0 + k + 1]).then_inc(n_hi, 1)

            def evacuate(done, spill):
                for b in (0, 2):
                    if not isinstance(spill, int) or spill > 0:
                        act.wait_ge(spilled[b], 16 * spill)
                    act.wait_ge(acc_done, 3 * done + (b + 1))
                    A(stage[b][:, :], acc[b][:, :], ACT.Copy).then_inc(acc_free[b], 1)

            def sweep(first, uses, ks=range(AHEAD, PAIRS + AHEAD)):
                for k in ks:
                    a = k % PAIRS
                    act.wait_ge(w_landed[a % RAW], 16 * (uses + (k // RAW + 1)))
                    if not isinstance(first, int) or first + k >= HL:
                        act.wait_ge(pair_done, first + (k - HL + 1))
                    A(w_hi[a % HL][:, :, :], raw[a % RAW][:, :, :], ACT.Copy).then_inc(hi_ready, 1)
                    yield k - AHEAD

            def run(first, uses, ks=range(AHEAD, PAIRS + AHEAD)):
                for _ in sweep(first, uses, ks):
                    pass

            norm(x_in, x_s, 0, 0, h_hi, lambda i: act.wait_ge(x_landed[i], 16))
            act.wait_ge(wg_landed, 16)
            A(wg_hi[:, :, :], wg, ACT.Copy).then_inc(wg_hi_ready, 1)
            run(0, 0, range(AHEAD))
            run(0, 0)
            evacuate(0, 0)
            with act.Fori(1, T_JOBS) as j:
                run(j * PAIRS, 2 * j)
                evacuate(j, j)
            with act.Fori(0, N_JOBS) as j:
                run(j * PAIRS + PAIR_N, 2 * j + PAIR_N // RAW)
                evacuate(j + JOB_N, j + JOB_N)
            for s in range(2):
                act.wait_ge(blk_ready, 6 * (s + 1))
                A(blk_hi[:, s, :, :], blk[:, s, :, :], ACT.Copy).then_inc(blk_hi_ready, 1)
            run(PAIR_C, PAIR_C // RAW)
            act.wait_ge(gn_done, 1)
            A(gates[:, :, :], ob[:, 0:NT * GN].rearrange("p (i n) -> p i n", i=NT), ACT.Sigmoid).then_inc(gates_ready, 1)
            run(PAIR_C + PAIRS, (PAIR_C + PAIRS) // RAW)
            for s in range(2):
                for u in range(2):
                    b = 2 * s + u
                    if u == 0:
                        act.wait_ge(hid_done, s + 1)
                    else:
                        act.wait_ge(pair_done, PAIR_C + PAIRS * (s + 1))
                    A(hid[:, s, u, :], acc[b][:, 0:NG * NC_], ACT.Gelu_apprx_tanh).then_inc(acc_free[b], 1)
            act.wait_ge(kvc_done, 1)
            A(kct[:, :], e[0][:, 0:NG * NC_], ACT.Copy).then_inc(kvc_ready, 1)

            with act.Fori(0, ITERS) as t:
                def exps(u):
                    p, l = (p_a, l1) if u < 5 else (p_b, l2)
                    for n, i in enumerate(ORDER):
                        act.wait_ge(z_ready, 24 * t + (4 * u + n + 1))
                        n = (i + 1) * P
                        A(p[:, ZOFF[i]:ZOFF[i] + n], z[:, ZOFF[i]:ZOFF[i] + n], ACT.Exp, bias=m[:, i:i + 1],
                          scale=-1.0, accum_out=l[:, i:i + 1]).then_inc(p_exp, 1)
                    if u in (0, 2):
                        act.wait_ge(zc_ready, 2 * t + (1 + u // 2))
                        A(pc[:, :, :], zc[:, :, :], ACT.Exp, scale=SCALE).then_inc(pc_exp, 1)

                def move_pt(u):
                    act.wait_ge(pt_done, 17 * t + (U_PT[u] + 2))
                    A(pt[:, 512:1024], e[1][:, :], ACT.Copy).then_inc(pt_ready, 1)
                    if u in (0, 2):
                        act.wait_ge(pt_done, 17 * t + (U_PT[u] + 4))
                        A(pct[:, :], ob[0:NC_, :], ACT.Copy).then_inc(pt_ready, 1)

                def outputs(u):
                    if u in (1, 3):
                        act.wait_ge(pv_done, 5 * t + (u + 1))
                        A(s_hi[u // 2][:, :], ob[:, :], ACT.Copy).then_inc(o_hi_ready, 1)
                    if u == 4:
                        act.wait_ge(on_ready, 2 * t + 2)
                        for i in range(NT):
                            A(z[:, 0:DV], on[:, i, :], ACT.Square, accum_out=ss[:, i:i + 1]).then_inc(on_sq, 1)
                            act.wait_ge(on_sq, 4 * t + (i + 1))
                        act.wait_ge(on_ms, t + 1)
                        A(rstd[:, :], ms[:, :], ACT.Sqrt).then_inc(on_rstd, 1)

                def turned_o(_):
                    for h in range(2):
                        act.wait_ge(ot_done, 2 * t + (h + 1))
                        A(s_hi[2 + h][:, :], e[1 + h][:, :], ACT.Copy, scale=hgcur[:, h:h + 1]).then_inc(o_hi_ready, 1)

                for n in range(2):
                    for k in sweep(t * (2 * PAIRS) + (PAIR_G + n * PAIRS), 4 * t + (PAIR_G // RAW + 2 * n)):
                        for i in range(2):
                            for kind, u in AT.get(16 * n + 2 * k + i, ()):
                                {"S": exps, "T": move_pt, "V": outputs, "O": turned_o}[kind](u)
                    evacuate(2 * t + (JOB_G + n - 1), 2 * t + (T_JOBS + N_JOBS + n))
                for k in range(4):
                    act.wait_ge(o_spilled[k], 32 * (t + 1))

            def up(c):
                for k in sweep(c * PAIRS + PAIR_UP, 2 * c + PAIR_UP // RAW):
                    if k == 0:
                        act.wait_ge(g_landed, 32 * (c + 1))
                    if k < 2:
                        t = (ga, gb)[k]
                        A(t[:, :, :], t[:, :, :], ACT.Sigmoid).then_inc(sig_ready, 1)
                for b in range(4):
                    act.wait_ge(mix_sum, 4 * c + (b + 1))
                    A(m_hi[:, bass.ds(4 * c + b, 1), :], gb[:, b:b + 1, :], ACT.Copy).then_inc(mix_hi, 1)
            with act.Fori(0, NT) as c:
                up(c)
            with act.Fori(0, NT) as c:
                run(c * PAIRS + PAIR_OUT, 2 * c + PAIR_OUT // RAW)
            norm(res, res_s, 1, 16, h2_hi, lambda i: act.wait_ge(acc_free[i], JOB_FF + 1))

            FD = JOB_FF - 1

            def silus(done, pair_end):
                for b in range(4):
                    if b < 3:
                        act.wait_ge(acc_done, 3 * done + (b + 1))
                    else:
                        act.wait_ge(pair_done, pair_end)
                    A(silu[:, b, :], acc[b][:, :], ACT.Silu).then_inc(acc_free[b], 1)

            def f_his(done):
                for b in range(4):
                    act.wait_ge(acc_free[b], done + (FREE_AHEAD + 1))
                    A(f_hi[:, b, :], silu[:, b, :], ACT.Copy).then_inc(f_hi_ready, 1)

            run(PAIR_FF, PAIR_FF // RAW)
            silus(FD, PAIR_FF + PAIRS)
            with act.Fori(0, CHUNKS - 1) as c:
                p0 = c * FF_PAIRS + PAIR_FF
                u0 = c * (FF_PAIRS // RAW) + PAIR_FF // RAW
                run(p0 + PAIRS, u0 + 2)
                f_his(c * FF_JOBS + (FD + 1))
                run(p0 + 2 * PAIRS, u0 + 4)
                act.wait_ge(f_lo_ready, 4 * (c + 1))
                silus(c * FF_JOBS + (FD + 2), p0 + 3 * PAIRS)
                run(p0 + 3 * PAIRS, u0 + 6)
            run(PAIR_END - 2 * PAIRS, PAIR_END // RAW - 4)
            f_his(FD + 1 + (CHUNKS - 1) * FF_JOBS)
            run(PAIR_END - PAIRS, PAIR_END // RAW - 2, range(AHEAD, PAIRS))
            for i in range(NT):
                act.wait_ge(acc_free[i], JOB_FF + 2 + CHUNKS * FF_JOBS)
                A(fin_s[:, i, :], res[:, i, :], ACT.Square, accum_out=ss[:, i:i + 1]).then_inc(sq_ready, 1)
                act.wait_ge(ms_ready, 2 * NT + i + 1)
                A(rstd[:, i:i + 1], ms[:, i:i + 1], ACT.Sqrt).then_inc(rstd_ready, 1)

        @block.vector
        def _(v):
            V = nc.vector
            chained = [0]

            def link(ins):
                chained[0] += 1
                ins.then_inc(dve, 1)
                v.wait_ge(dve, chained[0])

            V.memset(tab[BUCKETS:BUCKETS + 1, :], -MASKED).then_inc(tab_masked, 1)
            v.wait_ge(cols_turned, 1)
            link(V.tensor_copy(cols[:, :], ob[:, 0:108]))
            for n in range(2):
                V.tensor_tensor(lprod[:, n:n + 1], cols[:, 40 + 2 * n:41 + 2 * n], cols[:, 41 + 2 * n:42 + 2 * n], ALU.mult)\
                    .then_inc(lprod_ready, 1)
            V.tensor_scalar(hg[:, :], cols[:, 32:40], 1.0 - LAM_INIT, None, ALU.mult).then_inc(cols_ready, 1)
            for n in range(4):
                w = min(512, ROW - 512 * n)
                v.wait_ge(brow_done, n + 1)
                V.tensor_scalar(brow[:, 512 * n:512 * n + w], acc[n][0:NH + DH, 0:w], HD ** 0.5, None, ALU.mult)\
                    .then_inc(brow_ready, 1)
            v.wait_ge(lam_exp, 1)
            link(V.tensor_tensor(neglam[:, :], lexp[:, 1:2], lexp[:, 0:1], ALU.subtract))
            link(V.tensor_scalar(neglam[:, :], neglam[:, :], -LAM_INIT, None, ALU.add))

            def mean_square(i, width, n):
                v.wait_ge(sq_ready, n)
                link(V.tensor_scalar(inv[:, i:i + 1], ss[:, i:i + 1], 1.0 / width, EPS, ALU.mult, ALU.add))
                V.reciprocal(ms[:, i:i + 1], inv[:, i:i + 1]).then_inc(ms_ready, 1)
                v.wait_ge(rstd_ready, n)

            def norm(src, scaled, n, g0, hi, lo):
                for i in range(NT):
                    mean_square(i, DM, NT * n + i + 1)
                    V.tensor_scalar(scaled[:, i, :], src[:, i, :], rstd[:, i:i + 1], None, ALU.mult).then_inc(xs_ready, 1)
                for k in range(KT):
                    v.wait_ge(n_hi, KT * n + k + 1)
                    V.scalar_tensor_tensor(out=lo[:, k, :], in0=nbanks[k % 8][:, :], scalar=cols[:, g0 + k:g0 + k + 1],
                                           in1=hi[:, k, :].bitcast(F32), op0=ALU.mult, op1=ALU.subtract)\
                        .then_inc(n_lo if k < 12 else acc_free[k - 12], 1)

            def lows(pair, k):
                v.wait_ge(hi_ready, pair + (k + AHEAD + 1))
                s = (k + AHEAD) % HL
                V.tensor_tensor(w_lo[s][:, :, :], raw[(k + AHEAD) % RAW][:, :, :], w_hi[s][:, :, :].bitcast(F32),
                                ALU.subtract).then_inc(lo_ready, 1)

            def run(pair, end=None):
                for k in range(PAIRS):
                    if end is None or k + AHEAD < end:
                        lows(pair, k)

            def evacuate(done, pair_end, spill):
                for b in (1, 3):
                    if not isinstance(spill, int) or spill > 0:
                        v.wait_ge(spilled[b], 16 * spill)
                    if b < 3:
                        v.wait_ge(acc_done, 3 * done + (b + 1))
                    else:
                        v.wait_ge(pair_done, pair_end)
                    V.tensor_copy(stage[b][:, :], acc[b][:, :]).then_inc(acc_free[b], 1)

            norm(x_in, x_s, 0, 0, h_hi, h_lo)
            v.wait_ge(wg_hi_ready, 1)
            V.tensor_tensor(wg_lo[:, :, :], wg, wg_hi[:, :, :].bitcast(F32), ALU.subtract).then_inc(wg_lo_ready, 1)
            for k in range(AHEAD):
                lows(0, k - AHEAD)
            v.wait_ge(wg_lo_ready, 1)
            run(0)
            evacuate(0, PAIRS, 0)
            with v.Fori(1, T_JOBS) as j:
                run(j * PAIRS)
                evacuate(j, (j + 1) * PAIRS, j)
            with v.Fori(0, N_JOBS) as j:
                run(j * PAIRS + PAIR_N)
                evacuate(j + JOB_N, (j + 1) * PAIRS + PAIR_N, j + JOB_N)

            v.wait_ge(c_landed, 16)
            for s in range(2):
                emb = cols[:, 44 + CL * s:44 + CL * (s + 1)]
                for g in range(NG):
                    src = c_in[:, 2 * s + g, :].rearrange("p (c j) -> p j c", j=CS)
                    c0 = g * NC_
                    V.tensor_tensor(blk[:, s, 0:CS, c0:c0 + NC_], src, emb[:, 0:CS].unsqueeze(2).to_broadcast([P, CS, NC_]),
                                    ALU.add).then_inc(blk_ready, 1)
                    V.tensor_tensor(blk[:, s, CS:CL, c0:c0 + NC_ - 1], src[:, :, 1:NC_],
                                    emb[:, CS:CL].unsqueeze(2).to_broadcast([P, CS, NC_ - 1]), ALU.add).then_inc(blk_ready, 1)
                    V.tensor_copy(blk[:, s, CS:CL, c0 + NC_ - 1:c0 + NC_], emb[:, CS:CL].unsqueeze(2)).then_inc(blk_ready, 1)
            for s in range(2):
                v.wait_ge(blk_hi_ready, s + 1)
                V.tensor_tensor(blk_lo[:, s, :, :], blk[:, s, :, :], blk_hi[:, s, :, :].bitcast(F32), ALU.subtract)\
                    .then_inc(blk_lo_ready, 1)
            run(PAIR_C)
            run(PAIR_C + PAIRS)
            v.wait_ge(kvc_done, 2)
            V.tensor_copy(vc[:, :, :], e[1][0:NC_, 0:NG * HD].rearrange("p (g n) -> p g n", g=NG)).then_inc(kvc_ready, 1)
            v.wait_ge(kvc_ready, 2)
            v.wait_ge(gates_ready, 1)

            with v.Fori(0, ITERS) as t:
                LINKS = 28
                count = [0]

                def then(ins):
                    count[0] += 1
                    ins.then_inc(chain, 1)
                    v.wait_ge(chain, LINKS * t + count[0])

                g = t // 2
                V.tensor_copy(kcur[:, :], kct[:, bass.ds(g * NC_, NC_)]).then_inc(cur_ready, 1)
                V.tensor_copy(vcur[:, :], vc[:, bass.ds(g, 1), :].rearrange("p g n -> p (g n)")).then_inc(cur_ready, 1)
                V.tensor_copy(gcur[:, :, :], gates[:, :, bass.ds(6 * t, 6)]).then_inc(cur_ready, 1)
                V.tensor_copy(hgcur[:, :], hg[:, bass.ds(2 * t, 2)]).then_inc(cur_ready, 1)
                v.wait_ge(cur_ready, 4 * t + 4)

                def softmax(u):
                    head = u // 2 if u < 4 else 2
                    if u == 0:
                        v.wait_ge(nsa_loaded, 16 * 7 * (t + 1))
                    if u == 4:
                        v.wait_ge(diff_loaded, 16 * 4 * (t + 1))
                    if u == 5:
                        v.wait_ge(p_exp, 24 * t + 20)
                    for i in ORDER:
                        b, c = SEG[i]
                        n = (i + 1) * P
                        v.wait_ge(scores_done, 18 * t + (3 * u + BANK_END[i])).then_inc(dve_waited, 1)
                        V.tensor_tensor_reduce(z[:, ZOFF[i]:ZOFF[i] + n], e[b][:, c:c + n], bias[:, head, S - n:S],
                                               -SCALE, 3.0e38, ALU.add, ALU.min, m[:, i:i + 1]).then_inc(z_ready, 1)
                    if u in (0, 2):
                        sc = e[1][:, CSEG:CSEG + NT * NC_].rearrange("p (i c) -> p i c", i=NT)
                        then(V.tensor_reduce(cm[:, :], sc, AX.X, ALU.max))
                        then(V.tensor_scalar(cr[:, :], cm[:, :], -FLOOR, None, ALU.max))
                        V.tensor_tensor(zc[:, :, :], sc, cr[:, :].unsqueeze(2).to_broadcast([P, NT, NC_]), ALU.subtract)\
                            .then_inc(zc_ready, 1)
                    v.wait_ge(p_exp, 24 * t + 4 * (u + 1))
                    if u < 4:
                        then(V.reciprocal(r1[:, :], l1[:, :]))
                        then(V.tensor_tensor(r2[:, :], r1[:, :], gcur[:, :, 3 * head + 1 + u % 2], ALU.mult))
                        for i in range(NT):
                            s = slice(ZOFF[i], ZOFF[i] + (i + 1) * P)
                            V.tensor_scalar(p_a[:, s], p_a[:, s], r2[:, i:i + 1], None, ALU.mult).then_inc(p_scaled, 1)
                    elif u == 5:
                        then(V.reciprocal(r1[:, :], l1[:, :]))
                        then(V.reciprocal(cr[:, :], l2[:, :]))
                        then(V.tensor_scalar(r2[:, :], cr[:, :], neglam[:, 0:1], None, ALU.mult))
                        for i in range(NT):
                            s = slice(ZOFF[i], ZOFF[i] + (i + 1) * P)
                            then(V.tensor_scalar(p_a[:, s], p_a[:, s], r1[:, i:i + 1], None, ALU.mult))
                        for i in range(NT):
                            s = slice(ZOFF[i], ZOFF[i] + (i + 1) * P)
                            V.scalar_tensor_tensor(out=p_b[:, s], in0=p_b[:, s], scalar=r2[:, i:i + 1], in1=p_a[:, s],
                                                   op0=ALU.mult, op1=ALU.add).then_inc(p_scaled, 1)
                    if u in (0, 2):
                        v.wait_ge(pc_exp, 2 * t + (1 + u // 2))
                        then(V.tensor_reduce(cl[:, :], pc[:, :, :], AX.X, ALU.add))
                        then(V.tensor_scalar(cm[:, :], cl[:, :], 1e-30, None, ALU.max))
                        then(V.reciprocal(cr[:, :], cm[:, :]))
                        then(V.tensor_tensor(cl[:, :], cr[:, :], gcur[:, :, 3 * head], ALU.mult))
                        V.tensor_tensor(pc[:, :, :], pc[:, :, :], cl[:, :].unsqueeze(2).to_broadcast([P, NT, NC_]), ALU.mult)\
                            .then_inc(pc_scaled, 1)

                def move_pt(u):
                    v.wait_ge(pt_done, 17 * t + (U_PT[u] + 1))
                    V.tensor_copy(pt[:, 0:512], e[0][:, :]).then_inc(pt_ready, 1)
                    v.wait_ge(pt_done, 17 * t + (U_PT[u] + 3))
                    V.tensor_copy(pt[:, 1024:1280], e[2][:, 0:256]).then_inc(pt_ready, 1)

                def outputs(u):
                    if u in (1, 3):
                        v.wait_ge(o_hi_ready, 4 * t + (1 + u // 2))
                        V.tensor_tensor(s_lo[u // 2][:, :], ob[:, :], s_hi[u // 2][:, :].bitcast(F32), ALU.subtract)\
                            .then_inc(o_lo_ready, 1)
                    if u == 4:
                        v.wait_ge(pv_done, 5 * t + 5)
                        for n, o in enumerate((ob, e[0])):
                            V.tensor_copy(on[:, 2 * n:2 * n + 2, :], o[:, :].rearrange("p (i n) -> p i n", i=2)).then_inc(on_ready, 1)
                        v.wait_ge(on_sq, 4 * t + 4)
                        then(V.tensor_scalar(inv[:, :], ss[:, :], 1.0 / DV, EPS, ALU.mult, ALU.add))
                        V.reciprocal(ms[:, :], inv[:, :]).then_inc(on_ms, 1)
                        v.wait_ge(on_rstd, t + 1)
                        V.tensor_tensor(on[:, :, :], on[:, :, :], rstd[:, :].unsqueeze(2).to_broadcast([P, NT, DV]), ALU.mult)\
                            .then_inc(on_scaled, 1)

                def turned_o(_):
                    for h in range(2):
                        v.wait_ge(o_hi_ready, 4 * t + (3 + h))
                        V.scalar_tensor_tensor(out=s_lo[2 + h][:, :], in0=e[1 + h][:, :], scalar=hgcur[:, h:h + 1],
                                               in1=s_hi[2 + h][:, :].bitcast(F32), op0=ALU.mult, op1=ALU.subtract)\
                            .then_inc(o_lo_ready, 1)

                for n in range(2):
                    for k in range(PAIRS):
                        lows(t * (2 * PAIRS) + (PAIR_G + n * PAIRS), k)
                        for i in range(2):
                            for kind, u in AT.get(16 * n + 2 * k + i, ()):
                                {"S": softmax, "T": move_pt, "V": outputs, "O": turned_o}[kind](u)
                    evacuate(2 * t + (JOB_G + n - 1), t * (2 * PAIRS) + (PAIR_G + (n + 1) * PAIRS), 2 * t + (T_JOBS + N_JOBS + n))
                for k in range(4):
                    v.wait_ge(o_spilled[k], 32 * (t + 1))
                assert count[0] == LINKS

            with v.Fori(0, NT) as c:
                done = 2 * c + (JOB_UP - 1)
                first = c * PAIRS + PAIR_UP
                for n in range(2):
                    for k in range(4 * n, 4 * n + 4):
                        lows(first, k)
                    for b in range(4):
                        if b < 3:
                            v.wait_ge(acc_done, 3 * done + (3 * n + b + 1))
                        else:
                            v.wait_ge(pair_done, first + 4 * (n + 1))
                        if b == 0:
                            v.wait_ge(sig_ready, 2 * c + (n + 1))
                        t = (ga, gb)[n]
                        V.tensor_tensor(t[:, b, :], acc[b][:, :], t[:, b, :], ALU.mult).then_inc(acc_free[b], 1)
                for b in range(4):
                    v.wait_ge(acc_free[b], 2 * c + (JOB_UP + 3))
                    V.tensor_tensor(gb[:, b, :], ga[:, b, :], gb[:, b, :], ALU.add).then_inc(mix_sum, 1)
                for b in range(4):
                    v.wait_ge(mix_hi, 4 * c + (b + 1))
                    V.tensor_tensor(m_lo[:, bass.ds(4 * c + b, 1), :], gb[:, b:b + 1, :],
                                    m_hi[:, bass.ds(4 * c + b, 1), :].bitcast(F32), ALU.subtract).then_inc(mix_lo, 1)

            with v.Fori(0, NT) as c:
                run(c * PAIRS + PAIR_OUT)
                for b in range(4):
                    if b < 3:
                        v.wait_ge(acc_done, 3 * c + (3 * (JOB_OUT - 1) + b + 1))
                    else:
                        v.wait_ge(pair_done, (c + 1) * PAIRS + PAIR_OUT)
                    if b == 0:
                        v.wait_ge(res_landed, 16 * NT)
                    r = res[:, b, bass.ds(c * COLS, COLS)]
                    V.tensor_tensor(r, acc[b][:, :], r, ALU.add).then_inc(acc_free[b], 1)

            norm(res, res_s, 1, 16, h2_hi, h2_lo)
            FD = JOB_FF - 1

            def take_b(done, pair_end, c):
                for b in range(4):
                    if b < 3:
                        v.wait_ge(acc_done, 3 * done + (b + 1))
                    else:
                        v.wait_ge(pair_done, pair_end)
                    v.wait_ge(acc_free[b], done + FREE_AHEAD)
                    V.tensor_tensor(silu[:, b, :], acc[b][:, :], silu[:, b, :], ALU.mult).then_inc(acc_free[b], 1)
                for b in range(4):
                    v.wait_ge(f_hi_ready, 4 * c + (b + 1))
                    V.tensor_tensor(f_lo[:, b, :], silu[:, b, :], f_hi[:, b, :].bitcast(F32), ALU.subtract).then_inc(f_lo_ready, 1)

            def add_out(done, pair_end, n):
                for b in range(4):
                    if b < 3:
                        v.wait_ge(acc_done, 3 * done + (b + 1))
                    else:
                        v.wait_ge(pair_done, pair_end)
                    r = res[:, b, n * COLS:(n + 1) * COLS]
                    V.tensor_tensor(r, acc[b][:, :], r, ALU.add).then_inc(acc_free[b], 1)

            def outs(first, done):
                for n in range(NT):
                    for k in range(2):
                        yield 2 * n + k
                    add_out(done + n, first + 2 * (n + 1), n)

            run(PAIR_FF)
            with v.Fori(0, CHUNKS - 1) as c:
                p0 = c * FF_PAIRS + PAIR_FF
                run(p0 + PAIRS)
                take_b(c * FF_JOBS + (FD + 1), p0 + 2 * PAIRS, c)
                run(p0 + 2 * PAIRS)
                for k in outs(p0 + 3 * PAIRS, c * FF_JOBS + (FD + 3)):
                    lows(p0 + 3 * PAIRS, k)
            last = FD + (CHUNKS - 1) * FF_JOBS
            run(PAIR_END - 2 * PAIRS)
            take_b(last + 1, PAIR_END - PAIRS, CHUNKS - 1)
            for k in outs(PAIR_END - PAIRS, last + 2):
                if k + AHEAD < PAIRS:
                    lows(PAIR_END - PAIRS, k)

            v.wait_ge(fg_landed, 16)
            for i in range(NT):
                mean_square(i, DM, 2 * NT + i + 1)
                V.scalar_tensor_tensor(out=fin[:, i, :], in0=res[:, i, :], scalar=rstd[:, i:i + 1], in1=fg[:, :],
                                       op0=ALU.mult, op1=ALU.mult).then_inc(fin_ready, 1)


def kernel(**inputs):
    import concourse.bacc as bacc
    from concourse.bass_utils import run_bass_kernel_spmd

    a = {k: np.ascontiguousarray(v) for k, v in inputs.items()}
    w = a["w_in"][0]
    widths = [1024, 256, 256, 256, 256, 256, 256, 24, 1024, 1024, 1024, 4096]
    q_n, kc, vc, ksl, vsl, kw, vw, g_n, q_d, k_d, v_d, g_m = np.split(w, np.cumsum(widths)[:-1], axis=1)
    arrays = {
        "x": a["x"][0],
        "w_proj": np.concatenate([q_n, kc, vc, ksl, kw, q_d, k_d, g_m, vsl, vw, v_d, g_n], axis=1),
        "pe_k": a["cmp_pe_k"][0], "pe_v": a["cmp_pe_v"][0],
        "cw1": np.concatenate([a["cmp_w1_k"], a["cmp_w1_v"]], axis=0),
        "cw2": np.concatenate([a["cmp_w2_k"], a["cmp_w2_v"]], axis=0),
        "lq1": a["diff_lq1"][0], "lk1": a["diff_lk1"][0], "lq2": a["diff_lq2"][0], "lk2": a["diff_lk2"][0],
        "head_g": a["diff_head_g"][0], "mix_g": a["norm_mix_g"][0], "ff_g": a["norm_ff_g"][0],
        "final_g": a["norm_final_g"],
        "w_up": np.concatenate([a["w_up_nsa"][0], a["w_up_diff"][0]], axis=0),
        "w_out": a["w_out"][0], "w_ff_in": a["w_ff_in"][0], "w_ff_out": a["w_ff_out"][0],
        "table": a["rel_bias_table"], "onehot": bucket_onehot(),
    }
    nc = bacc.Bacc("TRN2", target_bir_lowering=False, num_devices=1)
    args = {}
    feed = {}
    for name, v in arrays.items():
        v = np.ascontiguousarray(v)
        feed[f"in_{name}"] = v
        args[name] = nc.dram_tensor(f"in_{name}", v.shape, mybir.dt.from_np(v.dtype), kind="ExternalInput").ap()
    out = nc.dram_tensor("out_0", (S, DM), F32, kind="ExternalOutput").ap()
    build(nc, **args, out=out)
    r = run_bass_kernel_spmd(nc, [feed], core_ids=[0])
    return r.results[0]["out_0"].reshape(1, S, DM)
```

```python
import math
from contextlib import ExitStack

import numpy as np

import concourse.bass as bass
from concourse import mybir

F32 = mybir.dt.float32
F32R = mybir.dt.float32r
ALU = mybir.AluOpType
ACT = mybir.ActivationFunctionType
AX = mybir.AxisListType

P = 128
S = 512
DM = 2048
HD = 128
NT = S // P
KT = DM // P
NH, NG, DH = 8, 2, 4
DV = 2 * HD
CL, CS = 32, 16
NC_ = S // CS
CH = 256
DFF = 5632
BUCKETS, MAX_EXACT, MAX_DIST = 32, 16, 128
EPS = 1e-6
SCALE = HD ** -0.5
LAM_INIT = 0.8 - 0.6 * math.exp(0.0)
MASKED = 1e30
FLOOR = 1e29
COLS = 512
PAIRS = KT // 2
RAW = 4
HL = 4
AHEAD = 2

T_JOBS = 8
G_JOBS = 8
N_JOBS = 3
N_COL0 = (T_JOBS + G_JOBS) * COLS
GN_COL0 = N_COL0 + N_JOBS * COLS
GN = 3 * NH
C_TILE, K_TILE, QD_TILE, KD_TILE, G_TILE = 8, 12, 16, 24, 32
REV = 640
FWD = 1024
FWD0 = S + CL // 2 - 1
ROW = REV + FWD
FF_CHUNK = 4
CHUNKS = DFF // (FF_CHUNK * P)
FF_PAIRS = 3 * PAIRS
PAIR_N = T_JOBS * PAIRS
PAIR_C = PAIR_N + N_JOBS * PAIRS
PAIR_G = PAIR_C + 2 * PAIRS
PAIR_UP = PAIR_G + G_JOBS * PAIRS
PAIR_OUT = PAIR_UP + NT * PAIRS
PAIR_FF = PAIR_OUT + NT * PAIRS
PAIR_END = PAIR_FF + CHUNKS * FF_PAIRS
JOB_N = T_JOBS
JOB_C = JOB_N + N_JOBS
JOB_G = JOB_C + 1
JOB_UP = JOB_G + G_JOBS
JOB_OUT = JOB_UP + 2 * NT
JOB_FF = JOB_OUT + NT
FF_JOBS = 6
FREE_AHEAD = 1
ITERS = DH
ORDER = (0, 2, 1, 3)
BANK_END = {0: 1, 2: 1, 1: 2, 3: 3}
U_PT = (0, 4, 7, 11, 14, 17)
AT = {3: [("S", 0)], 6: [("T", 0)], 7: [("V", 0), ("S", 1)], 10: [("T", 1)], 11: [("V", 1), ("S", 2)],
      14: [("T", 2)], 15: [("V", 2), ("S", 3)], 18: [("T", 3)], 19: [("V", 3), ("S", 4)],
      21: [("S", 5)], 25: [("T", 4)], 26: [("V", 4)], 29: [("O", 0)]}


def bucket_onehot():
    n = np.arange(S)
    large = MAX_EXACT + (np.log(np.maximum(n, 1) / MAX_EXACT) / math.log(MAX_DIST / MAX_EXACT)
                         * (BUCKETS - MAX_EXACT)).astype(np.int32)
    bucket = np.where(n < MAX_EXACT, n, np.minimum(large, BUCKETS - 1))
    rel = np.concatenate([S - 1 - np.arange(REV), np.arange(FWD) - FWD0])
    row = np.where((rel < 0) | (rel >= S), BUCKETS, bucket[np.clip(rel, 0, S - 1)])
    return (np.arange(BUCKETS + 1)[:, None] == row[None, :]).astype(np.float32)


def build(nc, x, w_proj, pe_k, pe_v, cw1, cw2, lq1, lk1, lq2, lk2, head_g, mix_g, ff_g, final_g,
          w_up, w_out, w_ff_in, w_ff_out, table, onehot, out):
    ctx = ExitStack()
    with ctx:
        proj_t = nc.dram_tensor("proj_t", [(T_JOBS + G_JOBS) * NT, P, S], F32).ap()
        proj_n = nc.dram_tensor("proj_n", [NT, P, N_JOBS * COLS], F32).ap()
        o_hi_d = nc.dram_tensor("o_hi_d", [KT, P, S], F32).ap()
        o_lo_d = nc.dram_tensor("o_lo_d", [KT, P, S], F32).ap()
        bias_d = nc.dram_tensor("bias_d", [NH + DH, ROW], F32).ap()

        skew_d = nc.dram_tensor("skew_d", [NH + DH, P * (REV + 1)], F32).ap()
        cskew_d = nc.dram_tensor("cskew_d", [NH, NC_ * (FWD + CS)], F32).ap()
        skew_w = skew_d.rearrange("h (p r) -> h p r", p=P)
        cskew_w = cskew_d.rearrange("h (c r) -> h c r", c=NC_)
        skew_r = skew_d[:, 0:P * REV].rearrange("h (p r) -> h p r", p=P)
        cskew_r = cskew_d[:, 0:NC_ * FWD].rearrange("h (c r) -> h c r", c=NC_)

        base = (nc.sbuf_base + 63) // 64 * 64
        KB = 1024
        R1, R2 = base, base + 64 * KB
        RING = base + 128 * KB
        MISC = RING + 48 * KB

        def at(name, shape, offset, dt=F32):
            return nc.alloc_sbuf_tensor_at(name, shape, dt, offset=offset)

        h_hi = at("h_hi", [P, KT, S], R1, F32R)
        h_lo = at("h_lo", [P, KT, S], R1 + 32 * KB, F32R)
        o_hi = at("o_hi", [P, KT, S], R1, F32R)
        o_lo = at("o_lo", [P, KT, S], R1 + 32 * KB, F32R)
        res = at("res", [P, NT, DM], R1)
        res_s = at("res_s", [P, NT, DM], R1 + 32 * KB)
        silu = at("silu", [P, FF_CHUNK, S], R1 + 32 * KB)
        f_hi = at("f_hi", [P, FF_CHUNK, S], R1 + 40 * KB, F32R)
        f_lo = at("f_lo", [P, FF_CHUNK, S], R1 + 48 * KB, F32R)
        fg = at("fg", [P, DM], R1 + 56 * KB)
        x_in = at("x_in", [P, NT, DM], R2)
        x_s = at("x_s", [P, NT, DM], R2 + 32 * KB)
        m_hi = at("m_hi", [P, KT, S], R2, F32R)
        m_lo = at("m_lo", [P, KT, S], R2 + 32 * KB, F32R)
        h2_hi = at("h2_hi", [P, KT, S], R2, F32R)
        h2_lo = at("h2_lo", [P, KT, S], R2 + 32 * KB, F32R)
        fin = at("fin", [P, NT, DM], R2)
        fin_s = at("fin_s", [P, NT, DM], R2 + 32 * KB)
        c_in = at("c_in", [P, 4, S], R2)
        blk = at("blk", [P, 2, CL, NG * NC_], R2 + 8 * KB)
        blk_hl = at("blk_hl", [P, 2, CL, 2 * NG * NC_], R2 + 24 * KB, F32R)
        hid = at("hid", [P, 2, 2, NG * NC_], R2 + 56 * KB)
        w2 = at("w2", [P, 2, 2, HD], R2 + 57 * KB)
        hid_hl = at("hid_hl", [P, 2, CH], R2 + 59 * KB)
        gates_t = at("gates_t", [GN, S], R2 + 61 * KB)
        wg_hi = at("wg_hi", [P, KT, P], R2 + 8 * KB, F32R)
        wg_lo = at("wg_lo", [P, KT, P], R2 + 16 * KB, F32R)
        q2 = at("q2", [P, 2, S], R2)
        k2 = at("k2", [P, 2, S], R2 + 4 * KB)
        v2 = at("v2", [P, NT, 2, HD], R2 + 8 * KB)
        qd = at("qd", [P, 2, S], R2 + 12 * KB)
        kd = at("kd", [P, 2, S], R2 + 16 * KB)
        vd = at("vd", [P, NT, DV], R2 + 20 * KB)
        bias = at("bias", [P, 3, S], R2 + 24 * KB)
        cbias = at("cbias", [NC_, 2, S], R2 + 30 * KB)
        z = at("z", [P, 1280], R2 + 34 * KB)
        p_a = at("p_a", [P, 1280], R2 + 39 * KB)
        p_b = at("p_b", [P, 1280], R2 + 44 * KB)
        pt = at("pt", [P, 1280], R2 + 49 * KB)
        zc = at("zc", [P, NT, NC_], R2 + 54 * KB)
        pc = at("pc", [P, NT, NC_], R2 + 54 * KB + 512)
        pct = at("pct", [NC_, S], R2 + 55 * KB)
        on = at("on", [P, NT, DV], R2 + 57 * KB)
        raw = [at(f"raw{s}", [P, 2, COLS], RING + 4 * KB * s) for s in range(RAW)]
        w_hi = [at(f"w_hi{s}", [P, 2, COLS], RING + 16 * KB + 4 * KB * s, F32R) for s in range(HL)]
        w_lo = [at(f"w_lo{s}", [P, 2, COLS], RING + 32 * KB + 4 * KB * s, F32R) for s in range(HL)]
        stage = [at(f"stage{b}", [P, S], MISC + 2 * KB * b) for b in range(4)]
        oh = at("oh", [BUCKETS + 1, ROW], MISC + 8 * KB)
        brow = at("brow", [NH + DH, ROW], MISC + 15 * KB)
        s_hi = [at(f"s_hi{k}", [P, S], MISC + 8 * KB + 2 * KB * k, F32R) for k in range(4)]
        s_lo = [at(f"s_lo{k}", [P, S], MISC + 16 * KB + 2 * KB * k, F32R) for k in range(4)]
        ga = at("ga", [P, NT, S], MISC + 8 * KB)
        gb = at("gb", [P, NT, S], MISC + 16 * KB)
        top = [MISC + 24 * KB]

        def small(name, shape, dt=F32):
            n = int(np.prod(shape[1:])) * 4
            t = at(name, shape, top[0], dt)
            top[0] += (n + 31) // 32 * 32
            return t

        ident = small("ident", [P, P])
        rows = at("rows", [108, P], MISC + 22 * KB)
        cols = small("cols", [P, 108])
        tab = small("tab", [BUCKETS + 1, NH + DH])
        wg = at("wg", [P, KT, GN], MISC + 22 * KB + 512)
        twice = small("twice", [P, NG * NC_])
        gates = small("gates", [P, NT, GN])
        gcur = small("gcur", [P, NT, 6])
        ones = small("ones", [P, P])
        kct = small("kct", [P, NG * NC_])
        kcur = small("kcur", [P, NC_])
        vc = small("vc", [NC_, NG, HD])
        vcur = small("vcur", [NC_, HD])
        hg = small("hg", [P, 2 * DH])
        hgcur = small("hgcur", [P, 2])
        lprod = small("lprod", [P, 2])
        lexp = small("lexp", [P, 2])
        neglam = small("neglam", [P, 1])
        ss = small("ss", [P, NT])
        ssp = small("ssp", [P, NT, NT])
        ms = small("ms", [P, NT])
        rstd = small("rstd", [P, NT])
        inv = small("inv", [P, NT])
        m = small("m", [P, NT])
        l1 = small("l1", [P, NT])
        l2 = small("l2", [P, NT])
        r1 = small("r1", [P, NT])
        r2 = small("r2", [P, NT])
        cm = small("cm", [P, NT])
        cl = small("cl", [P, NT])
        cr = small("cr", [P, NT])
        assert top[0] <= nc.sbuf_usable_end, (top[0], nc.sbuf_usable_end)

        def bank(name):
            return ctx.enter_context(nc.psum_tensor(name, [P, 512], F32))

        acc = [bank(f"acc{b}") for b in range(4)]
        e = [bank(f"e{b}") for b in range(3)]
        ob = bank("ob")
        bbanks = [e[1], e[2], ob, e[1]]
        nbanks = e + [ob]

        SEG = [(0, 0), (1, 0), (0, 128), (2, 0)]
        CSEG = 256
        ZOFF = [0, 128, 384, 768]
        TSEG = [(0, 0), (1, 0), (2, 0), (1, 384)]

        def sem(name):
            return ctx.enter_context(nc.semaphore(name))

        pool_waited, dve_waited = sem("pool_waited"), sem("dve_waited")
        x_landed = [sem(f"x_landed{i}") for i in range(NT)]
        w_landed = [sem(f"w_landed{s}") for s in range(RAW)]
        hi_ready = sem("hi_ready")
        lo_ready = sem("lo_ready")
        pair_done = sem("pair_done")
        acc_done = sem("acc_done")
        acc_free = [sem(f"acc_free{b}") for b in range(4)]
        spilled = [sem(f"spilled{b}") for b in range(4)]
        rows_landed, tab_landed, oh_landed, wg_landed = sem("rows_landed"), sem("tab_landed"), sem("oh_landed"), sem("wg_landed")
        tab_masked = sem("tab_masked")
        ident_ready, ones_ready = sem("ident_ready"), sem("ones_ready")
        cols_turned, cols_ready = sem("cols_turned"), sem("cols_ready")
        brow_done, brow_ready, brow_spilled = sem("brow_done"), sem("brow_ready"), sem("brow_spilled")
        skewed = sem("skewed")
        hg_ready, lprod_ready, lam_sum, lam_exp = sem("hg_ready"), sem("lprod_ready"), sem("lam_sum"), sem("lam_exp")
        dve = sem("dve")
        sq_ready, ms_ready, rstd_ready, xs_ready = sem("sq_ready"), sem("ms_ready"), sem("rstd_ready"), sem("xs_ready")
        turned, n_hi, n_lo = sem("turned"), sem("n_hi"), sem("n_lo")
        wg_padded, wg_hi_ready, wg_lo_ready, gn_done = sem("wg_padded"), sem("wg_hi_ready"), sem("wg_lo_ready"), sem("gn_done")
        gates_t_ready, gates_turned, gates_ready = sem("gates_t_ready"), sem("gates_turned"), sem("gates_ready")
        c_landed, w2_landed = sem("c_landed"), sem("w2_landed")
        twice_ready, blk_ready, blk_hi_ready, blk_lo_ready = sem("twice_ready"), sem("blk_ready"), sem("blk_hi_ready"), sem("blk_lo_ready")
        hid_done, kvc_done, kvc_ready = sem("hid_done"), sem("kvc_done"), sem("kvc_ready")
        nsa_loaded, diff_loaded = sem("nsa_loaded"), sem("diff_loaded")
        cur_ready = sem("cur_ready")
        scores_done, z_ready, p_exp, p_scaled = sem("scores_done"), sem("z_ready"), sem("p_exp"), sem("p_scaled")
        zc_ready, pc_exp, pc_scaled = sem("zc_ready"), sem("pc_exp"), sem("pc_scaled")
        pt_done, pt_ready, pv_done = sem("pt_done"), sem("pt_ready"), sem("pv_done")
        o_hi_ready, o_lo_ready = sem("o_hi_ready"), sem("o_lo_ready")
        o_spilled = [sem(f"o_spilled{k}") for k in range(4)]
        on_ready, on_sq, on_ms, on_rstd, on_scaled, ot_done = (sem("on_ready"), sem("on_sq"), sem("on_ms"),
                                                               sem("on_rstd"), sem("on_scaled"), sem("ot_done"))
        chain = sem("chain")
        o_landed = [sem(f"o_landed{k}") for k in range(PAIRS)]
        g_landed = [sem("ga_landed"), sem("gb_landed")]
        sig_ready, mix_sum, mix_hi, mix_lo = sem("sig_ready"), sem("mix_sum"), sem("mix_hi"), sem("mix_lo")
        res_landed = sem("res_landed")
        f_hi_ready, f_lo_ready = sem("f_hi_ready"), sem("f_lo_ready")
        fg_landed, fin_ready, out_stored = sem("fg_landed"), sem("fin_ready"), sem("out_stored")

        w_proj_v = w_proj.rearrange("(k p) n -> p k n", p=P)
        w_up_v = w_up.rearrange("(k p) n -> p k n", p=P)
        w_out_v = w_out.rearrange("(k p) n -> p k n", p=P)
        w_ff_in_v = w_ff_in.rearrange("(k p) n -> p k n", p=P)
        w_ff_out_v = w_ff_out.rearrange("(c k p) n -> p c k n", p=P, k=FF_CHUNK)
        cw1_v = cw1.rearrange("s (j p) n -> s p j n", p=P)
        x_v = x.rearrange("(i p) n -> p i n", p=P)
        out_v = out.rearrange("(i p) n -> p i n", p=P)
        pt_v = proj_t.rearrange("f p s -> p f s")
        pn_v = proj_n.rearrange("i p n -> p i n")

        block = ctx.enter_context(nc.Block())

        @block.sync
        def _(sp):
            for i in range(NT):
                sp.dma_start(x_in[:, i, :], x_v[:, i, :]).then_inc(x_landed[i], 16)

            def load(pair, k, source):
                if not isinstance(pair, int) or pair >= RAW:
                    sp.wait_ge(lo_ready, pair - RAW + 1)
                sp.dma_start(raw[k % RAW][:, :, :], source).then_inc(w_landed[k % RAW], 16)

            def job(pair, weights, col):
                for k in range(PAIRS):
                    load(pair + k, k, weights[:, 2 * k:2 * k + 2, bass.ds(col, COLS)])

            job(0, w_proj_v, 0)
            with sp.Fori(1, T_JOBS) as j:
                job(j * PAIRS, w_proj_v, j * COLS)
            with sp.Fori(0, N_JOBS) as j:
                job(j * PAIRS + PAIR_N, w_proj_v, j * COLS + N_COL0)
            for s in range(2):
                for k in range(PAIRS):
                    load(PAIR_C + PAIRS * s + k, k,
                         cw1_v[s, :, 4 * k:4 * k + 4, :])
            with sp.Fori(0, G_JOBS) as j:
                job(j * PAIRS + PAIR_G, w_proj_v, (j + T_JOBS) * COLS)
            with sp.Fori(0, NT) as c:
                job(c * PAIRS + PAIR_UP, w_up_v, c * COLS)
            with sp.Fori(0, NT) as c:
                job(c * PAIRS + PAIR_OUT, w_out_v, c * COLS)
            def ff_out(pair, c):
                for n in range(NT):
                    for k in range(2):
                        load(pair + 2 * n + k, 2 * n + k,
                             w_ff_out_v[:, bass.ds(c, 1), 2 * k:2 * k + 2, n * COLS:(n + 1) * COLS].rearrange("p c k n -> p (c k) n"))
            job(PAIR_FF, w_ff_in_v, 0)
            with sp.Fori(0, CHUNKS - 1) as c:
                job(c * FF_PAIRS + PAIR_FF + PAIRS, w_ff_in_v, c * COLS + DFF)
                job(c * FF_PAIRS + PAIR_FF + 2 * PAIRS, w_ff_in_v, c * COLS + COLS)
                ff_out(c * FF_PAIRS + PAIR_FF + 3 * PAIRS, c)
            job(PAIR_END - 2 * PAIRS, w_ff_in_v, (CHUNKS - 1) * COLS + DFF)
            ff_out(PAIR_END - PAIRS, CHUNKS - 1)
            for i in range(NT):
                sp.wait_ge(fin_ready, i + 1)
                sp.dma_start(out_v[:, i, :], fin[:, i, :]).then_inc(out_stored, 16)
            sp.wait_ge(out_stored, 16 * NT)

        @block.gpsimd
        def _(pool):
            pool.memset(ident[:, :], 0.0).then_inc(ident_ready, 1)
            pool.wait_ge(ident_ready, 1)
            pool.affine_select(out=ident[:, :], in_=ident[:, :], compare_op=ALU.not_equal, fill=1.0, base=0,
                               pattern=[[-1, P]], channel_multiplier=1).then_inc(ident_ready, 1)
            pool.memset(ones[:, :], 1.0).then_inc(ones_ready, 1)
            pool.dma_start(tab[0:BUCKETS, :], table).then_inc(tab_landed, 16)
            pool.dma_start(oh[:, :], onehot).then_inc(oh_landed, 16)
            pool.dma_start(wg[:, :, :], w_proj_v[:, :, GN_COL0:GN_COL0 + GN]).then_inc(wg_landed, 16)
            pool.wait_ge(xs_ready, NT * NT)
            pool.memset(wg_hi[:, :, GN:P].bitcast(F32), 0.0).then_inc(wg_padded, 1)
            pool.memset(wg_lo[:, :, GN:P].bitcast(F32), 0.0).then_inc(wg_padded, 1)

            def spill_t(j, tile0, job):
                for b in range(4):
                    pool.wait_ge(acc_free[b], job + 1).then_inc(pool_waited, 1)
                    pool.dma_start(pt_v[:, bass.ds(tile0 + b, 1), :].rearrange("p f s -> p (f s)"),
                                   stage[b][:, :]).then_inc(spilled[b], 16)

            with pool.Fori(0, T_JOBS) as j:
                spill_t(j, j * NT, j)
            for b in range(4):
                pool.wait_ge(spilled[b], 16 * T_JOBS)
            pool.dma_start(c_in[:, :, :], pt_v[:, C_TILE:C_TILE + 4, :]).then_inc(c_landed, 16)
            pool.wait_ge(gn_done, 1)
            pool.dma_start(w2[:, :, :, :], cw2.rearrange("s (k p) n -> p s k n", p=P)).then_inc(w2_landed, 16)
            pool.wait_ge(brow_ready, 4)
            pool.dma_start(bias_d, brow[:, :]).then_inc(brow_spilled, 16)
            pool.wait_ge(brow_spilled, 16)
            for h in range(NH + DH):
                pool.dma_start(skew_w[h, :, 0:REV], bias_d[h:h + 1, 0:REV].to_broadcast([P, REV])).then_inc(skewed, 16)
            for h in range(NH):
                pool.dma_start(cskew_w[h, :, 0:FWD], bias_d[h:h + 1, REV:ROW].to_broadcast([NC_, FWD])).then_inc(skewed, 16)


            with pool.Fori(0, N_JOBS) as j:
                for b in range(4):
                    pool.wait_ge(acc_free[b], j + (JOB_N + 1)).then_inc(pool_waited, 1)
                    pool.dma_start(proj_n[b, :, bass.ds(j * COLS, COLS)], stage[b][:, :]).then_inc(spilled[b], 16)
            for b in range(4):
                pool.wait_ge(spilled[b], 16 * (T_JOBS + N_JOBS))

            def load_nsa(t, g):
                pool.dma_start(q2[:, :, :], pt_v[:, bass.ds(2 * t, 2), :]).then_inc(nsa_loaded, 16)
                for n in range(2):
                    pool.dma_start(k2[:, n, :], pt_v[:, bass.ds(g + (K_TILE + 2 * n), 1), :].rearrange("p f s -> p (f s)"))\
                        .then_inc(nsa_loaded, 16)
                for n in range(2):
                    pool.dma_start(v2[:, :, n, :], pn_v[:, :, bass.ds(g * HD + n * DV, HD)]).then_inc(nsa_loaded, 16)

            def load_nsa_bias(t):
                pool.dma_start(bias[:, 0:2, :], skew_r[bass.ds(2 * t, 2), :, P - 1:P - 1 + S].rearrange("h p s -> p h s"))\
                    .then_inc(nsa_loaded, 16)
                pool.dma_start(cbias[:, :, :], cskew_r[bass.ds(2 * t, 2), :, FWD0 - CL + 1:FWD0 - CL + 1 + S]
                               .rearrange("h c s -> c h s")).then_inc(nsa_loaded, 16)

            def load_diff(t):
                pool.dma_start(qd[:, :, :], pt_v[:, bass.ds(2 * t + QD_TILE, 2), :]).then_inc(diff_loaded, 16)
                pool.dma_start(kd[:, :, :], pt_v[:, bass.ds(2 * t + KD_TILE, 2), :]).then_inc(diff_loaded, 16)
                pool.dma_start(vd[:, :, :], pn_v[:, :, bass.ds(t * DV + COLS, DV)]).then_inc(diff_loaded, 16)

            def load_diff_bias(t):
                pool.dma_start(bias[:, 2, :], skew_r[bass.ds(t + NH, 1), :, P - 1:P - 1 + S].rearrange("h p s -> p (h s)"))\
                    .then_inc(diff_loaded, 16)

            pool.wait_ge(blk_lo_ready, 2)
            load_nsa(0, 0)
            load_diff(0)
            pool.wait_ge(skewed, 16 * (2 * NH + DH))
            pool.wait_ge(pair_done, PAIR_C + PAIRS)
            load_nsa_bias(0)
            load_diff_bias(0)

            def spill_o(slot, ready, tile):
                pool.wait_ge(o_lo_ready, ready).then_inc(pool_waited, 1)
                pool.dma_start(o_hi_d[bass.ds(tile, 1), :, :].rearrange("f p s -> (f p) s"),
                               s_hi[slot][:, :].bitcast(F32)).then_inc(o_spilled[slot], 16)
                pool.dma_start(o_lo_d[bass.ds(tile, 1), :, :].rearrange("f p s -> (f p) s"),
                               s_lo[slot][:, :].bitcast(F32)).then_inc(o_spilled[slot], 16)

            with pool.Fori(0, ITERS - 1) as t:
                spill_o(0, 4 * t + 1, 2 * t)
                spill_t(0, 8 * t + G_TILE, 2 * t + JOB_G)
                spill_o(1, 4 * t + 2, 2 * t + 1)
                load_nsa(t + 1, (t + 1) // 2)
                load_nsa_bias(t + 1)
                spill_o(2, 4 * t + 3, 2 * t + NH)
                spill_o(3, 4 * t + 4, 2 * t + (NH + 1))
                load_diff(t + 1)
                load_diff_bias(t + 1)
                spill_t(0, 8 * t + (G_TILE + 4), 2 * t + (JOB_G + 1))

            def reload_o(ks):
                for k in ks:
                    pool.wait_ge(pair_done, PAIR_UP - PAIRS + k + 1)
                    for d, t in ((o_hi_d, o_hi), (o_lo_d, o_lo)):
                        pool.dma_start(t[:, 2 * k:2 * k + 2, :].bitcast(F32),
                                       d[2 * k:2 * k + 2].rearrange("f p s -> p f s")).then_inc(o_landed[k], 16)

            t = ITERS - 1
            spill_o(0, 4 * t + 1, 2 * t)
            spill_t(0, 8 * t + G_TILE, 2 * t + JOB_G)
            spill_o(1, 4 * t + 2, 2 * t + 1)
            for k in range(2):
                pool.wait_ge(o_spilled[k], 32 * ITERS)
            reload_o(range(4))
            spill_o(2, 4 * t + 3, 2 * t + NH)
            spill_o(3, 4 * t + 4, 2 * t + (NH + 1))
            for k in range(2, 4):
                pool.wait_ge(o_spilled[k], 32 * ITERS)
            reload_o(range(4, PAIRS))
            for b in range(4):
                pool.wait_ge(spilled[b], 16 * (T_JOBS + N_JOBS + G_JOBS - 1))
            for n, t in enumerate((ga, gb)):
                pool.dma_start(t[:, :, :], pt_v[:, G_TILE + KT * n:G_TILE + KT * n + NT, :]).then_inc(g_landed[n], 16)
            spill_t(0, 8 * (ITERS - 1) + (G_TILE + 4), JOB_UP - 1)
            for b in range(4):
                pool.wait_ge(spilled[b], 16 * (T_JOBS + N_JOBS + G_JOBS))
            with pool.Fori(1, NT) as c:
                pool.wait_ge(mix_lo, c * NT).then_inc(pool_waited, 1)
                for n, t in enumerate((ga, gb)):
                    pool.dma_start(t[:, :, :], pt_v[:, bass.ds(c * NT + (G_TILE + KT * n), NT), :]).then_inc(g_landed[n], 16)
            pool.wait_ge(pair_done, PAIR_OUT)
            for i in range(NT):
                pool.dma_start(res[:, i, :], x_v[:, i, :]).then_inc(res_landed, 16)
            pool.wait_ge(turned, 2 * KT)
            pool.dma_start(fg[:, :], bass.AP(final_g.tensor, 0, [[0, P], [1, DM]])).then_inc(fg_landed, 16)

        @block.tensor
        def _(pe):
            mm = nc.tensor.matmul

            pe.wait_ge(ident_ready, 2)
            pe.wait_ge(rows_landed, 16 * 9)
            nc.tensor.transpose(acc[3][:, 0:108], rows[:, :], ident[0:108, 0:108]).then_inc(cols_turned, 1)

            def turn(src, norm, k):
                if k % NT == 0:
                    pe.wait_ge(xs_ready, NT * NT * norm + k + NT)
                if NT * norm + k >= NT:
                    pe.wait_ge(n_lo, KT * norm + k - (NT - 1))
                for i in range(NT):
                    t = nc.tensor.transpose(nbanks[k % NT][:, i * P:(i + 1) * P], src[:, i, k * P:(k + 1) * P], ident[:, :])
                t.then_inc(turned, 1)

            def turning(src, norm):
                def before(kt):
                    for k in range(kt + 3 if kt else 0, min(kt + 4, KT)):
                        turn(src, norm, k)
                    pe.wait_ge(n_lo, KT * norm + kt + 1)
                return before

            def tile(slot, i, a_hi, a_lo, a, natural, first, last, done, job, width=COLS):
                wh, wl = w_hi[slot], w_lo[slot]
                for b in range(4):
                    if first and not (isinstance(job, int) and job == 0):
                        pe.wait_ge(acc_free[b], job)
                    bl = slice(b * P, (b + 1) * P)
                    for n, (w, h) in enumerate(((wl, a_hi), (wh, a_lo), (wh, a_hi))):
                        lhs, rhs = (h[:, a, bl], w[:, i, :]) if natural else (w[:, i, bl], h[:, a, :])
                        t = mm(acc[b][:, :], lhs, rhs, start=first and n == 0, stop=last and n == 2)
                    if last and b < 3:
                        t.then_inc(acc_done, 1)
                if done:
                    t.then_inc(pair_done, 1)

            def job(pair, number, a_hi, a_lo, natural, k0=0, k1=PAIRS, before=None, a0=0):
                for k in range(k0, k1):
                    pe.wait_ge(lo_ready, pair + (k - k0 + 1))
                    for i in range(2):
                        if before:
                            before(2 * k + i)
                        tile(k % HL, i, a_hi, a_lo, a0 + 2 * k + i, natural, k == k0 and i == 0,
                             k == k1 - 1 and i == 1, i == 1, number)

            pe.wait_ge(cols_ready, 1)
            job(0, 0, h_hi, h_lo, False, before=turning(x_s, 0))
            with pe.Fori(1, T_JOBS) as j:
                job(j * PAIRS, j, h_hi, h_lo, False)
            pe.wait_ge(wg_lo_ready, 1)
            for k in range(KT):
                for n, (w, h) in enumerate(((wg_lo, h_hi), (wg_hi, h_lo), (wg_hi, h_hi))):
                    t = mm(e[0][:, :], w[:, k, :], h[:, k, :], start=k == 0 and n == 0, stop=k == KT - 1 and n == 2)
            t.then_inc(gn_done, 1)

            pe.wait_ge(tab_landed, 16)
            pe.wait_ge(tab_masked, 1)
            pe.wait_ge(oh_landed, 16)
            for n in range(4):
                w = min(512, ROW - 512 * n)
                if n == 3:
                    pe.wait_ge(brow_ready, 1)
                mm(bbanks[n][0:NH + DH, 0:w], tab[:, :], oh[:, 512 * n:512 * n + w], start=True, stop=True).then_inc(brow_done, 1)

            with pe.Fori(0, N_JOBS) as j:
                job(j * PAIRS + PAIR_N, j + JOB_N, h_hi, h_lo, True)

            pe.wait_ge(gates_t_ready, 1)
            for i in range(NT):
                t = nc.tensor.transpose(e[0][:, i * GN:(i + 1) * GN], gates_t[:, i * P:(i + 1) * P], ident[0:GN, 0:GN])
            t.then_inc(gates_turned, 1)
            pe.wait_ge(ones_ready, 1)
            pe.wait_ge(lprod_ready, 2)
            pe.wait_ge(brow_ready, 4)
            mm(e[1][:, 0:2], ones[:, :], lprod[:, :], start=True, stop=True).then_inc(lam_sum, 1)

            for s in range(2):
                pe.wait_ge(blk_lo_ready, s + 1)
                pe.wait_ge(acc_free[2 * s], JOB_C)
                for k in range(PAIRS):
                    pe.wait_ge(lo_ready, PAIR_C + PAIRS * s + k + 1)
                    wh = w_hi[k % HL][:, :, :].rearrange("p a (b n) -> p (a b) n", b=2)
                    wl = w_lo[k % HL][:, :, :].rearrange("p a (b n) -> p (a b) n", b=2)
                    for jj in range(4):
                        j = 4 * k + jj
                        for n, w in enumerate((wl, wh)):
                            t = mm(acc[2 * s][:, 0:CH], blk_hl[:, s, j, :], w[:, jj, :],
                                   start=j == 0 and n == 0, stop=j == CL - 1 and n == 1)
                    t.then_inc(pair_done, 1)
            pe.wait_ge(twice_ready, 1)
            for s in range(2):
                pe.wait_ge(acc_free[2 * s], JOB_C + 1)
                pe.wait_ge(acc_free[2 * s + 1], JOB_C)
                for u in range(2):
                    t = mm(acc[2 * s + 1][:, u * NG * NC_:(u + 1) * NG * NC_], hid_hl[:, s, u * P:(u + 1) * P], twice[:, :],
                           start=True, stop=True)
                t.then_inc(hid_done, 1)
            pe.wait_ge(w2_landed, 16)
            pe.wait_ge(acc_free[1], JOB_C + 1)
            pe.wait_ge(gates_ready, 1)
            for u in range(2):
                t = mm(e[0][:, 0:NG * NC_], w2[:, 0, u, :], hid[:, 0, u, :], start=u == 0, stop=u == 1)
            t.then_inc(kvc_done, 1)
            pe.wait_ge(acc_free[3], JOB_C + 1)
            pe.wait_ge(lam_exp, 1)
            for g in range(NG):
                for u in range(2):
                    t = mm(e[1][0:NC_, g * HD:(g + 1) * HD], hid[:, 1, u, g * NC_:(g + 1) * NC_], w2[:, 1, u, :],
                           start=u == 0, stop=u == 1)
            t.then_inc(kvc_done, 1)
            pe.wait_ge(kvc_ready, 2)

            with pe.Fori(0, ITERS) as t:
                def scores(u):
                    q, k = (q2, k2) if u < 4 else (qd, kd)
                    qs, ks = (u // 2, u % 2) if u < 4 else (u - 4, u - 4)
                    if u == 0:
                        pe.wait_ge(nsa_loaded, 16 * 7 * (t + 1))
                        pe.wait_ge(cur_ready, 4 * t + 4)
                    if u == 4:
                        pe.wait_ge(diff_loaded, 16 * 4 * (t + 1))
                    if u == 5:
                        pe.wait_ge(z_ready, 24 * t + 20)
                    for i in ORDER:
                        b, c = SEG[i]
                        n = (i + 1) * P
                        s = mm(e[b][:, c:c + n], q[:, qs, i * P:(i + 1) * P], k[:, ks, 0:n], start=True, stop=True)
                        if i == 1 and u in (0, 2):
                            for j in range(NT):
                                c = CSEG + j * NC_
                                mm(e[1][:, c:c + NC_], q[:, qs, j * P:(j + 1) * P], kcur[:, :], start=True, stop=False)
                                s = mm(e[1][:, c:c + NC_], cbias[:, qs, j * P:(j + 1) * P], ident[0:NC_, 0:NC_],
                                       start=False, stop=True)
                        if i > 0:
                            s.then_inc(scores_done, 1)

                def transposes(u):
                    p = p_a if u < 4 else p_b
                    pe.wait_ge(p_scaled, 20 * t + 4 * (u + 1))
                    for kt in (0, 1, 3, 2):
                        b, c = TSEG[kt]
                        for i in range(kt, NT):
                            s = nc.tensor.transpose(e[b][:, c + (i - kt) * P:c + (i - kt + 1) * P],
                                                    p[:, ZOFF[i] + kt * P:ZOFF[i] + (kt + 1) * P], ident[:, :])
                        if kt != 1:
                            s.then_inc(pt_done, 1)
                    if u in (0, 2):
                        if u == 2:
                            pe.wait_ge(o_lo_ready, 4 * t + 1)
                        pe.wait_ge(pc_scaled, 2 * t + (1 + u // 2))
                        for i in range(NT):
                            s = mm(ob[0:NC_, i * P:(i + 1) * P], pc[:, i, :], ident[:, :], start=True, stop=True)
                        s.then_inc(pt_done, 1)

                def values(u):
                    pe.wait_ge(pt_ready, 17 * t + U_PT[u + 1])
                    if u < 4:
                        if u % 2 == 0:
                            mm(ob[:, :], vcur[:, :], pct[:, :], start=True, stop=False)
                        for kt in range(NT):
                            b, c = TSEG[kt]
                            n = (NT - kt) * P
                            s = mm(ob[:, kt * P:S], v2[:, kt, u % 2, :], pt[:, 512 * b + c:512 * b + c + n],
                                   start=False, stop=u % 2 == 1 and kt == NT - 1)
                    else:
                        pe.wait_ge(o_lo_ready, 4 * t + 2)
                        for i in range(NT):
                            o, c = (ob, i * DV) if i < 2 else (e[0], (i - 2) * DV)
                            for kt in range(i + 1):
                                b, c0 = TSEG[kt]
                                c1 = 512 * b + c0 + (i - kt) * P
                                s = mm(o[:, c:c + DV], pt[:, c1:c1 + P], vd[:, kt, :], start=kt == 0, stop=kt == i)
                    s.then_inc(pv_done, 1)

                def turn_o(_):
                    pe.wait_ge(on_scaled, t + 1)
                    for h in range(2):
                        for i in range(NT):
                            s = nc.tensor.transpose(e[1 + h][:, i * P:(i + 1) * P], on[:, i, h * P:(h + 1) * P], ident[:, :])
                        s.then_inc(ot_done, 1)

                def pieces(first):
                    def before(tile):
                        for kind, u in AT.get(first + tile, ()):
                            {"S": scores, "T": transposes, "V": values, "O": turn_o}[kind](u)
                    return before

                for n in range(2):
                    job(t * (2 * PAIRS) + (PAIR_G + n * PAIRS), 2 * t + (JOB_G + n), h_hi, h_lo, False, before=pieces(16 * n))
                pe.wait_ge(o_lo_ready, 4 * t + 4)

            def up(c, landed):
                for n in range(2):
                    k0 = 4 * n
                    for k in range(k0, k0 + 4):
                        pe.wait_ge(lo_ready, c * PAIRS + (PAIR_UP + k + 1))
                        if landed:
                            pe.wait_ge(o_landed[k], 32)
                        for i in range(2):
                            tile(k % HL, i, o_hi, o_lo, 2 * k + i, False, k == k0 and i == 0, k == k0 + 3 and i == 1,
                                 i == 1, 2 * c + (JOB_UP + n))
            up(0, True)
            with pe.Fori(1, NT) as c:
                up(c, False)

            with pe.Fori(0, NT) as c:
                job(c * PAIRS + PAIR_OUT, c + JOB_OUT, m_hi, m_lo, True,
                    before=lambda k: pe.wait_ge(mix_lo, k + 1))

            def ff_out(pair, number, c):
                pe.wait_ge(f_lo_ready, 4 * (c + 1))
                for n in range(NT):
                    for k in range(2):
                        pe.wait_ge(lo_ready, pair + (2 * n + k + 1))
                        for i in range(2):
                            tile((2 * n + k) % HL, i, f_hi, f_lo, 2 * k + i, True, k == 0 and i == 0,
                                 k == 1 and i == 1, i == 1, number + n)

            FJ = JOB_FF
            job(PAIR_FF, FJ, h2_hi, h2_lo, False, before=turning(res_s, 1))
            with pe.Fori(0, CHUNKS - 1) as c:
                job(c * FF_PAIRS + (PAIR_FF + PAIRS), c * FF_JOBS + (FJ + 1), h2_hi, h2_lo, False)
                job(c * FF_PAIRS + (PAIR_FF + 2 * PAIRS), c * FF_JOBS + (FJ + 2), h2_hi, h2_lo, False)
                ff_out(c * FF_PAIRS + (PAIR_FF + 3 * PAIRS), c * FF_JOBS + (FJ + 3), c)
            last = FJ + (CHUNKS - 1) * FF_JOBS
            job(PAIR_END - 2 * PAIRS, last + 1, h2_hi, h2_lo, False)
            ff_out(PAIR_END - PAIRS, last + 2, CHUNKS - 1)

        @block.scalar
        def _(act):
            A = nc.scalar.activation

            act.dma_start(rows[0:16, :], mix_g.rearrange("(k p) -> k p", p=P)).then_inc(rows_landed, 16)
            act.dma_start(rows[16:32, :], ff_g.rearrange("(k p) -> k p", p=P)).then_inc(rows_landed, 16)
            act.dma_start(rows[32:40, :], head_g.rearrange("h (k p) -> (h k) p", p=P)).then_inc(rows_landed, 16)
            for n, v in enumerate((lq1, lk1, lq2, lk2)):
                act.dma_start(rows[40 + n:41 + n, :], v.rearrange("(a p) -> a p", a=1)).then_inc(rows_landed, 16)
            act.dma_start(rows[44:76, :], pe_k).then_inc(rows_landed, 16)
            act.dma_start(rows[76:108, :], pe_v).then_inc(rows_landed, 16)

            def norm_hi(norm, ks, g0, dst):
                for k in ks:
                    act.wait_ge(turned, KT * norm + k + 1)
                    A(dst[:, k, :], nbanks[k % NT][:, :], ACT.Copy, scale=cols[:, g0 + k:g0 + k + 1]).then_inc(n_hi, 1)

            def evacuate(done, spill):
                for b in (0, 2):
                    if not isinstance(spill, int) or spill > 0:
                        act.wait_ge(spilled[b], 16 * spill)
                    act.wait_ge(acc_done, 3 * done + (b + 1))
                    A(stage[b][:, :], acc[b][:, :], ACT.Copy).then_inc(acc_free[b], 1)

            def sweep(first, uses, ks=range(AHEAD, PAIRS + AHEAD)):
                for k in ks:
                    a = k % PAIRS
                    act.wait_ge(w_landed[a % RAW], 16 * (uses + (k // RAW + 1)))
                    if not isinstance(first, int) or first + k >= HL:
                        act.wait_ge(pair_done, first + (k - HL + 1))
                    A(w_hi[a % HL][:, :, :], raw[a % RAW][:, :, :], ACT.Copy).then_inc(hi_ready, 1)
                    yield k - AHEAD

            def run(first, uses, ks=range(AHEAD, PAIRS + AHEAD)):
                for _ in sweep(first, uses, ks):
                    pass

            def norm_job(first, uses, norm, g0, dst):
                norm_hi(norm, (0, 1), g0, dst)
                for k in sweep(first, uses):
                    norm_hi(norm, (2 * k + 2, 2 * k + 3) if k < PAIRS - 1 else (), g0, dst)

            for i in range(NT):
                act.wait_ge(x_landed[i], 16)
                A(x_s[:, i, :], x_in[:, i, :], ACT.Square, accum_out=ss[:, i:i + 1]).then_inc(sq_ready, 1)
            run(0, 0, range(AHEAD))
            act.wait_ge(ms_ready, 1)
            A(rstd[:, :], ms[:, :], ACT.Sqrt).then_inc(rstd_ready, 1)
            act.wait_ge(cols_ready, 1)
            norm_job(0, 0, 0, 0, h_hi)
            evacuate(0, 0)
            with act.Fori(1, T_JOBS) as j:
                run(j * PAIRS, 2 * j)
                evacuate(j, j)
            act.wait_ge(wg_landed, 16)
            act.wait_ge(xs_ready, NT * NT)
            A(wg_hi[:, :, 0:GN], wg[:, :, :], ACT.Copy).then_inc(wg_hi_ready, 1)
            for j in range(N_JOBS):
                for k in sweep(j * PAIRS + PAIR_N, 2 * j + PAIR_N // RAW):
                    if j == 0 and k == 4:
                        act.wait_ge(gn_done, 1)
                        A(gates_t[:, :], e[0][0:GN, :], ACT.Sigmoid).then_inc(gates_t_ready, 1)
                    if j > 0 and k == 4:
                        act.wait_ge(blk_ready, 6 * j)
                        A(blk_hl[:, j - 1, :, 0:NG * NC_], blk[:, j - 1, :, :], ACT.Copy).then_inc(blk_hi_ready, 1)
                evacuate(j + JOB_N, j + JOB_N)
            act.wait_ge(lam_sum, 1)
            A(lexp[:, :], e[1][:, 0:2], ACT.Exp).then_inc(lam_exp, 1)
            run(PAIR_C, PAIR_C // RAW)
            run(PAIR_C + PAIRS, (PAIR_C + PAIRS) // RAW)
            for s in range(2):
                act.wait_ge(hid_done, s + 1)
                A(hid[:, s, :, :], acc[2 * s + 1][:, 0:2 * NG * NC_].rearrange("p (u n) -> p u n", u=2), ACT.Gelu_apprx_tanh)\
                    .then_inc(acc_free[2 * s + 1], 1)
            act.wait_ge(kvc_done, 1)
            A(kct[:, :], e[0][:, 0:NG * NC_], ACT.Copy).then_inc(kvc_ready, 1)

            with act.Fori(0, ITERS) as t:
                def exps(u):
                    p, l = (p_a, l1) if u < 5 else (p_b, l2)
                    for n, i in enumerate(ORDER):
                        act.wait_ge(z_ready, 24 * t + (4 * u + n + 1))
                        n = (i + 1) * P
                        A(p[:, ZOFF[i]:ZOFF[i] + n], z[:, ZOFF[i]:ZOFF[i] + n], ACT.Exp, bias=m[:, i:i + 1],
                          scale=-1.0, accum_out=l[:, i:i + 1]).then_inc(p_exp, 1)
                    if u in (0, 2):
                        act.wait_ge(zc_ready, 2 * t + (1 + u // 2))
                        A(pc[:, :, :], zc[:, :, :], ACT.Exp, scale=SCALE).then_inc(pc_exp, 1)

                def move_pt(u):
                    act.wait_ge(pt_done, 17 * t + (U_PT[u] + 2))
                    A(pt[:, 512:1024], e[1][:, :], ACT.Copy).then_inc(pt_ready, 1)
                    if u in (0, 2):
                        act.wait_ge(pt_done, 17 * t + (U_PT[u] + 4))
                        A(pct[:, :], ob[0:NC_, :], ACT.Copy).then_inc(pt_ready, 1)

                def outputs(u):
                    if u in (1, 3):
                        act.wait_ge(pv_done, 5 * t + (u + 1))
                        A(s_hi[u // 2][:, :], ob[:, :], ACT.Copy).then_inc(o_hi_ready, 1)
                    if u == 4:
                        act.wait_ge(on_ready, 2 * t + 2)
                        for i in range(NT):
                            A(z[:, 0:DV], on[:, i, :], ACT.Square, accum_out=ss[:, i:i + 1]).then_inc(on_sq, 1)
                            act.wait_ge(on_sq, 4 * t + (i + 1))
                        act.wait_ge(on_ms, t + 1)
                        A(rstd[:, :], ms[:, :], ACT.Sqrt).then_inc(on_rstd, 1)

                def turned_o(_):
                    for h in range(2):
                        act.wait_ge(ot_done, 2 * t + (h + 1))
                        A(s_hi[2 + h][:, :], e[1 + h][:, :], ACT.Copy, scale=hgcur[:, h:h + 1]).then_inc(o_hi_ready, 1)

                for n in range(2):
                    for k in sweep(t * (2 * PAIRS) + (PAIR_G + n * PAIRS), 4 * t + (PAIR_G // RAW + 2 * n)):
                        for i in range(2):
                            for kind, u in AT.get(16 * n + 2 * k + i, ()):
                                {"S": exps, "T": move_pt, "V": outputs, "O": turned_o}[kind](u)
                    evacuate(2 * t + (JOB_G + n - 1), 2 * t + (T_JOBS + N_JOBS + n))
                for k in range(4):
                    act.wait_ge(o_spilled[k], 32 * (t + 1))

            def up(c):
                for k in sweep(c * PAIRS + PAIR_UP, 2 * c + PAIR_UP // RAW):
                    if k in (2, 3):
                        act.wait_ge(g_landed[k - 2], 16 * (c + 1))
                        t = (ga, gb)[k - 2]
                        A(t[:, :, :], t[:, :, :], ACT.Sigmoid).then_inc(sig_ready, 1)
                for b in range(4):
                    act.wait_ge(mix_sum, 4 * c + (b + 1))
                    A(m_hi[:, bass.ds(4 * c + b, 1), :], gb[:, b:b + 1, :], ACT.Copy).then_inc(mix_hi, 1)
            with act.Fori(0, NT) as c:
                up(c)
            with act.Fori(0, NT) as c:
                run(c * PAIRS + PAIR_OUT, 2 * c + PAIR_OUT // RAW)
                for b in range(NT):
                    act.wait_ge(acc_free[b], c + (JOB_OUT + 1))
                    A(ga[:, b, :], res[:, b, bass.ds(c * COLS, COLS)], ACT.Square,
                      accum_out=ssp[:, b, bass.ds(c, 1)]).then_inc(sq_ready, 1)
            act.wait_ge(ms_ready, 2)
            A(rstd[:, :], ms[:, :], ACT.Sqrt).then_inc(rstd_ready, 1)

            FD = JOB_FF - 1

            def silus(done, pair_end):
                for b in range(4):
                    if b < 3:
                        act.wait_ge(acc_done, 3 * done + (b + 1))
                    else:
                        act.wait_ge(pair_done, pair_end)
                    A(silu[:, b, :], acc[b][:, :], ACT.Silu).then_inc(acc_free[b], 1)

            def f_his(done):
                for b in range(4):
                    act.wait_ge(acc_free[b], done + (FREE_AHEAD + 1))
                    A(f_hi[:, b, :], silu[:, b, :], ACT.Copy).then_inc(f_hi_ready, 1)

            norm_job(PAIR_FF, PAIR_FF // RAW, 1, 16, h2_hi)
            silus(FD, PAIR_FF + PAIRS)
            with act.Fori(0, CHUNKS - 1) as c:
                p0 = c * FF_PAIRS + PAIR_FF
                u0 = c * (FF_PAIRS // RAW) + PAIR_FF // RAW
                run(p0 + PAIRS, u0 + 2)
                f_his(c * FF_JOBS + (FD + 1))
                run(p0 + 2 * PAIRS, u0 + 4)
                act.wait_ge(f_lo_ready, 4 * (c + 1))
                silus(c * FF_JOBS + (FD + 2), p0 + 3 * PAIRS)
                run(p0 + 3 * PAIRS, u0 + 6)
            run(PAIR_END - 2 * PAIRS, PAIR_END // RAW - 4)
            f_his(FD + 1 + (CHUNKS - 1) * FF_JOBS)
            run(PAIR_END - PAIRS, PAIR_END // RAW - 2, range(AHEAD, PAIRS))
            for i in range(NT):
                act.wait_ge(acc_free[i], JOB_FF + CHUNKS * FF_JOBS)
                A(fin_s[:, i, :], res[:, i, :], ACT.Square, accum_out=ss[:, i:i + 1]).then_inc(sq_ready, 1)
                act.wait_ge(ms_ready, i + 3)
                A(rstd[:, i:i + 1], ms[:, i:i + 1], ACT.Sqrt).then_inc(rstd_ready, 1)

        @block.vector
        def _(v):
            V = nc.vector
            chained = [0]

            def link(ins):
                chained[0] += 1
                ins.then_inc(dve, 1)
                v.wait_ge(dve, chained[0])

            V.memset(tab[BUCKETS:BUCKETS + 1, :], -MASKED).then_inc(tab_masked, 1)
            v.wait_ge(cols_turned, 1)
            V.tensor_copy(cols[:, :], acc[3][:, 0:108]).then_inc(cols_ready, 1)
            v.wait_ge(cols_ready, 1)

            def root(i0, i1, n):
                link(V.tensor_scalar(inv[:, i0:i1], ss[:, i0:i1], 1.0 / DM, EPS, ALU.mult, ALU.add))
                V.reciprocal(ms[:, i0:i1], inv[:, i0:i1]).then_inc(ms_ready, 1)
                v.wait_ge(rstd_ready, n)

            def scale(src, scaled, block):
                for i in range(NT):
                    bl = slice(block * COLS, (block + 1) * COLS)
                    V.tensor_scalar(scaled[:, i, bl], src[:, i, bl], rstd[:, i:i + 1], None, ALU.mult).then_inc(xs_ready, 1)

            def norm_lo(norm, ks, g0, hi, lo):
                for k in ks:
                    v.wait_ge(n_hi, KT * norm + k + 1)
                    V.scalar_tensor_tensor(out=lo[:, k, :], in0=nbanks[k % NT][:, :], scalar=cols[:, g0 + k:g0 + k + 1],
                                           in1=hi[:, k, :].bitcast(F32), op0=ALU.mult, op1=ALU.subtract).then_inc(n_lo, 1)

            def norm_job(first, src, scaled, norm, g0, hi, lo):
                scale(src, scaled, 0)
                norm_lo(norm, (0, 1), g0, hi, lo)
                scale(src, scaled, 1)
                for k in range(PAIRS):
                    lows(first, k)
                    norm_lo(norm, (2 * k + 2, 2 * k + 3) if k < PAIRS - 1 else (), g0, hi, lo)
                    if k in (0, 2):
                        scale(src, scaled, 2 + k // 2)

            def lows(pair, k):
                v.wait_ge(hi_ready, pair + (k + AHEAD + 1))
                s = (k + AHEAD) % HL
                V.tensor_tensor(w_lo[s][:, :, :], raw[(k + AHEAD) % RAW][:, :, :], w_hi[s][:, :, :].bitcast(F32),
                                ALU.subtract).then_inc(lo_ready, 1)

            def run(pair, end=None):
                for k in range(PAIRS):
                    if end is None or k + AHEAD < end:
                        lows(pair, k)

            def evacuate(done, pair_end, spill):
                for b in (1, 3):
                    if not isinstance(spill, int) or spill > 0:
                        v.wait_ge(spilled[b], 16 * spill)
                    if b < 3:
                        v.wait_ge(acc_done, 3 * done + (b + 1))
                    else:
                        v.wait_ge(pair_done, pair_end)
                    V.tensor_copy(stage[b][:, :], acc[b][:, :]).then_inc(acc_free[b], 1)

            for k in range(AHEAD):
                lows(0, k - AHEAD)
            v.wait_ge(sq_ready, NT)
            root(0, NT, 1)
            norm_job(0, x_in, x_s, 0, 0, h_hi, h_lo)
            evacuate(0, PAIRS, 0)
            with v.Fori(1, T_JOBS) as j:
                run(j * PAIRS)
                evacuate(j, (j + 1) * PAIRS, j)
            for n in range(2):
                V.tensor_tensor(lprod[:, n:n + 1], cols[:, 40 + 2 * n:41 + 2 * n], cols[:, 41 + 2 * n:42 + 2 * n], ALU.mult)\
                    .then_inc(lprod_ready, 1)
            V.tensor_scalar(hg[:, :], cols[:, 32:40], 1.0 - LAM_INIT, None, ALU.mult).then_inc(hg_ready, 1)
            v.wait_ge(ident_ready, 2)
            V.tensor_tensor(twice[:, :], ident[:, 0:NG * NC_], ident[:, NG * NC_:P], ALU.add).then_inc(twice_ready, 1)
            v.wait_ge(wg_hi_ready, 1)
            v.wait_ge(wg_padded, 2)
            V.tensor_tensor(wg_lo[:, :, 0:GN], wg[:, :, :], wg_hi[:, :, 0:GN].bitcast(F32), ALU.subtract).then_inc(wg_lo_ready, 1)
            for n in range(4):
                w = min(512, ROW - 512 * n)
                v.wait_ge(brow_done, n + 1)
                V.tensor_scalar(brow[:, 512 * n:512 * n + w], bbanks[n][0:NH + DH, 0:w], HD ** 0.5, None, ALU.mult)\
                    .then_inc(brow_ready, 1)

            def blocks(s):
                emb = cols[:, 44 + CL * s:44 + CL * (s + 1)]
                for g in range(NG):
                    src = c_in[:, 2 * s + g, :].rearrange("p (c j) -> p j c", j=CS)
                    c0 = g * NC_
                    V.tensor_tensor(blk[:, s, 0:CS, c0:c0 + NC_], src, emb[:, 0:CS].unsqueeze(2).to_broadcast([P, CS, NC_]),
                                    ALU.add).then_inc(blk_ready, 1)
                    V.tensor_tensor(blk[:, s, CS:CL, c0:c0 + NC_ - 1], src[:, :, 1:NC_],
                                    emb[:, CS:CL].unsqueeze(2).to_broadcast([P, CS, NC_ - 1]), ALU.add).then_inc(blk_ready, 1)
                    V.tensor_copy(blk[:, s, CS:CL, c0 + NC_ - 1:c0 + NC_], emb[:, CS:CL].unsqueeze(2)).then_inc(blk_ready, 1)

            for j in range(N_JOBS):
                for k in range(PAIRS):
                    lows(j * PAIRS + PAIR_N, k)
                    if j > 0 and k == 2:
                        if j == 1:
                            v.wait_ge(c_landed, 16)
                            v.wait_ge(gn_done, 1)
                        blocks(j - 1)
                    if j > 0 and k == 5:
                        v.wait_ge(blk_hi_ready, j)
                        V.tensor_tensor(blk_hl[:, j - 1, :, NG * NC_:P], blk[:, j - 1, :, :],
                                        blk_hl[:, j - 1, :, 0:NG * NC_].bitcast(F32), ALU.subtract).then_inc(blk_lo_ready, 1)
                evacuate(j + JOB_N, (j + 1) * PAIRS + PAIR_N, j + JOB_N)
            v.wait_ge(gates_turned, 1)
            V.tensor_copy(gates[:, :, :], e[0][:, 0:NT * GN].rearrange("p (i n) -> p i n", i=NT)).then_inc(gates_ready, 1)
            run(PAIR_C)
            v.wait_ge(lam_exp, 1)
            link(V.tensor_tensor(neglam[:, :], lexp[:, 1:2], lexp[:, 0:1], ALU.subtract))
            link(V.tensor_scalar(neglam[:, :], neglam[:, :], -LAM_INIT, None, ALU.add))
            for k in range(PAIRS):
                if k == 2:
                    v.wait_ge(pair_done, PAIR_C + PAIRS)
                    V.tensor_copy(hid_hl[:, 0, :], acc[0][:, 0:CH]).then_inc(acc_free[0], 1)
                lows(PAIR_C + PAIRS, k)
            v.wait_ge(pair_done, PAIR_C + 2 * PAIRS)
            V.tensor_copy(hid_hl[:, 1, :], acc[2][:, 0:CH]).then_inc(acc_free[2], 1)
            v.wait_ge(kvc_done, 2)
            V.tensor_copy(vc[:, :, :], e[1][0:NC_, 0:NG * HD].rearrange("p (g n) -> p g n", g=NG)).then_inc(kvc_ready, 1)
            v.wait_ge(kvc_ready, 2)
            v.wait_ge(gates_ready, 1)
            v.wait_ge(hg_ready, 1)

            with v.Fori(0, ITERS) as t:
                LINKS = 28
                count = [0]

                def then(ins):
                    count[0] += 1
                    ins.then_inc(chain, 1)
                    v.wait_ge(chain, LINKS * t + count[0])

                g = t // 2
                V.tensor_copy(kcur[:, :], kct[:, bass.ds(g * NC_, NC_)]).then_inc(cur_ready, 1)
                V.tensor_copy(vcur[:, :], vc[:, bass.ds(g, 1), :].rearrange("p g n -> p (g n)")).then_inc(cur_ready, 1)
                V.tensor_copy(gcur[:, :, :], gates[:, :, bass.ds(6 * t, 6)]).then_inc(cur_ready, 1)
                V.tensor_copy(hgcur[:, :], hg[:, bass.ds(2 * t, 2)]).then_inc(cur_ready, 1)
                v.wait_ge(cur_ready, 4 * t + 4)

                def softmax(u):
                    head = u // 2 if u < 4 else 2
                    if u == 0:
                        v.wait_ge(nsa_loaded, 16 * 7 * (t + 1))
                    if u == 4:
                        v.wait_ge(diff_loaded, 16 * 4 * (t + 1))
                    if u == 5:
                        v.wait_ge(p_exp, 24 * t + 20)
                    for i in ORDER:
                        b, c = SEG[i]
                        n = (i + 1) * P
                        v.wait_ge(scores_done, 18 * t + (3 * u + BANK_END[i])).then_inc(dve_waited, 1)
                        V.tensor_tensor_reduce(z[:, ZOFF[i]:ZOFF[i] + n], e[b][:, c:c + n], bias[:, head, S - n:S],
                                               -SCALE, 3.0e38, ALU.add, ALU.min, m[:, i:i + 1]).then_inc(z_ready, 1)
                    if u in (0, 2):
                        sc = e[1][:, CSEG:CSEG + NT * NC_].rearrange("p (i c) -> p i c", i=NT)
                        then(V.tensor_reduce(cm[:, :], sc, AX.X, ALU.max))
                        then(V.tensor_scalar(cr[:, :], cm[:, :], -FLOOR, None, ALU.max))
                        V.tensor_tensor(zc[:, :, :], sc, cr[:, :].unsqueeze(2).to_broadcast([P, NT, NC_]), ALU.subtract)\
                            .then_inc(zc_ready, 1)
                    v.wait_ge(p_exp, 24 * t + 4 * (u + 1))
                    if u < 4:
                        then(V.reciprocal(r1[:, :], l1[:, :]))
                        then(V.tensor_tensor(r2[:, :], r1[:, :], gcur[:, :, 3 * head + 1 + u % 2], ALU.mult))
                        for i in range(NT):
                            s = slice(ZOFF[i], ZOFF[i] + (i + 1) * P)
                            V.tensor_scalar(p_a[:, s], p_a[:, s], r2[:, i:i + 1], None, ALU.mult).then_inc(p_scaled, 1)
                    elif u == 5:
                        then(V.reciprocal(r1[:, :], l1[:, :]))
                        then(V.reciprocal(cr[:, :], l2[:, :]))
                        then(V.tensor_scalar(r2[:, :], cr[:, :], neglam[:, 0:1], None, ALU.mult))
                        for i in range(NT):
                            s = slice(ZOFF[i], ZOFF[i] + (i + 1) * P)
                            then(V.tensor_scalar(p_a[:, s], p_a[:, s], r1[:, i:i + 1], None, ALU.mult))
                        for i in range(NT):
                            s = slice(ZOFF[i], ZOFF[i] + (i + 1) * P)
                            V.scalar_tensor_tensor(out=p_b[:, s], in0=p_b[:, s], scalar=r2[:, i:i + 1], in1=p_a[:, s],
                                                   op0=ALU.mult, op1=ALU.add).then_inc(p_scaled, 1)
                    if u in (0, 2):
                        v.wait_ge(pc_exp, 2 * t + (1 + u // 2))
                        then(V.tensor_reduce(cl[:, :], pc[:, :, :], AX.X, ALU.add))
                        then(V.tensor_scalar(cm[:, :], cl[:, :], 1e-30, None, ALU.max))
                        then(V.reciprocal(cr[:, :], cm[:, :]))
                        then(V.tensor_tensor(cl[:, :], cr[:, :], gcur[:, :, 3 * head], ALU.mult))
                        V.tensor_tensor(pc[:, :, :], pc[:, :, :], cl[:, :].unsqueeze(2).to_broadcast([P, NT, NC_]), ALU.mult)\
                            .then_inc(pc_scaled, 1)

                def move_pt(u):
                    v.wait_ge(pt_done, 17 * t + (U_PT[u] + 1))
                    V.tensor_copy(pt[:, 0:512], e[0][:, :]).then_inc(pt_ready, 1)
                    v.wait_ge(pt_done, 17 * t + (U_PT[u] + 3))
                    V.tensor_copy(pt[:, 1024:1280], e[2][:, 0:256]).then_inc(pt_ready, 1)

                def outputs(u):
                    if u in (1, 3):
                        v.wait_ge(o_hi_ready, 4 * t + (1 + u // 2))
                        V.tensor_tensor(s_lo[u // 2][:, :], ob[:, :], s_hi[u // 2][:, :].bitcast(F32), ALU.subtract)\
                            .then_inc(o_lo_ready, 1)
                    if u == 4:
                        v.wait_ge(pv_done, 5 * t + 5)
                        for n, o in enumerate((ob, e[0])):
                            V.tensor_copy(on[:, 2 * n:2 * n + 2, :], o[:, :].rearrange("p (i n) -> p i n", i=2)).then_inc(on_ready, 1)
                        v.wait_ge(on_sq, 4 * t + 4)
                        then(V.tensor_scalar(inv[:, :], ss[:, :], 1.0 / DV, EPS, ALU.mult, ALU.add))
                        V.reciprocal(ms[:, :], inv[:, :]).then_inc(on_ms, 1)
                        v.wait_ge(on_rstd, t + 1)
                        V.tensor_tensor(on[:, :, :], on[:, :, :], rstd[:, :].unsqueeze(2).to_broadcast([P, NT, DV]), ALU.mult)\
                            .then_inc(on_scaled, 1)

                def turned_o(_):
                    for h in range(2):
                        v.wait_ge(o_hi_ready, 4 * t + (3 + h))
                        V.scalar_tensor_tensor(out=s_lo[2 + h][:, :], in0=e[1 + h][:, :], scalar=hgcur[:, h:h + 1],
                                               in1=s_hi[2 + h][:, :].bitcast(F32), op0=ALU.mult, op1=ALU.subtract)\
                            .then_inc(o_lo_ready, 1)

                for n in range(2):
                    for k in range(PAIRS):
                        lows(t * (2 * PAIRS) + (PAIR_G + n * PAIRS), k)
                        for i in range(2):
                            for kind, u in AT.get(16 * n + 2 * k + i, ()):
                                {"S": softmax, "T": move_pt, "V": outputs, "O": turned_o}[kind](u)
                    evacuate(2 * t + (JOB_G + n - 1), t * (2 * PAIRS) + (PAIR_G + (n + 1) * PAIRS), 2 * t + (T_JOBS + N_JOBS + n))
                for k in range(4):
                    v.wait_ge(o_spilled[k], 32 * (t + 1))
                assert count[0] == LINKS

            with v.Fori(0, NT) as c:
                done = 2 * c + (JOB_UP - 1)
                first = c * PAIRS + PAIR_UP
                for n in range(2):
                    for k in range(4 * n, 4 * n + 4):
                        lows(first, k)
                    for b in range(4):
                        if b < 3:
                            v.wait_ge(acc_done, 3 * done + (3 * n + b + 1))
                        else:
                            v.wait_ge(pair_done, first + 4 * (n + 1))
                        if b == 0:
                            v.wait_ge(sig_ready, 2 * c + (n + 1))
                        t = (ga, gb)[n]
                        V.tensor_tensor(t[:, b, :], acc[b][:, :], t[:, b, :], ALU.mult).then_inc(acc_free[b], 1)
                for b in range(4):
                    v.wait_ge(acc_free[b], 2 * c + (JOB_UP + 2))
                    V.tensor_tensor(gb[:, b, :], ga[:, b, :], gb[:, b, :], ALU.add).then_inc(mix_sum, 1)
                for b in range(4):
                    v.wait_ge(mix_hi, 4 * c + (b + 1))
                    V.tensor_tensor(m_lo[:, bass.ds(4 * c + b, 1), :], gb[:, b:b + 1, :],
                                    m_hi[:, bass.ds(4 * c + b, 1), :].bitcast(F32), ALU.subtract).then_inc(mix_lo, 1)

            with v.Fori(0, NT) as c:
                run(c * PAIRS + PAIR_OUT)
                for b in range(4):
                    if b < 3:
                        v.wait_ge(acc_done, 3 * c + (3 * (JOB_OUT - 1) + b + 1))
                    else:
                        v.wait_ge(pair_done, (c + 1) * PAIRS + PAIR_OUT)
                    if b == 0:
                        v.wait_ge(res_landed, 16 * NT)
                    r = res[:, b, bass.ds(c * COLS, COLS)]
                    V.tensor_tensor(r, acc[b][:, :], r, ALU.add).then_inc(acc_free[b], 1)

            v.wait_ge(sq_ready, NT + NT * NT)
            link(V.tensor_reduce(ss[:, :], ssp[:, :, :], AX.X, ALU.add))
            root(0, NT, 2)
            FD = JOB_FF - 1

            def take_b(done, pair_end, c):
                for b in range(4):
                    if b < 3:
                        v.wait_ge(acc_done, 3 * done + (b + 1))
                    else:
                        v.wait_ge(pair_done, pair_end)
                    v.wait_ge(acc_free[b], done + FREE_AHEAD)
                    V.tensor_tensor(silu[:, b, :], acc[b][:, :], silu[:, b, :], ALU.mult).then_inc(acc_free[b], 1)
                for b in range(4):
                    v.wait_ge(f_hi_ready, 4 * c + (b + 1))
                    V.tensor_tensor(f_lo[:, b, :], silu[:, b, :], f_hi[:, b, :].bitcast(F32), ALU.subtract).then_inc(f_lo_ready, 1)

            def add_out(done, pair_end, n):
                for b in range(4):
                    if b < 3:
                        v.wait_ge(acc_done, 3 * done + (b + 1))
                    else:
                        v.wait_ge(pair_done, pair_end)
                    r = res[:, b, n * COLS:(n + 1) * COLS]
                    V.tensor_tensor(r, acc[b][:, :], r, ALU.add).then_inc(acc_free[b], 1)

            def outs(first, done):
                for n in range(NT):
                    for k in range(2):
                        yield 2 * n + k
                    add_out(done + n, first + 2 * (n + 1), n)

            norm_job(PAIR_FF, res, res_s, 1, 16, h2_hi, h2_lo)
            with v.Fori(0, CHUNKS - 1) as c:
                p0 = c * FF_PAIRS + PAIR_FF
                run(p0 + PAIRS)
                take_b(c * FF_JOBS + (FD + 1), p0 + 2 * PAIRS, c)
                run(p0 + 2 * PAIRS)
                for k in outs(p0 + 3 * PAIRS, c * FF_JOBS + (FD + 3)):
                    lows(p0 + 3 * PAIRS, k)
            last = FD + (CHUNKS - 1) * FF_JOBS
            run(PAIR_END - 2 * PAIRS)
            take_b(last + 1, PAIR_END - PAIRS, CHUNKS - 1)
            for k in outs(PAIR_END - PAIRS, last + 2):
                if k + AHEAD < PAIRS:
                    lows(PAIR_END - PAIRS, k)

            v.wait_ge(fg_landed, 16)
            for i in range(NT):
                v.wait_ge(sq_ready, NT + NT * NT + i + 1)
                root(i, i + 1, 3 + i)
                V.scalar_tensor_tensor(out=fin[:, i, :], in0=res[:, i, :], scalar=rstd[:, i:i + 1], in1=fg[:, :],
                                       op0=ALU.mult, op1=ALU.mult).then_inc(fin_ready, 1)


def kernel(**inputs):
    import concourse.bacc as bacc
    from concourse.bass_utils import run_bass_kernel_spmd

    a = {k: np.ascontiguousarray(v) for k, v in inputs.items()}
    w = a["w_in"][0]
    widths = [1024, 256, 256, 256, 256, 256, 256, 24, 1024, 1024, 1024, 4096]
    q_n, kc, vc, ksl, vsl, kw, vw, g_n, q_d, k_d, v_d, g_m = np.split(w, np.cumsum(widths)[:-1], axis=1)
    arrays = {
        "x": a["x"][0],
        "w_proj": np.concatenate([q_n, kc, vc, ksl, kw, q_d, k_d, g_m, vsl, vw, v_d, g_n], axis=1),
        "pe_k": a["cmp_pe_k"][0], "pe_v": a["cmp_pe_v"][0],
        "cw1": np.concatenate([a["cmp_w1_k"], a["cmp_w1_v"]], axis=0),
        "cw2": np.concatenate([a["cmp_w2_k"], a["cmp_w2_v"]], axis=0),
        "lq1": a["diff_lq1"][0], "lk1": a["diff_lk1"][0], "lq2": a["diff_lq2"][0], "lk2": a["diff_lk2"][0],
        "head_g": a["diff_head_g"][0], "mix_g": a["norm_mix_g"][0], "ff_g": a["norm_ff_g"][0],
        "final_g": a["norm_final_g"],
        "w_up": np.concatenate([a["w_up_nsa"][0], a["w_up_diff"][0]], axis=0),
        "w_out": a["w_out"][0], "w_ff_in": a["w_ff_in"][0], "w_ff_out": a["w_ff_out"][0],
        "table": a["rel_bias_table"], "onehot": bucket_onehot(),
    }
    nc = bacc.Bacc("TRN2", target_bir_lowering=False, num_devices=1)
    args = {}
    feed = {}
    for name, v in arrays.items():
        v = np.ascontiguousarray(v)
        feed[f"in_{name}"] = v
        args[name] = nc.dram_tensor(f"in_{name}", v.shape, mybir.dt.from_np(v.dtype), kind="ExternalInput").ap()
    out = nc.dram_tensor("out_0", (S, DM), F32, kind="ExternalOutput").ap()
    build(nc, **args, out=out)
    r = run_bass_kernel_spmd(nc, [feed], core_ids=[0])
    return r.results[0]["out_0"].reshape(1, S, DM)
```

```python
import math
from contextlib import ExitStack

import numpy as np

import concourse.bass as bass
from concourse import mybir

F32 = mybir.dt.float32
F32R = mybir.dt.float32r
ALU = mybir.AluOpType
ACT = mybir.ActivationFunctionType
AX = mybir.AxisListType

P = 128
S = 512
DM = 2048
HD = 128
NT = S // P
KT = DM // P
NH, NG, DH = 8, 2, 4
DV = 2 * HD
CL, CS = 32, 16
NC_ = S // CS
CH = 256
DFF = 5632
BUCKETS, MAX_EXACT, MAX_DIST = 32, 16, 128
EPS = 1e-6
SCALE = HD ** -0.5
LAM_INIT = 0.8 - 0.6 * math.exp(0.0)
MASKED = 1e30
FLOOR = 1e29
COLS = 512
PAIRS = KT // 2
RAW = 4
HL = 4
AHEAD = 2

T_JOBS = 8
G_JOBS = 8
N_JOBS = 3
N_COL0 = (T_JOBS + G_JOBS) * COLS
GN_COL0 = N_COL0 + N_JOBS * COLS
GN = 3 * NH
C_TILE, K_TILE, QD_TILE, KD_TILE, G_TILE = 8, 12, 16, 24, 32
REV = 640
FWD = 1024
FWD0 = S + CL // 2 - 1
ROW = REV + FWD
FF_CHUNK = 4
CHUNKS = DFF // (FF_CHUNK * P)
FF_PAIRS = 3 * PAIRS
PAIR_N = T_JOBS * PAIRS
PAIR_G = PAIR_N + N_JOBS * PAIRS + 2 * PAIRS
PAIR_UP = PAIR_G + G_JOBS * PAIRS
PAIR_OUT = PAIR_UP + NT * PAIRS
PAIR_FF = PAIR_OUT + NT * PAIRS
PAIR_END = PAIR_FF + CHUNKS * FF_PAIRS
JOB_N = T_JOBS
JOB_G = JOB_N + N_JOBS
JOB_UP = JOB_G + G_JOBS
JOB_OUT = JOB_UP + 2 * NT
JOB_FF = JOB_OUT + NT
FF_JOBS = 6
NAT = []
for _j in range(N_JOBS):
    for _k in range(PAIRS):
        NAT.append(("N", _j, _k))
        if _j == 1:
            NAT.append(("C", 0, _k))
        if _j == 2 and _k < PAIRS // 2:
            NAT += [("C", 1, 2 * _k), ("C", 1, 2 * _k + 1)]
C_END = [PAIR_N + NAT.index(("C", _s, PAIRS - 1)) + 1 for _s in range(2)]
ITERS = DH
ORDER = (0, 2, 1, 3)
BANK_END = {0: 1, 2: 1, 1: 2, 3: 3}
U_PT = (0, 4, 7, 11, 14, 17)
AT = {3: [("S", 0)], 6: [("T", 0)], 7: [("V", 0), ("S", 1)], 10: [("T", 1)], 11: [("V", 1), ("S", 2)],
      14: [("T", 2)], 15: [("V", 2)], 16: [("S", 3)], 19: [("T", 3)], 20: [("V", 3), ("S", 4)],
      22: [("S", 5)], 26: [("T", 4)], 27: [("V", 4)], 30: [("O", 0)]}


def bucket_onehot():
    n = np.arange(S)
    large = MAX_EXACT + (np.log(np.maximum(n, 1) / MAX_EXACT) / math.log(MAX_DIST / MAX_EXACT)
                         * (BUCKETS - MAX_EXACT)).astype(np.int32)
    bucket = np.where(n < MAX_EXACT, n, np.minimum(large, BUCKETS - 1))
    rel = np.concatenate([S - 1 - np.arange(REV), np.arange(FWD) - FWD0])
    row = np.where((rel < 0) | (rel >= S), BUCKETS, bucket[np.clip(rel, 0, S - 1)])
    return (np.arange(BUCKETS + 1)[:, None] == row[None, :]).astype(np.float32)


def build(nc, x, w_proj, vectors, cw1, cw2, final_g,
          w_up, w_out, w_ff_in, w_ff_out, table, onehot, out):
    ctx = ExitStack()
    with ctx:
        proj_t = nc.dram_tensor("proj_t", [(T_JOBS + G_JOBS) * NT, P, S], F32).ap()
        proj_n = nc.dram_tensor("proj_n", [NT, P, N_JOBS * COLS], F32).ap()
        o_hi_d = nc.dram_tensor("o_hi_d", [KT, P, S], F32).ap()
        o_lo_d = nc.dram_tensor("o_lo_d", [KT, P, S], F32).ap()
        bias_d = nc.dram_tensor("bias_d", [NH + DH, ROW], F32).ap()

        skew_d = nc.dram_tensor("skew_d", [NH + DH, P * (REV + 1)], F32).ap()
        cskew_d = nc.dram_tensor("cskew_d", [NH, NC_ * (FWD + CS)], F32).ap()
        skew_w = skew_d.rearrange("h (p r) -> h p r", p=P)
        cskew_w = cskew_d.rearrange("h (c r) -> h c r", c=NC_)
        skew_r = skew_d[:, 0:P * REV].rearrange("h (p r) -> h p r", p=P)
        cskew_r = cskew_d[:, 0:NC_ * FWD].rearrange("h (c r) -> h c r", c=NC_)

        base = (nc.sbuf_base + 63) // 64 * 64
        KB = 1024
        R1, R2 = base, base + 64 * KB
        RING = base + 128 * KB
        MISC = RING + 48 * KB

        def at(name, shape, offset, dt=F32):
            return nc.alloc_sbuf_tensor_at(name, shape, dt, offset=offset)

        h_hi = at("h_hi", [P, KT, S], R1, F32R)
        h_lo = at("h_lo", [P, KT, S], R1 + 32 * KB, F32R)
        o_hi = at("o_hi", [P, KT, S], R1, F32R)
        o_lo = at("o_lo", [P, KT, S], R1 + 32 * KB, F32R)
        res = at("res", [P, NT, DM], R1)
        silu = at("silu", [P, FF_CHUNK, S], R1 + 32 * KB)
        f_hi = at("f_hi", [P, FF_CHUNK, S], R1 + 40 * KB, F32R)
        f_lo = at("f_lo", [P, FF_CHUNK, S], R1 + 48 * KB, F32R)
        diag2 = at("diag2", [P, NT, P], R1 + 40 * KB)
        fg = at("fg", [P, DM], R1 + 56 * KB)
        x_in = at("x_in", [P, NT, DM], R2)
        x_sq = at("x_sq", [P, NT, DM], R2 + 32 * KB)
        diag1 = at("diag1", [P, NT, P], R2 + 32 * KB)
        m_hi = at("m_hi", [P, KT, S], R2, F32R)
        m_lo = at("m_lo", [P, KT, S], R2 + 32 * KB, F32R)
        h2_hi = at("h2_hi", [P, KT, S], R2, F32R)
        h2_lo = at("h2_lo", [P, KT, S], R2 + 32 * KB, F32R)

        def last_w(half, k):
            return (h2_hi, h2_lo)[half][:, 2 * k:2 * k + 2, :]

        c_in = at("c_in", [P, 4, S], R2)
        blk = at("blk", [P, 2, CL, NG * NC_], R2 + 8 * KB)
        blk_hl = at("blk_hl", [P, 2, CL, 2 * NG * NC_], R2 + 24 * KB, F32R)
        hid = at("hid", [P, 2, 2, NG * NC_], R2 + 56 * KB)
        w2 = at("w2", [P, 2, 2, HD], R2 + 57 * KB)
        hid_hl = at("hid_hl", [P, 2, CH], R2 + 59 * KB)
        gates_t = at("gates_t", [P, S], R2 + 61 * KB)
        wg_hl = at("wg_hl", [P, KT, 2, P // 2], R2 + 8 * KB, F32R)
        q2 = at("q2", [P, 2, S], R2)
        k2 = at("k2", [P, 2, S], R2 + 4 * KB)
        v2 = at("v2", [P, NT, 2, HD], R2 + 8 * KB)
        qd = at("qd", [P, 2, S], R2 + 12 * KB)
        kd = at("kd", [P, 2, S], R2 + 16 * KB)
        vd = at("vd", [P, NT, DV], R2 + 20 * KB)
        bias = at("bias", [P, 3, S], R2 + 24 * KB)
        cbias = at("cbias", [NC_, 2, S], R2 + 30 * KB)
        z = at("z", [P, 1280], R2 + 34 * KB)
        p_a = at("p_a", [P, 1280], R2 + 39 * KB)
        p_b = at("p_b", [P, 1280], R2 + 44 * KB)
        pt = at("pt", [P, 1280], R2 + 49 * KB)
        zc = at("zc", [P, NT, NC_], R2 + 54 * KB)
        pc = at("pc", [P, NT, NC_], R2 + 54 * KB + 512)
        pct = at("pct", [NC_, S], R2 + 55 * KB)
        on = at("on", [P, NT, DV], R2 + 57 * KB)
        raw = [at(f"raw{s}", [P, 2, COLS], RING + 4 * KB * s) for s in range(RAW)]
        w_hi = [at(f"w_hi{s}", [P, 2, COLS], RING + 16 * KB + 4 * KB * s, F32R) for s in range(HL)]
        w_lo = [at(f"w_lo{s}", [P, 2, COLS], RING + 32 * KB + 4 * KB * s, F32R) for s in range(HL)]
        stage = [at(f"stage{b}", [P, S], MISC + 2 * KB * b) for b in range(4)]
        oh = at("oh", [BUCKETS + 1, ROW], MISC + 8 * KB)
        brow = at("brow", [NH + DH, ROW], MISC + 15 * KB)
        s_hi = [at(f"s_hi{k}", [P, S], MISC + 8 * KB + 2 * KB * k, F32R) for k in range(4)]
        s_lo = [at(f"s_lo{k}", [P, S], MISC + 16 * KB + 2 * KB * k, F32R) for k in range(4)]
        ga = at("ga", [P, NT, S], MISC + 8 * KB)
        gb = at("gb", [P, NT, S], MISC + 16 * KB)
        top = [MISC + 24 * KB]

        def small(name, shape, dt=F32):
            n = int(np.prod(shape[1:])) * 4
            t = at(name, shape, top[0], dt)
            top[0] += (n + 31) // 32 * 32
            return t

        ident = small("ident", [P, P])
        rows = at("rows", [108, P], MISC + 22 * KB)
        cols = small("cols", [P, 108])
        tab = small("tab", [BUCKETS + 1, NH + DH])
        wg = at("wg", [P, KT, GN], MISC + 22 * KB + 512)
        twice = small("twice", [P, NG * NC_])
        gates = small("gates", [P, NT, GN])
        gcur = small("gcur", [P, NT, 6])
        ones = small("ones", [P, P])
        roots = small("roots", [P, S])
        kct = small("kct", [P, NG * NC_])
        kcur = small("kcur", [P, NC_])
        vc = small("vc", [NC_, NG, HD])
        vcur = small("vcur", [NC_, HD])
        hg = small("hg", [P, 2 * DH])
        hgcur = small("hgcur", [P, 2])
        lprod = small("lprod", [P, 2])
        lexp = small("lexp", [P, 2])
        neglam = small("neglam", [P, 1])
        warm = small("warm", [P, 1])
        ss = small("ss", [P, NT])
        ssp = small("ssp", [P, NT, NT])
        ms = small("ms", [P, NT])
        rstd = small("rstd", [P, NT])
        inv = small("inv", [P, NT])
        m = small("m", [P, NT])
        l1 = small("l1", [P, NT])
        l2 = small("l2", [P, NT])
        r1 = small("r1", [P, NT])
        r2 = small("r2", [P, NT])
        cm = small("cm", [P, NT])
        cl = small("cl", [P, NT])
        cr = small("cr", [P, NT])
        assert top[0] <= nc.sbuf_usable_end, (top[0], nc.sbuf_usable_end)

        def bank(name):
            return ctx.enter_context(nc.psum_tensor(name, [P, 512], F32))

        acc = [bank(f"acc{b}") for b in range(4)]
        e = [bank(f"e{b}") for b in range(3)]
        ob = bank("ob")
        bbanks = [e[1], e[2], ob, e[1]]
        nbanks = e + [ob]

        SEG = [(0, 0), (1, 0), (0, 128), (2, 0)]
        CSEG = 256
        ZOFF = [0, 128, 384, 768]
        TSEG = [(0, 0), (1, 0), (2, 0), (1, 384)]

        def sem(name):
            return ctx.enter_context(nc.semaphore(name))

        pool_waited, dve_waited = sem("pool_waited"), sem("dve_waited")
        x_landed = [sem(f"x_landed{n}") for n in range(NT)]
        diag_ready, roots_done, roots_ready = sem("diag_ready"), sem("roots_done"), sem("roots_ready")
        w_landed = [sem(f"w_landed{s}") for s in range(RAW)]
        hi_ready = sem("hi_ready")
        lo_ready = sem("lo_ready")
        pair_done = sem("pair_done")
        acc_done = sem("acc_done")
        acc_free = [sem(f"acc_free{b}") for b in range(4)]
        spilled = [sem(f"spilled{b}") for b in range(4)]
        rows_landed, tab_landed = sem("rows_landed"), sem("tab_landed")
        oh_landed, wg_landed = sem("oh_landed"), sem("wg_landed")
        tab_masked = sem("tab_masked")
        ident_ready, ones_ready = sem("ident_ready"), sem("ones_ready")
        cols_turned, cols_ready = sem("cols_turned"), sem("cols_ready")
        brow_done, brow_ready, brow_spilled = sem("brow_done"), sem("brow_ready"), sem("brow_spilled")
        skewed = sem("skewed")
        hg_ready, lprod_ready, lam_sum, lam_exp = sem("hg_ready"), sem("lprod_ready"), sem("lam_sum"), sem("lam_exp")
        dve = sem("dve")
        sq_ready, ms_ready, rstd_ready = sem("sq_ready"), sem("ms_ready"), sem("rstd_ready")
        turned, n_hi, n_lo = sem("turned"), sem("n_hi"), sem("n_lo")
        wg_padded, wg_hi_ready, wg_lo_ready, gn_done = sem("wg_padded"), sem("wg_hi_ready"), sem("wg_lo_ready"), sem("gn_done")
        gates_t_ready, gates_turned, gates_ready = sem("gates_t_ready"), sem("gates_turned"), sem("gates_ready")
        c_landed, w2_landed = sem("c_landed"), sem("w2_landed")
        twice_ready = sem("twice_ready")
        blk_ready, blk_hi_ready, blk_lo_ready = sem("blk_ready"), sem("blk_hi_ready"), sem("blk_lo_ready")
        hid_copied, hid_done, hid_ready = sem("hid_copied"), sem("hid_done"), sem("hid_ready")
        kvc_done, kvc_ready = sem("kvc_done"), sem("kvc_ready")
        nsa_loaded, diff_loaded = sem("nsa_loaded"), sem("diff_loaded")
        cur_ready = sem("cur_ready")
        scores_done, z_ready, p_exp, p_scaled = sem("scores_done"), sem("z_ready"), sem("p_exp"), sem("p_scaled")
        zc_ready, pc_exp, pc_scaled = sem("zc_ready"), sem("pc_exp"), sem("pc_scaled")
        pt_done, pt_ready, pv_done = sem("pt_done"), sem("pt_ready"), sem("pv_done")
        o_hi_ready, o_lo_ready = sem("o_hi_ready"), sem("o_lo_ready")
        o_spilled = [sem(f"o_spilled{k}") for k in range(4)]
        on_ready, on_sq, on_ms, on_rstd, on_scaled, ot_done = (sem("on_ready"), sem("on_sq"), sem("on_ms"),
                                                               sem("on_rstd"), sem("on_scaled"), sem("ot_done"))
        chain = sem("chain")
        o_landed = [sem(f"o_landed{k}") for k in range(PAIRS)]
        g_landed = [sem("ga_landed"), sem("gb_landed")]
        sig_ready, mix_sum, mix_hi, mix_lo = sem("sig_ready"), sem("mix_sum"), sem("mix_hi"), sem("mix_lo")
        res_landed = sem("res_landed")
        silu_ready, silu_rooted = sem("silu_ready"), sem("silu_rooted")
        f_hi_ready, f_lo_ready = sem("f_hi_ready"), sem("f_lo_ready")
        tail_done, weighted = sem("tail_done"), sem("weighted")
        fin_v_ready, fin_a_ready = sem("fin_v_ready"), sem("fin_a_ready")
        fg_landed, out_stored = sem("fg_landed"), sem("out_stored")

        w_proj_v = w_proj.rearrange("(k p) n -> p k n", p=P)
        w_up_v = w_up.rearrange("(k p) n -> p k n", p=P)
        w_out_v = w_out.rearrange("(k p) n -> p k n", p=P)
        w_ff_in_v = w_ff_in.rearrange("(k p) n -> p k n", p=P)
        w_ff_out_v = w_ff_out.rearrange("(c k p) n -> p c k n", p=P, k=FF_CHUNK)
        cw1_v = cw1.rearrange("s (j p) n -> s p j n", p=P)
        x_v = x.rearrange("(i p) n -> p i n", p=P)
        out_v = out.rearrange("(i p) n -> p i n", p=P)
        pt_v = proj_t.rearrange("f p s -> p f s")
        pn_v = proj_n.rearrange("i p n -> p i n")

        block = ctx.enter_context(nc.Block())

        @block.sync
        def _(sp):
            sp.dma_start(rows[:, :], vectors).then_inc(rows_landed, 16)

            def load(pair, k, source):
                if not isinstance(pair, int) or pair >= RAW:
                    sp.wait_ge(lo_ready, pair - RAW + 1)
                sp.dma_start(raw[k % RAW][:, :, :], source).then_inc(w_landed[k % RAW], 16)

            def job(pair, weights, col):
                for k in range(PAIRS):
                    load(pair + k, k, weights[:, 2 * k:2 * k + 2, bass.ds(col, COLS)])

            for k in range(PAIRS):
                if k < NT:
                    sp.dma_start(x_in[:, :, k * COLS:(k + 1) * COLS], x_v[:, :, k * COLS:(k + 1) * COLS]).then_inc(x_landed[k], 16)
                load(k, k, w_proj_v[:, 2 * k:2 * k + 2, 0:COLS])
                if k == NT - 1:
                    sp.dma_start(tab[0:BUCKETS, :], table).then_inc(tab_landed, 16)
                    sp.dma_start(oh[:, :], onehot).then_inc(oh_landed, 16)
            with sp.Fori(1, T_JOBS) as j:
                job(j * PAIRS, w_proj_v, j * COLS)
            for n, (kind, j, k) in enumerate(NAT):
                load(PAIR_N + n, n, w_proj_v[:, 2 * k:2 * k + 2, N_COL0 + j * COLS:N_COL0 + (j + 1) * COLS] if kind == "N"
                     else cw1_v[j, :, 4 * k:4 * k + 4, :])
            with sp.Fori(0, G_JOBS) as j:
                job(j * PAIRS + PAIR_G, w_proj_v, (j + T_JOBS) * COLS)
            with sp.Fori(0, NT) as c:
                job(c * PAIRS + PAIR_UP, w_up_v, c * COLS)
            with sp.Fori(0, NT) as c:
                job(c * PAIRS + PAIR_OUT, w_out_v, c * COLS)
            def ff_out(pair, c):
                for n in range(NT):
                    for k in range(2):
                        load(pair + 2 * n + k, 2 * n + k,
                             w_ff_out_v[:, bass.ds(c, 1), 2 * k:2 * k + 2, n * COLS:(n + 1) * COLS].rearrange("p c k n -> p (c k) n"))
            job(PAIR_FF, w_ff_in_v, 0)
            with sp.Fori(0, CHUNKS - 1) as c:
                job(c * FF_PAIRS + PAIR_FF + PAIRS, w_ff_in_v, c * COLS + DFF)
                job(c * FF_PAIRS + PAIR_FF + 2 * PAIRS, w_ff_in_v, c * COLS + COLS)
                ff_out(c * FF_PAIRS + PAIR_FF + 3 * PAIRS, c)
            job(PAIR_END - 2 * PAIRS, w_ff_in_v, (CHUNKS - 1) * COLS + DFF)
            ff_out(PAIR_END - PAIRS, CHUNKS - 1)
            for i in range(NT):
                for n, ready in enumerate((fin_v_ready, fin_a_ready)):
                    sp.wait_ge(ready, i + 1)
                    half = slice(n * DM // 2, (n + 1) * DM // 2)
                    sp.dma_start(out_v[:, i, half], res[:, i, half]).then_inc(out_stored, 16)
            sp.wait_ge(out_stored, 16 * 2 * NT)

        @block.gpsimd
        def _(pool):
            pool.memset(ident[:, :], 0.0).then_inc(ident_ready, 1)
            pool.wait_ge(ident_ready, 1)
            pool.affine_select(out=ident[:, :], in_=ident[:, :], compare_op=ALU.not_equal, fill=1.0, base=0,
                               pattern=[[-1, P]], channel_multiplier=1).then_inc(ident_ready, 1)
            pool.memset(ones[:, :], 1.0).then_inc(ones_ready, 1)
            pool.dma_start(wg[:, :, :], w_proj_v[:, :, GN_COL0:GN_COL0 + GN]).then_inc(wg_landed, 16)
            pool.wait_ge(turned, KT)
            pool.wait_ge(sq_ready, NT * NT)
            pool.memset(wg_hl[:, :, :, GN:P // 2].bitcast(F32), 0.0).then_inc(wg_padded, 1)

            def spill_t(tile0, job):
                for b in range(4):
                    pool.wait_ge(acc_free[b], job + 1).then_inc(pool_waited, 1)
                    pool.dma_start(pt_v[:, bass.ds(tile0 + b, 1), :].rearrange("p f s -> p (f s)"),
                                   stage[b][:, :]).then_inc(spilled[b], 16)

            with pool.Fori(0, T_JOBS) as j:
                spill_t(j * NT, j)
            for b in range(4):
                pool.wait_ge(spilled[b], 16 * T_JOBS)
            pool.dma_start(c_in[:, :, :], pt_v[:, C_TILE:C_TILE + 4, :]).then_inc(c_landed, 16)
            pool.wait_ge(gn_done, 1)
            pool.dma_start(w2[:, :, :, :], cw2.rearrange("s (k p) n -> p s k n", p=P)).then_inc(w2_landed, 16)
            pool.wait_ge(brow_ready, 4)
            pool.dma_start(bias_d, brow[:, :]).then_inc(brow_spilled, 16)
            pool.wait_ge(brow_spilled, 16)
            for h in range(NH + DH):
                pool.dma_start(skew_w[h, :, 0:REV], bias_d[h:h + 1, 0:REV].to_broadcast([P, REV])).then_inc(skewed, 16)
            for h in range(NH):
                pool.dma_start(cskew_w[h, :, 0:FWD], bias_d[h:h + 1, REV:ROW].to_broadcast([NC_, FWD])).then_inc(skewed, 16)


            def load_nsa(t, g):
                pool.dma_start(q2[:, :, :], pt_v[:, bass.ds(2 * t, 2), :]).then_inc(nsa_loaded, 16)
                for n in range(2):
                    pool.dma_start(k2[:, n, :], pt_v[:, bass.ds(g + (K_TILE + 2 * n), 1), :].rearrange("p f s -> p (f s)"))\
                        .then_inc(nsa_loaded, 16)
                if isinstance(t, int):
                    for b in range(4):
                        pool.wait_ge(spilled[b], 16 * (T_JOBS + 1))
                for n in range(2):
                    pool.dma_start(v2[:, :, n, :], pn_v[:, :, bass.ds(g * HD + n * DV, HD)]).then_inc(nsa_loaded, 16)

            def load_nsa_bias(t):
                pool.dma_start(bias[:, 0:2, :], skew_r[bass.ds(2 * t, 2), :, P - 1:P - 1 + S].rearrange("h p s -> p h s"))\
                    .then_inc(nsa_loaded, 16)
                pool.dma_start(cbias[:, :, :], cskew_r[bass.ds(2 * t, 2), :, FWD0 - CL + 1:FWD0 - CL + 1 + S]
                               .rearrange("h c s -> c h s")).then_inc(nsa_loaded, 16)

            def load_diff_qk(t):
                pool.dma_start(qd[:, :, :], pt_v[:, bass.ds(2 * t + QD_TILE, 2), :]).then_inc(diff_loaded, 16)
                pool.dma_start(kd[:, :, :], pt_v[:, bass.ds(2 * t + KD_TILE, 2), :]).then_inc(diff_loaded, 16)

            def load_diff_v(t):
                pool.dma_start(vd[:, :, :], pn_v[:, :, bass.ds(t * DV + COLS, DV)]).then_inc(diff_loaded, 16)

            def load_diff_bias(t):
                pool.dma_start(bias[:, 2, :], skew_r[bass.ds(t + NH, 1), :, P - 1:P - 1 + S].rearrange("h p s -> p (h s)"))\
                    .then_inc(diff_loaded, 16)

            for j in range(N_JOBS):
                for b in range(4):
                    pool.wait_ge(acc_free[b], JOB_N + j + 1)
                    pool.dma_start(proj_n[b, :, j * COLS:(j + 1) * COLS], stage[b][:, :]).then_inc(spilled[b], 16)
                if j == 1:
                    pool.wait_ge(blk_lo_ready, 2)
                    load_nsa(0, 0)
                    load_diff_qk(0)
                    pool.wait_ge(skewed, 16 * (2 * NH + DH))
                    pool.wait_ge(pair_done, C_END[0])
                    load_nsa_bias(0)
                    load_diff_bias(0)
            for b in range(4):
                pool.wait_ge(spilled[b], 16 * (T_JOBS + N_JOBS))
            load_diff_v(0)

            def spill_o(slot, ready, tile):
                pool.wait_ge(o_lo_ready, ready).then_inc(pool_waited, 1)
                pool.dma_start(o_hi_d[bass.ds(tile, 1), :, :].rearrange("f p s -> (f p) s"),
                               s_hi[slot][:, :].bitcast(F32)).then_inc(o_spilled[slot], 16)
                pool.dma_start(o_lo_d[bass.ds(tile, 1), :, :].rearrange("f p s -> (f p) s"),
                               s_lo[slot][:, :].bitcast(F32)).then_inc(o_spilled[slot], 16)

            with pool.Fori(0, ITERS - 1) as t:
                spill_o(0, 4 * t + 1, 2 * t)
                spill_t(8 * t + G_TILE, 2 * t + JOB_G)
                spill_o(1, 4 * t + 2, 2 * t + 1)
                load_nsa(t + 1, (t + 1) // 2)
                load_nsa_bias(t + 1)
                spill_o(2, 4 * t + 3, 2 * t + NH)
                spill_o(3, 4 * t + 4, 2 * t + (NH + 1))
                load_diff_qk(t + 1)
                load_diff_v(t + 1)
                load_diff_bias(t + 1)
                spill_t(8 * t + (G_TILE + 4), 2 * t + (JOB_G + 1))

            def reload_o(ks):
                for k in ks:
                    pool.wait_ge(pair_done, PAIR_UP - PAIRS + k + 1)
                    for d, t in ((o_hi_d, o_hi), (o_lo_d, o_lo)):
                        pool.dma_start(t[:, 2 * k:2 * k + 2, :].bitcast(F32),
                                       d[2 * k:2 * k + 2].rearrange("f p s -> p f s")).then_inc(o_landed[k], 16)

            t = ITERS - 1
            spill_o(0, 4 * t + 1, 2 * t)
            spill_t(8 * t + G_TILE, 2 * t + JOB_G)
            spill_o(1, 4 * t + 2, 2 * t + 1)
            for k in range(2):
                pool.wait_ge(o_spilled[k], 32 * ITERS)
            reload_o(range(4))
            spill_o(2, 4 * t + 3, 2 * t + NH)
            spill_o(3, 4 * t + 4, 2 * t + (NH + 1))
            for k in range(2, 4):
                pool.wait_ge(o_spilled[k], 32 * ITERS)
            for b in range(4):
                pool.wait_ge(spilled[b], 16 * (T_JOBS + N_JOBS + G_JOBS - 1))
            for n, t in enumerate((ga, gb)):
                pool.dma_start(t[:, :, :], pt_v[:, G_TILE + KT * n:G_TILE + KT * n + NT, :]).then_inc(g_landed[n], 16)
                reload_o(range(4 + 2 * n, 6 + 2 * n))
            spill_t(8 * (ITERS - 1) + (G_TILE + 4), JOB_UP - 1)
            for b in range(4):
                pool.wait_ge(spilled[b], 16 * (T_JOBS + N_JOBS + G_JOBS))
            with pool.Fori(1, NT) as c:
                pool.wait_ge(mix_lo, c * NT).then_inc(pool_waited, 1)
                for n, t in enumerate((ga, gb)):
                    pool.dma_start(t[:, :, :], pt_v[:, bass.ds(c * NT + (G_TILE + KT * n), NT), :]).then_inc(g_landed[n], 16)
            pool.wait_ge(pair_done, PAIR_OUT)
            for i in range(NT):
                pool.dma_start(res[:, i, :], x_v[:, i, :]).then_inc(res_landed, 16)
            pool.dma_start(fg[:, :], bass.AP(final_g.tensor, 0, [[0, P], [1, DM]])).then_inc(fg_landed, 16)

        @block.tensor
        def _(pe):
            mm = nc.tensor.matmul

            pe.wait_ge(ident_ready, 2)
            pe.wait_ge(rows_landed, 16)
            nc.tensor.transpose(acc[3][:, 0:108], rows[:, :], ident[0:108, 0:108]).then_inc(cols_turned, 1)

            def turn(src, norm, k):
                if norm == 0 and k % NT == 0:
                    pe.wait_ge(x_landed[k // NT], 16)
                if NT * norm + k >= NT:
                    pe.wait_ge(n_lo, KT * norm + k - (NT - 1))
                for i in range(NT):
                    t = nc.tensor.transpose(nbanks[k % NT][:, i * P:(i + 1) * P], src[:, i, k * P:(k + 1) * P], ident[:, :])
                t.then_inc(turned, 1)

            def turning(src, diag, norm):
                def before(kt):
                    first = 2 * kt if norm == 0 and kt < 2 else kt + 2
                    for k in range(first, min(kt + 3 if norm == 1 or kt else 2, KT)):
                        turn(src, norm, k)
                    pe.wait_ge(n_lo, KT * norm + kt + 1)
                    if kt == KT - 1:
                        pe.wait_ge(ones_ready, 1)
                        for i in range(NT):
                            pe.wait_ge(diag_ready, NT * norm + i + 1)
                            t = mm(e[0][:, i * P:(i + 1) * P], ones[:, :], diag[:, i, :], start=True, stop=True)
                        t.then_inc(roots_done, 1)
                return before

            def tile(slot, i, a_hi, a_lo, a, natural, first, last, done, job):
                wh, wl = w_hi[slot], w_lo[slot]
                for b in range(4):
                    if first and not (isinstance(job, int) and job == 0):
                        pe.wait_ge(acc_free[b], job)
                    bl = slice(b * P, (b + 1) * P)
                    for n, (w, h) in enumerate(((wl, a_hi), (wh, a_lo), (wh, a_hi))):
                        lhs, rhs = (h[:, a, bl], w[:, i, :]) if natural else (w[:, i, bl], h[:, a, :])
                        t = mm(acc[b][:, :], lhs, rhs, start=first and n == 0, stop=last and n == 2)
                    if last and b < 3:
                        t.then_inc(acc_done, 1)
                if done:
                    t.then_inc(pair_done, 1)

            def job(pair, number, a_hi, a_lo, natural, k0=0, k1=PAIRS, before=None):
                for k in range(k0, k1):
                    for i in range(2):
                        if before:
                            before(2 * k + i)
                        if i == 0:
                            pe.wait_ge(lo_ready, pair + (k - k0 + 1))
                        tile(k % HL, i, a_hi, a_lo, 2 * k + i, natural, k == k0 and i == 0,
                             k == k1 - 1 and i == 1, i == 1, number)

            pe.wait_ge(cols_ready, 1)
            job(0, 0, h_hi, h_lo, False, before=turning(x_in, diag1, 0))
            with pe.Fori(1, T_JOBS) as j:
                job(j * PAIRS, j, h_hi, h_lo, False)

            pe.wait_ge(roots_ready, 1)
            pe.wait_ge(wg_lo_ready, 1)
            pe.wait_ge(wg_padded, 1)
            for k in range(KT):
                for n, h in enumerate((h_lo, h_hi)):
                    t = mm(e[0][:, :], wg_hl[:, k, :, :].rearrange("p h n -> p (h n)"), h[:, k, :],
                           start=k == 0 and n == 0, stop=k == KT - 1 and n == 1)
            t.then_inc(gn_done, 1)

            pe.wait_ge(tab_landed, 16)
            pe.wait_ge(tab_masked, 1)
            pe.wait_ge(oh_landed, 16)
            for n in range(4):
                w = min(512, ROW - 512 * n)
                if n == 3:
                    pe.wait_ge(brow_ready, 1)
                mm(bbanks[n][0:NH + DH, 0:w], tab[:, :], oh[:, 512 * n:512 * n + w], start=True, stop=True).then_inc(brow_done, 1)

            def turn_gates():
                pe.wait_ge(gates_t_ready, 1)
                pe.wait_ge(twice_ready, 1)
                for i in range(NT):
                    t = mm(e[0][:, i * P // 2:(i + 1) * P // 2], gates_t[:, i * P:(i + 1) * P], twice[:, :], start=True, stop=True)
                t.then_inc(gates_turned, 1)

            def lambda_sums():
                pe.wait_ge(ones_ready, 1)
                pe.wait_ge(lprod_ready, 2)
                pe.wait_ge(gates_ready, NT)
                mm(e[0][:, 0:2], ones[:, :], lprod[:, :], start=True, stop=True).then_inc(lam_sum, 1)

            def sum_halves(s):
                pe.wait_ge(hid_copied, s + 1)
                if s == 1:
                    pe.wait_ge(hid_ready, 1)
                for u in range(2):
                    t = mm(e[1][:, u * NG * NC_:(u + 1) * NG * NC_], hid_hl[:, s, u * P:(u + 1) * P], twice[:, :],
                           start=True, stop=True)
                t.then_inc(hid_done, 1)

            def compressed_k():
                pe.wait_ge(w2_landed, 16)
                pe.wait_ge(hid_ready, 1)
                pe.wait_ge(lam_exp, 1)
                for u in range(2):
                    t = mm(e[0][:, 0:NG * NC_], w2[:, 0, u, :], hid[:, 0, u, :], start=u == 0, stop=u == 1)
                t.then_inc(kvc_done, 1)

            def compressed_v():
                pe.wait_ge(hid_ready, 2)
                for g in range(NG):
                    for u in range(2):
                        t = mm(e[2][0:NC_, g * HD:(g + 1) * HD], hid[:, 1, u, g * NC_:(g + 1) * NC_], w2[:, 1, u, :],
                               start=u == 0, stop=u == 1)
                t.then_inc(kvc_done, 1)

            for n, step in enumerate(NAT):
                if step == ("N", 0, 6):
                    turn_gates()
                elif step == ("N", 1, 0):
                    lambda_sums()
                elif step == ("N", 2, 1):
                    sum_halves(0)
                elif step == ("N", 2, 4):
                    compressed_k()
                elif step == ("N", 2, 5):
                    sum_halves(1)
                elif step == ("N", 2, 7):
                    compressed_v()
                pe.wait_ge(lo_ready, PAIR_N + n + 1)
                kind, j, k = step
                if kind == "N":
                    for i in range(2):
                        tile(n % HL, i, h_hi, h_lo, 2 * k + i, True, k == 0 and i == 0, k == PAIRS - 1 and i == 1,
                             i == 1, JOB_N + j)
                    continue
                if k == 0:
                    pe.wait_ge(blk_lo_ready, j + 1)
                    pe.wait_ge(brow_ready, 4)
                wh = w_hi[n % HL][:, :, :].rearrange("p a (b n) -> p (a b) n", b=2)
                wl = w_lo[n % HL][:, :, :].rearrange("p a (b n) -> p (a b) n", b=2)
                for jj in range(4):
                    for part, w in enumerate((wl, wh)):
                        t = mm((e[2], ob)[j][:, 0:CH], blk_hl[:, j, 4 * k + jj, :], w[:, jj, :],
                               start=k == 0 and jj == 0 and part == 0, stop=k == PAIRS - 1 and jj == 3 and part == 1)
                t.then_inc(pair_done, 1)
            pe.wait_ge(kvc_ready, 2)

            with pe.Fori(0, ITERS) as t:
                def scores(u):
                    q, k = (q2, k2) if u < 4 else (qd, kd)
                    qs, ks = (u // 2, u % 2) if u < 4 else (u - 4, u - 4)
                    if u == 0:
                        pe.wait_ge(nsa_loaded, 16 * 7 * (t + 1))
                        pe.wait_ge(cur_ready, 4 * t + 4)
                    if u == 4:
                        pe.wait_ge(diff_loaded, 16 * 4 * (t + 1))
                    if u == 5:
                        pe.wait_ge(z_ready, 24 * t + 20)
                    for i in ORDER:
                        b, c = SEG[i]
                        n = (i + 1) * P
                        s = mm(e[b][:, c:c + n], q[:, qs, i * P:(i + 1) * P], k[:, ks, 0:n], start=True, stop=True)
                        if i == 1 and u in (0, 2):
                            for j in range(NT):
                                c = CSEG + j * NC_
                                mm(e[1][:, c:c + NC_], q[:, qs, j * P:(j + 1) * P], kcur[:, :], start=True, stop=False)
                                s = mm(e[1][:, c:c + NC_], cbias[:, qs, j * P:(j + 1) * P], ident[0:NC_, 0:NC_],
                                       start=False, stop=True)
                        if i > 0:
                            s.then_inc(scores_done, 1)

                def transposes(u):
                    p = p_a if u < 4 else p_b
                    pe.wait_ge(p_scaled, 20 * t + 4 * (u + 1))
                    for kt in (0, 1, 3, 2):
                        b, c = TSEG[kt]
                        for i in range(kt, NT):
                            s = nc.tensor.transpose(e[b][:, c + (i - kt) * P:c + (i - kt + 1) * P],
                                                    p[:, ZOFF[i] + kt * P:ZOFF[i] + (kt + 1) * P], ident[:, :])
                        if kt != 1:
                            s.then_inc(pt_done, 1)
                    if u in (0, 2):
                        if u == 2:
                            pe.wait_ge(o_lo_ready, 4 * t + 1)
                        pe.wait_ge(pc_scaled, 2 * t + (1 + u // 2))
                        for i in range(NT):
                            s = nc.tensor.transpose(ob[0:NC_, i * P:(i + 1) * P], pc[:, i, :], ident[:, :])
                        s.then_inc(pt_done, 1)

                def values(u):
                    pe.wait_ge(pt_ready, 17 * t + U_PT[u + 1])
                    if u < 4:
                        if u % 2 == 0:
                            mm(ob[:, :], vcur[:, :], pct[:, :], start=True, stop=False)
                        for kt in range(NT):
                            b, c = TSEG[kt]
                            n = (NT - kt) * P
                            s = mm(ob[:, kt * P:S], v2[:, kt, u % 2, :], pt[:, 512 * b + c:512 * b + c + n],
                                   start=False, stop=u % 2 == 1 and kt == NT - 1)
                    else:
                        pe.wait_ge(o_lo_ready, 4 * t + 2)
                        for i in range(NT):
                            o, c = (ob, i * DV) if i < 2 else (e[0], (i - 2) * DV)
                            for kt in range(i + 1):
                                b, c0 = TSEG[kt]
                                c1 = 512 * b + c0 + (i - kt) * P
                                s = mm(o[:, c:c + DV], pt[:, c1:c1 + P], vd[:, kt, :], start=kt == 0, stop=kt == i)
                    s.then_inc(pv_done, 1)

                def turn_o(_):
                    pe.wait_ge(on_scaled, t + 1)
                    for h in range(2):
                        for i in range(NT):
                            s = nc.tensor.transpose(e[1 + h][:, i * P:(i + 1) * P], on[:, i, h * P:(h + 1) * P], ident[:, :])
                        s.then_inc(ot_done, 1)

                def pieces(first):
                    def before(tile):
                        for kind, u in AT.get(first + tile, ()):
                            {"S": scores, "T": transposes, "V": values, "O": turn_o}[kind](u)
                    return before

                for n in range(2):
                    job(t * (2 * PAIRS) + (PAIR_G + n * PAIRS), 2 * t + (JOB_G + n), h_hi, h_lo, False, before=pieces(16 * n))
                pe.wait_ge(o_lo_ready, 4 * t + 4)

            def up(c, landed):
                for n in range(2):
                    k0 = 4 * n
                    for k in range(k0, k0 + 4):
                        pe.wait_ge(lo_ready, c * PAIRS + (PAIR_UP + k + 1))
                        if landed:
                            pe.wait_ge(o_landed[k], 32)
                        for i in range(2):
                            tile(k % HL, i, o_hi, o_lo, 2 * k + i, False, k == k0 and i == 0, k == k0 + 3 and i == 1,
                                 i == 1, 2 * c + (JOB_UP + n))
            up(0, True)
            with pe.Fori(1, NT) as c:
                up(c, False)

            with pe.Fori(0, NT - 1) as c:
                job(c * PAIRS + PAIR_OUT, c + JOB_OUT, m_hi, m_lo, True,
                    before=lambda k: pe.wait_ge(mix_lo, k + 1))
            job((NT - 1) * PAIRS + PAIR_OUT, NT - 1 + JOB_OUT, m_hi, m_lo, True,
                before=lambda k: turn(res, 1, (k - 13) // 2) if k in (13, 15) else None)

            def ff_out(pair, number, c):
                for n in range(NT):
                    for k in range(2):
                        pe.wait_ge(lo_ready, pair + (2 * n + k + 1))
                        for i in range(2):
                            if n == 0:
                                pe.wait_ge(f_lo_ready, 4 * c + (2 * k + i + 1))
                            tile((2 * n + k) % HL, i, f_hi, f_lo, 2 * k + i, True, k == 0 and i == 0,
                                 k == 1 and i == 1, i == 1, number + n)

            job(PAIR_FF, JOB_FF, h2_hi, h2_lo, False, before=turning(res, diag2, 1))
            with pe.Fori(0, CHUNKS - 1) as c:
                job(c * FF_PAIRS + (PAIR_FF + PAIRS), c * FF_JOBS + (JOB_FF + 1), h2_hi, h2_lo, False)
                job(c * FF_PAIRS + (PAIR_FF + 2 * PAIRS), c * FF_JOBS + (JOB_FF + 2), h2_hi, h2_lo, False)
                ff_out(c * FF_PAIRS + (PAIR_FF + 3 * PAIRS), c * FF_JOBS + (JOB_FF + 3), c)
            last = JOB_FF + (CHUNKS - 1) * FF_JOBS
            job(PAIR_END - 2 * PAIRS, last + 1, h2_hi, h2_lo, False)
            c = CHUNKS - 1
            for i in range(NT):
                bl = slice(i * P, (i + 1) * P)
                for n in range(NT):
                    pe.wait_ge(acc_free[n], last + 2 + i)
                    for k in range(FF_CHUNK):
                        if i == 0:
                            if k % 2 == 0:
                                pe.wait_ge(lo_ready, PAIR_END - PAIRS + 2 * n + k // 2 + 1)
                            if n == 0:
                                pe.wait_ge(f_lo_ready, 4 * c + k + 1)
                        wh, wl = (last_w(half, 2 * n + k // 2)[:, k % 2, :] for half in range(2))
                        for part, (w, h) in enumerate(((wl, f_hi), (wh, f_lo), (wh, f_hi))):
                            t = mm(acc[n][:, :], h[:, k, bl], w, start=k == 0 and part == 0, stop=k == FF_CHUNK - 1 and part == 2)
                    t.then_inc(tail_done, 1)

        @block.scalar
        def _(act):
            A = nc.scalar.activation

            def norm_hi(norm, ks, g0, dst):
                for k in ks:
                    act.wait_ge(turned, KT * norm + k + 1)
                    A(dst[:, k, :], nbanks[k % NT][:, :], ACT.Copy, scale=cols[:, g0 + k:g0 + k + 1]).then_inc(n_hi, 1)

            def evacuate(done, spill):
                for b in (0, 2):
                    act.wait_ge(spilled[b], 16 * spill)
                    act.wait_ge(acc_done, 3 * done + (b + 1))
                    A(stage[b][:, :], acc[b][:, :], ACT.Copy, scale=rstd[:, b:b + 1]).then_inc(acc_free[b], 1)

            def sweep(first, uses, ks=range(AHEAD, PAIRS + AHEAD)):
                for k in ks:
                    a = k % PAIRS
                    act.wait_ge(w_landed[a % RAW], 16 * (uses + (k // RAW + 1)))
                    if not isinstance(first, int) or first + k >= HL:
                        act.wait_ge(pair_done, first + (k - HL + 1))
                    A(w_hi[a % HL][:, :, :], raw[a % RAW][:, :, :], ACT.Copy).then_inc(hi_ready, 1)
                    yield k - AHEAD

            def run(first, uses, ks=range(AHEAD, PAIRS + AHEAD)):
                for _ in sweep(first, uses, ks):
                    pass

            def norm_job(first, uses, norm, g0, dst):
                if norm == 0:
                    for k in range(AHEAD):
                        norm_hi(norm, (k,), g0, dst)
                        run(first, uses, (k,))
                for k in sweep(first, uses):
                    norm_hi(norm, (2 * k + 2, 2 * k + 3) if k < PAIRS - 1 else (), g0, dst)
                    if norm == 0 and 1 <= k <= NT:
                        act.wait_ge(x_landed[k - 1], 16)
                        bl = slice((k - 1) * COLS, k * COLS)
                        for i in range(NT):
                            A(x_sq[:, i, bl], x_in[:, i, bl], ACT.Square, accum_out=ssp[:, i, k - 1:k]).then_inc(sq_ready, 1)
                    if k == (NT + 1, 1)[norm]:
                        act.wait_ge(ms_ready, norm + 1)
                        A(rstd[:, :], ms[:, :], ACT.Sqrt).then_inc(rstd_ready, 1)

            def warm_sqrt():
                A(warm[:, :], ones[:, 0:1], ACT.Sqrt)

            act.wait_ge(cols_turned, 1)
            A(cols[:, :], acc[3][:, 0:108], ACT.Copy).then_inc(cols_ready, 1)
            act.wait_ge(cols_ready, 1)
            norm_job(0, 0, 0, 0, h_hi)
            act.wait_ge(wg_landed, 16)
            A(wg_hl[:, :, 0, 0:GN], wg[:, :, :], ACT.Copy).then_inc(wg_hi_ready, 1)
            with act.Fori(1, T_JOBS) as j:
                run(j * PAIRS, 2 * j)
            def move_gates():
                act.wait_ge(gn_done, 1)
                A(gates_t[:, :], e[0][:, :], ACT.Copy).then_inc(gates_t_ready, 1)

            def sigmoid_gates():
                act.wait_ge(gates_turned, 1)
                for i in range(NT):
                    A(gates[:, i, :], e[0][:, i * P // 2:i * P // 2 + GN], ACT.Sigmoid, scale=rstd[:, i:i + 1])\
                        .then_inc(gates_ready, 1)

            def block_hi(s):
                act.wait_ge(blk_ready, 6 * (s + 1))
                A(blk_hl[:, s, :, 0:NG * NC_], blk[:, s, :, :], ACT.Copy).then_inc(blk_hi_ready, 1)

            def exp_lambda():
                act.wait_ge(lam_sum, 1)
                A(lexp[:, :], e[0][:, 0:2], ACT.Exp).then_inc(lam_exp, 1)

            def gelu(s):
                act.wait_ge(hid_done, s + 1)
                A(hid[:, s, :, :], e[1][:, 0:2 * NG * NC_].rearrange("p (u n) -> p u n", u=2), ACT.Gelu_apprx_tanh)\
                    .then_inc(hid_ready, 1)

            def move_kc():
                act.wait_ge(kvc_done, 1)
                A(kct[:, :], e[0][:, 0:NG * NC_], ACT.Copy).then_inc(kvc_ready, 1)

            for n in sweep(PAIR_N, PAIR_N // RAW, range(AHEAD, len(NAT) + AHEAD)):
                if NAT[n] == ("N", 0, 0):
                    move_gates()
                elif NAT[n] == ("N", 0, 5):
                    block_hi(0)
                elif NAT[n] == ("N", 0, 6):
                    sigmoid_gates()
                elif NAT[n] == ("N", 1, 1):
                    exp_lambda()
                elif NAT[n] == ("N", 1, 4):
                    block_hi(1)
                elif NAT[n] == ("N", 2, 1):
                    gelu(0)
                elif NAT[n] == ("N", 2, 4):
                    move_kc()
                elif NAT[n] == ("N", 2, 5):
                    gelu(1)
                if NAT[n][0] == "N" and NAT[n][2] == PAIRS - 1:
                    evacuate(NAT[n][1] + JOB_N, NAT[n][1] + JOB_N)

            with act.Fori(0, ITERS) as t:
                def exps(u):
                    p, l = (p_a, l1) if u < 5 else (p_b, l2)
                    for n, i in enumerate(ORDER):
                        act.wait_ge(z_ready, 24 * t + (4 * u + n + 1))
                        n = (i + 1) * P
                        A(p[:, ZOFF[i]:ZOFF[i] + n], z[:, ZOFF[i]:ZOFF[i] + n], ACT.Exp, bias=m[:, i:i + 1],
                          scale=-1.0, accum_out=l[:, i:i + 1]).then_inc(p_exp, 1)
                    if u in (0, 2):
                        act.wait_ge(zc_ready, 2 * t + (1 + u // 2))
                        A(pc[:, :, :], zc[:, :, :], ACT.Exp, scale=SCALE).then_inc(pc_exp, 1)

                def move_pt(u):
                    act.wait_ge(pt_done, 17 * t + (U_PT[u] + 2))
                    A(pt[:, 512:1024], e[1][:, :], ACT.Copy).then_inc(pt_ready, 1)
                    if u in (0, 2):
                        act.wait_ge(pt_done, 17 * t + (U_PT[u] + 4))
                        A(pct[:, :], ob[0:NC_, :], ACT.Copy).then_inc(pt_ready, 1)

                def outputs(u):
                    if u in (1, 3):
                        act.wait_ge(pv_done, 5 * t + (u + 1))
                        A(s_hi[u // 2][:, :], ob[:, :], ACT.Copy).then_inc(o_hi_ready, 1)
                    if u == 4:
                        act.wait_ge(on_ready, 2 * t + 2)
                        for i in range(NT):
                            A(z[:, 0:DV], on[:, i, :], ACT.Square, accum_out=ss[:, i:i + 1]).then_inc(on_sq, 1)
                            act.wait_ge(on_sq, 4 * t + (i + 1))
                        act.wait_ge(on_ms, t + 1)
                        A(rstd[:, :], ms[:, :], ACT.Sqrt).then_inc(on_rstd, 1)

                def turned_o(_):
                    for h in range(2):
                        act.wait_ge(ot_done, 2 * t + (h + 1))
                        A(s_hi[2 + h][:, :], e[1 + h][:, :], ACT.Copy, scale=hgcur[:, h:h + 1]).then_inc(o_hi_ready, 1)

                for n in range(2):
                    for k in sweep(t * (2 * PAIRS) + (PAIR_G + n * PAIRS), 4 * t + (PAIR_G // RAW + 2 * n)):
                        for i in range(2):
                            for kind, u in AT.get(16 * n + 2 * k + i, ()):
                                {"S": exps, "T": move_pt, "V": outputs, "O": turned_o}[kind](u)
                for k in range(4):
                    act.wait_ge(o_spilled[k], 32 * (t + 1))

            def up(c):
                for k in sweep(c * PAIRS + PAIR_UP, 2 * c + PAIR_UP // RAW):
                    if k in (2, 3):
                        act.wait_ge(g_landed[k - 2], 16 * (c + 1))
                        t = (ga, gb)[k - 2]
                        A(t[:, :, :], t[:, :, :], ACT.Sigmoid).then_inc(sig_ready, 1)
                for b in range(4):
                    act.wait_ge(mix_sum, 4 * c + (b + 1))
                    A(m_hi[:, bass.ds(4 * c + b, 1), :], gb[:, b:b + 1, :], ACT.Copy).then_inc(mix_hi, 1)
            with act.Fori(0, NT) as c:
                up(c)
            def square_block(c):
                for b in range(NT):
                    act.wait_ge(acc_free[b], c + (JOB_OUT + 1))
                    A(ga[:, b, :], res[:, b, bass.ds(c * COLS, COLS)], ACT.Square,
                      accum_out=ssp[:, b, bass.ds(c, 1)]).then_inc(sq_ready, 1)

            with act.Fori(0, NT - 1) as c:
                run(c * PAIRS + PAIR_OUT, 2 * c + PAIR_OUT // RAW)
                square_block(c)
            for k in sweep((NT - 1) * PAIRS + PAIR_OUT, 2 * (NT - 1) + PAIR_OUT // RAW):
                if k >= PAIRS - 2:
                    act.wait_ge(pair_done, PAIR_FF - PAIRS + 1)
                    norm_hi(1, (k - (PAIRS - 2),), 16, h2_hi)
            square_block(NT - 1)

            def silus(done):
                for b in range(4):
                    act.wait_ge(acc_free[b], done + 1)
                    A(silu[:, b, :], silu[:, b, :], ACT.Silu).then_inc(silu_ready, 1)

            def f_his(done):
                for b in range(4):
                    act.wait_ge(acc_free[b], done + 1)
                    A(f_hi[:, b, :], silu[:, b, :], ACT.Copy).then_inc(f_hi_ready, 1)

            norm_job(PAIR_FF, PAIR_FF // RAW, 1, 16, h2_hi)
            silus(JOB_FF)
            with act.Fori(0, CHUNKS - 1) as c:
                p0 = c * FF_PAIRS + PAIR_FF
                u0 = c * (FF_PAIRS // RAW) + PAIR_FF // RAW
                run(p0 + PAIRS, u0 + 2)
                f_his(c * FF_JOBS + (JOB_FF + 1))
                run(p0 + 2 * PAIRS, u0 + 4)
                silus(c * FF_JOBS + (JOB_FF + 2))
                run(p0 + 3 * PAIRS, u0 + 6)
            run(PAIR_END - 2 * PAIRS, PAIR_END // RAW - 4, range(AHEAD, PAIRS))

            def last_his(ks):
                for k in ks:
                    act.wait_ge(w_landed[k % RAW], 16 * ((PAIR_END - PAIRS + k) // RAW + 1))
                    act.wait_ge(pair_done, PAIR_END - 2 * PAIRS + k + 1)
                    A(last_w(0, k), raw[k % RAW][:, :, :], ACT.Copy).then_inc(hi_ready, 1)

            last = JOB_FF + (CHUNKS - 1) * FF_JOBS
            last_his(range(4))
            f_his(last + 1)
            last_his(range(4, PAIRS))
            warm_sqrt()
            for i in range(NT):
                for n in range(NT):
                    act.wait_ge(acc_free[n], last + i + 3)
                    A(ga[:, n, :], res[:, i, n * COLS:(n + 1) * COLS], ACT.Square, accum_out=ssp[:, i, n:n + 1]).then_inc(sq_ready, 1)
                act.wait_ge(ms_ready, i + 3)
                A(rstd[:, i:i + 1], ms[:, i:i + 1], ACT.Sqrt).then_inc(rstd_ready, 1)
                act.wait_ge(rstd_ready, i + 3)
                act.wait_ge(weighted, NT * (i + 1))
                A(res[:, i, DM // 2:DM], res[:, i, DM // 2:DM], ACT.Copy, scale=rstd[:, i:i + 1]).then_inc(fin_a_ready, 1)

        @block.vector
        def _(v):
            V = nc.vector
            chained = [0]

            def link(ins):
                chained[0] += 1
                ins.then_inc(dve, 1)
                v.wait_ge(dve, chained[0])

            V.memset(tab[BUCKETS:BUCKETS + 1, :], -MASKED).then_inc(tab_masked, 1)
            v.wait_ge(cols_ready, 1)

            def root(i0, i1, n):
                link(V.tensor_scalar(inv[:, i0:i1], ss[:, i0:i1], 1.0 / DM, EPS, ALU.mult, ALU.add))
                V.reciprocal(ms[:, i0:i1], inv[:, i0:i1]).then_inc(ms_ready, 1)
                v.wait_ge(rstd_ready, n)

            def norm_lo(norm, ks, g0, hi, lo):
                for k in ks:
                    v.wait_ge(n_hi, KT * norm + k + 1)
                    V.scalar_tensor_tensor(out=lo[:, k, :], in0=nbanks[k % NT][:, :], scalar=cols[:, g0 + k:g0 + k + 1],
                                           in1=hi[:, k, :].bitcast(F32), op0=ALU.mult, op1=ALU.subtract).then_inc(n_lo, 1)

            def norm_job(first, norm, g0, hi, lo, diag):
                if norm == 0:
                    for k in range(AHEAD):
                        norm_lo(norm, (k,), g0, hi, lo)
                        lows(first, k - AHEAD)
                for k in range(PAIRS):
                    lows(first, k)
                    norm_lo(norm, (2 * k + 2, 2 * k + 3) if k < PAIRS - 1 else (), g0, hi, lo)
                    if k == (NT + 1, 1)[norm]:
                        v.wait_ge(sq_ready, NT * NT * (norm + 1))
                        link(V.tensor_reduce(ss[:, :], ssp[:, :, :], AX.X, ALU.add))
                        root(0, NT, norm + 1)
                        for i in range(NT):
                            V.tensor_scalar(diag[:, i, :], ident[:, :], rstd[:, i:i + 1], None, ALU.mult).then_inc(diag_ready, 1)
                v.wait_ge(roots_done, norm + 1)
                V.tensor_copy(roots[:, :], e[0][:, :]).then_inc(roots_ready, 1)
                v.wait_ge(roots_ready, norm + 1)

            def lows(pair, k):
                v.wait_ge(hi_ready, pair + (k + AHEAD + 1))
                s = (k + AHEAD) % HL
                V.tensor_tensor(w_lo[s][:, :, :], raw[(k + AHEAD) % RAW][:, :, :], w_hi[s][:, :, :].bitcast(F32),
                                ALU.subtract).then_inc(lo_ready, 1)

            def run(pair):
                for k in range(PAIRS):
                    lows(pair, k)

            def evacuate(done, pair_end, spill, natural=False):
                for b in (1, 3) if natural else range(4):
                    if not isinstance(spill, int) or spill > 0:
                        v.wait_ge(spilled[b], 16 * spill)
                    if b < 3:
                        v.wait_ge(acc_done, 3 * done + (b + 1))
                    else:
                        v.wait_ge(pair_done, pair_end)
                    if natural:
                        V.tensor_scalar(stage[b][:, :], acc[b][:, :], rstd[:, b:b + 1], None, ALU.mult).then_inc(acc_free[b], 1)
                    else:
                        V.tensor_tensor(stage[b][:, :], acc[b][:, :], roots[:, :], ALU.mult).then_inc(acc_free[b], 1)

            v.wait_ge(ident_ready, 2)
            norm_job(0, 0, 0, h_hi, h_lo, diag1)
            evacuate(0, PAIRS, 0)
            v.wait_ge(wg_hi_ready, 1)
            V.tensor_tensor(wg_hl[:, :, 1, 0:GN], wg[:, :, :], wg_hl[:, :, 0, 0:GN].bitcast(F32), ALU.subtract).then_inc(wg_lo_ready, 1)
            with v.Fori(1, T_JOBS) as j:
                run(j * PAIRS)
                evacuate(j, (j + 1) * PAIRS, j)
            for n in range(2):
                V.tensor_tensor(lprod[:, n:n + 1], cols[:, 40 + 2 * n:41 + 2 * n], cols[:, 41 + 2 * n:42 + 2 * n], ALU.mult)\
                    .then_inc(lprod_ready, 1)
            V.tensor_scalar(hg[:, :], cols[:, 32:40], 1.0 - LAM_INIT, None, ALU.mult).then_inc(hg_ready, 1)
            V.tensor_tensor(twice[:, :], ident[:, 0:NG * NC_], ident[:, NG * NC_:P], ALU.add).then_inc(twice_ready, 1)

            for n in range(4):
                w = min(512, ROW - 512 * n)
                v.wait_ge(brow_done, n + 1)
                V.tensor_scalar(brow[:, 512 * n:512 * n + w], bbanks[n][0:NH + DH, 0:w], HD ** 0.5, None, ALU.mult)\
                    .then_inc(brow_ready, 1)

            def blocks(s):
                emb = cols[:, 44 + CL * s:44 + CL * (s + 1)]
                for g in range(NG):
                    src = c_in[:, 2 * s + g, :].rearrange("p (c j) -> p j c", j=CS)
                    c0 = g * NC_
                    V.tensor_tensor(blk[:, s, 0:CS, c0:c0 + NC_], src, emb[:, 0:CS].unsqueeze(2).to_broadcast([P, CS, NC_]),
                                    ALU.add).then_inc(blk_ready, 1)
                    V.tensor_tensor(blk[:, s, CS:CL, c0:c0 + NC_ - 1], src[:, :, 1:NC_],
                                    emb[:, CS:CL].unsqueeze(2).to_broadcast([P, CS, NC_ - 1]), ALU.add).then_inc(blk_ready, 1)
                    V.tensor_copy(blk[:, s, CS:CL, c0 + NC_ - 1:c0 + NC_], emb[:, CS:CL].unsqueeze(2)).then_inc(blk_ready, 1)

            def block_lo(s):
                v.wait_ge(blk_hi_ready, s + 1)
                V.tensor_tensor(blk_hl[:, s, :, NG * NC_:P], blk[:, s, :, :], blk_hl[:, s, :, 0:NG * NC_].bitcast(F32),
                                ALU.subtract).then_inc(blk_lo_ready, 1)

            def first_blocks():
                v.wait_ge(c_landed, 16)
                v.wait_ge(gn_done, 1)
                blocks(0)

            def neg_lambda():
                v.wait_ge(lam_exp, 1)
                link(V.tensor_tensor(neglam[:, :], lexp[:, 1:2], lexp[:, 0:1], ALU.subtract))
                link(V.tensor_scalar(neglam[:, :], neglam[:, :], -LAM_INIT, None, ALU.add))

            def move_hidden(s):
                v.wait_ge(pair_done, C_END[s])
                V.tensor_copy(hid_hl[:, s, :], (e[2], ob)[s][:, 0:CH]).then_inc(hid_copied, 1)

            def move_vc():
                v.wait_ge(kvc_done, 2)
                V.tensor_copy(vc[:, :, :], e[2][0:NC_, 0:NG * HD].rearrange("p (g n) -> p g n", g=NG)).then_inc(kvc_ready, 1)

            for n in range(len(NAT)):
                lows(PAIR_N, n)
                if NAT[n] == ("N", 0, 3):
                    first_blocks()
                elif NAT[n] == ("N", 0, 7):
                    block_lo(0)
                elif NAT[n] == ("N", 1, 2):
                    neg_lambda()
                elif NAT[n] == ("N", 1, 3):
                    blocks(1)
                elif NAT[n] == ("N", 1, 5):
                    block_lo(1)
                elif NAT[n] == ("N", 2, 0):
                    move_hidden(0)
                elif NAT[n] == ("N", 2, 4):
                    move_hidden(1)
                elif NAT[n] == ("N", 2, 7):
                    move_vc()
                if NAT[n][0] == "N" and NAT[n][2] == PAIRS - 1:
                    evacuate(NAT[n][1] + JOB_N, PAIR_N + n + 1, NAT[n][1] + JOB_N, natural=True)
            v.wait_ge(kvc_ready, 2)
            v.wait_ge(gates_ready, NT)
            v.wait_ge(hg_ready, 1)

            with v.Fori(0, ITERS) as t:
                LINKS = 28
                count = [0]

                def then(ins):
                    count[0] += 1
                    ins.then_inc(chain, 1)
                    v.wait_ge(chain, LINKS * t + count[0])

                g = t // 2
                V.tensor_copy(kcur[:, :], kct[:, bass.ds(g * NC_, NC_)]).then_inc(cur_ready, 1)
                V.tensor_copy(vcur[:, :], vc[:, bass.ds(g, 1), :].rearrange("p g n -> p (g n)")).then_inc(cur_ready, 1)
                V.tensor_copy(gcur[:, :, :], gates[:, :, bass.ds(6 * t, 6)]).then_inc(cur_ready, 1)
                V.tensor_copy(hgcur[:, :], hg[:, bass.ds(2 * t, 2)]).then_inc(cur_ready, 1)
                v.wait_ge(cur_ready, 4 * t + 4)

                def softmax(u):
                    head = u // 2 if u < 4 else 2
                    if u == 0:
                        v.wait_ge(nsa_loaded, 16 * 7 * (t + 1))
                    if u == 4:
                        v.wait_ge(diff_loaded, 16 * 4 * (t + 1))
                    if u == 5:
                        v.wait_ge(p_exp, 24 * t + 20)
                    for i in ORDER:
                        b, c = SEG[i]
                        n = (i + 1) * P
                        v.wait_ge(scores_done, 18 * t + (3 * u + BANK_END[i])).then_inc(dve_waited, 1)
                        V.tensor_tensor_reduce(z[:, ZOFF[i]:ZOFF[i] + n], e[b][:, c:c + n], bias[:, head, S - n:S],
                                               -SCALE, 3.0e38, ALU.add, ALU.min, m[:, i:i + 1]).then_inc(z_ready, 1)
                    if u in (0, 2):
                        sc = e[1][:, CSEG:CSEG + NT * NC_].rearrange("p (i c) -> p i c", i=NT)
                        then(V.tensor_reduce(cm[:, :], sc, AX.X, ALU.max))
                        then(V.tensor_scalar(cr[:, :], cm[:, :], -FLOOR, None, ALU.max))
                        V.tensor_tensor(zc[:, :, :], sc, cr[:, :].unsqueeze(2).to_broadcast([P, NT, NC_]), ALU.subtract)\
                            .then_inc(zc_ready, 1)
                    v.wait_ge(p_exp, 24 * t + 4 * (u + 1))
                    if u < 4:
                        then(V.reciprocal(r1[:, :], l1[:, :]))
                        then(V.tensor_tensor(r2[:, :], r1[:, :], gcur[:, :, 3 * head + 1 + u % 2], ALU.mult))
                        for i in range(NT):
                            s = slice(ZOFF[i], ZOFF[i] + (i + 1) * P)
                            V.tensor_scalar(p_a[:, s], p_a[:, s], r2[:, i:i + 1], None, ALU.mult).then_inc(p_scaled, 1)
                    elif u == 5:
                        then(V.reciprocal(r1[:, :], l1[:, :]))
                        then(V.reciprocal(cr[:, :], l2[:, :]))
                        then(V.tensor_scalar(r2[:, :], cr[:, :], neglam[:, 0:1], None, ALU.mult))
                        for i in range(NT):
                            s = slice(ZOFF[i], ZOFF[i] + (i + 1) * P)
                            then(V.tensor_scalar(p_a[:, s], p_a[:, s], r1[:, i:i + 1], None, ALU.mult))
                        for i in range(NT):
                            s = slice(ZOFF[i], ZOFF[i] + (i + 1) * P)
                            V.scalar_tensor_tensor(out=p_b[:, s], in0=p_b[:, s], scalar=r2[:, i:i + 1], in1=p_a[:, s],
                                                   op0=ALU.mult, op1=ALU.add).then_inc(p_scaled, 1)
                    if u in (0, 2):
                        v.wait_ge(pc_exp, 2 * t + (1 + u // 2))
                        then(V.tensor_reduce(cl[:, :], pc[:, :, :], AX.X, ALU.add))
                        then(V.tensor_scalar(cm[:, :], cl[:, :], 1e-30, None, ALU.max))
                        then(V.reciprocal(cr[:, :], cm[:, :]))
                        then(V.tensor_tensor(cl[:, :], cr[:, :], gcur[:, :, 3 * head], ALU.mult))
                        V.tensor_tensor(pc[:, :, :], pc[:, :, :], cl[:, :].unsqueeze(2).to_broadcast([P, NT, NC_]), ALU.mult)\
                            .then_inc(pc_scaled, 1)

                def move_pt(u):
                    v.wait_ge(pt_done, 17 * t + (U_PT[u] + 1))
                    V.tensor_copy(pt[:, 0:512], e[0][:, :]).then_inc(pt_ready, 1)
                    v.wait_ge(pt_done, 17 * t + (U_PT[u] + 3))
                    V.tensor_copy(pt[:, 1024:1280], e[2][:, 0:256]).then_inc(pt_ready, 1)

                def outputs(u):
                    if u in (1, 3):
                        v.wait_ge(o_hi_ready, 4 * t + (1 + u // 2))
                        V.tensor_tensor(s_lo[u // 2][:, :], ob[:, :], s_hi[u // 2][:, :].bitcast(F32), ALU.subtract)\
                            .then_inc(o_lo_ready, 1)
                    if u == 4:
                        v.wait_ge(pv_done, 5 * t + 5)
                        for n, o in enumerate((ob, e[0])):
                            V.tensor_copy(on[:, 2 * n:2 * n + 2, :], o[:, :].rearrange("p (i n) -> p i n", i=2)).then_inc(on_ready, 1)
                        v.wait_ge(on_sq, 4 * t + 4)
                        then(V.tensor_scalar(inv[:, :], ss[:, :], 1.0 / DV, EPS, ALU.mult, ALU.add))
                        V.reciprocal(ms[:, :], inv[:, :]).then_inc(on_ms, 1)
                        v.wait_ge(on_rstd, t + 1)
                        V.tensor_tensor(on[:, :, :], on[:, :, :], rstd[:, :].unsqueeze(2).to_broadcast([P, NT, DV]), ALU.mult)\
                            .then_inc(on_scaled, 1)

                def turned_o(_):
                    for h in range(2):
                        v.wait_ge(o_hi_ready, 4 * t + (3 + h))
                        V.scalar_tensor_tensor(out=s_lo[2 + h][:, :], in0=e[1 + h][:, :], scalar=hgcur[:, h:h + 1],
                                               in1=s_hi[2 + h][:, :].bitcast(F32), op0=ALU.mult, op1=ALU.subtract)\
                            .then_inc(o_lo_ready, 1)

                for n in range(2):
                    for k in range(PAIRS):
                        lows(t * (2 * PAIRS) + (PAIR_G + n * PAIRS), k)
                        for i in range(2):
                            for kind, u in AT.get(16 * n + 2 * k + i, ()):
                                {"S": softmax, "T": move_pt, "V": outputs, "O": turned_o}[kind](u)
                    evacuate(2 * t + (JOB_G + n), t * (2 * PAIRS) + (PAIR_G + (n + 1) * PAIRS), 2 * t + (T_JOBS + N_JOBS + n))
                for k in range(4):
                    v.wait_ge(o_spilled[k], 32 * (t + 1))
                assert count[0] == LINKS

            with v.Fori(0, NT) as c:
                done = 2 * c + JOB_UP
                first = c * PAIRS + PAIR_UP
                for n in range(2):
                    for k in range(4 * n, 4 * n + 4):
                        lows(first, k)
                    for b in range(4):
                        if b < 3:
                            v.wait_ge(acc_done, 3 * done + (3 * n + b + 1))
                        else:
                            v.wait_ge(pair_done, first + 4 * (n + 1))
                        if b == 0:
                            v.wait_ge(sig_ready, 2 * c + (n + 1))
                        t = (ga, gb)[n]
                        V.tensor_tensor(t[:, b, :], acc[b][:, :], t[:, b, :], ALU.mult).then_inc(acc_free[b], 1)
                for b in range(4):
                    v.wait_ge(acc_free[b], 2 * c + (JOB_UP + 2))
                    V.tensor_tensor(gb[:, b, :], ga[:, b, :], gb[:, b, :], ALU.add).then_inc(mix_sum, 1)
                for b in range(4):
                    v.wait_ge(mix_hi, 4 * c + (b + 1))
                    V.tensor_tensor(m_lo[:, bass.ds(4 * c + b, 1), :], gb[:, b:b + 1, :],
                                    m_hi[:, bass.ds(4 * c + b, 1), :].bitcast(F32), ALU.subtract).then_inc(mix_lo, 1)

            def add_block(c):
                for b in range(4):
                    if b < 3:
                        v.wait_ge(acc_done, 3 * c + (3 * JOB_OUT + b + 1))
                    else:
                        v.wait_ge(pair_done, (c + 1) * PAIRS + PAIR_OUT)
                    if b == 0:
                        v.wait_ge(res_landed, 16 * NT)
                    r = res[:, b, bass.ds(c * COLS, COLS)]
                    V.tensor_tensor(r, acc[b][:, :], r, ALU.add).then_inc(acc_free[b], 1)

            with v.Fori(0, NT - 1) as c:
                run(c * PAIRS + PAIR_OUT)
                add_block(c)
            for k in range(PAIRS):
                lows((NT - 1) * PAIRS + PAIR_OUT, k)
                if k >= PAIRS - 2:
                    v.wait_ge(pair_done, PAIR_FF - PAIRS + 1)
                    norm_lo(1, (k - (PAIRS - 2),), 16, h2_hi, h2_lo)
            add_block(NT - 1)

            def f_low(b, c):
                v.wait_ge(f_hi_ready, 4 * c + (b + 1))
                V.tensor_tensor(f_lo[:, b, :], silu[:, b, :], f_hi[:, b, :].bitcast(F32), ALU.subtract).then_inc(f_lo_ready, 1)

            def take_a(done, pair_end):
                for b in range(4):
                    if b < 3:
                        v.wait_ge(acc_done, 3 * done + (b + 1))
                    else:
                        v.wait_ge(pair_done, pair_end)
                    V.tensor_tensor(silu[:, b, :], acc[b][:, :], roots[:, :], ALU.mult).then_inc(acc_free[b], 1)

            def run_b(first, c):
                for k in range(PAIRS):
                    if k == 2:
                        for b in range(4):
                            v.wait_ge(silu_ready, 4 * c + (b + 1))
                            V.tensor_tensor(silu[:, b, :], silu[:, b, :], roots[:, :], ALU.mult).then_inc(silu_rooted, 1)
                    if not isinstance(first, int) or k + AHEAD < PAIRS:
                        lows(first, k)

            def take_b(done, pair_end, c):
                for b in range(4):
                    if b < 3:
                        v.wait_ge(acc_done, 3 * done + (b + 1))
                    else:
                        v.wait_ge(pair_done, pair_end)
                    v.wait_ge(silu_rooted, 4 * c + (b + 1))
                    V.tensor_tensor(silu[:, b, :], acc[b][:, :], silu[:, b, :], ALU.mult).then_inc(acc_free[b], 1)
                    if b > 0:
                        f_low(b - 1, c)
                f_low(3, c)

            def add_out(done, pair_end, n):
                for b in range(4):
                    if b < 3:
                        v.wait_ge(acc_done, 3 * done + (b + 1))
                    else:
                        v.wait_ge(pair_done, pair_end)
                    r = res[:, b, n * COLS:(n + 1) * COLS]
                    V.tensor_tensor(r, acc[b][:, :], r, ALU.add).then_inc(acc_free[b], 1)

            def outs(first, done):
                for n in range(NT):
                    for k in range(2):
                        yield 2 * n + k
                    add_out(done + n, first + 2 * (n + 1), n)

            norm_job(PAIR_FF, 1, 16, h2_hi, h2_lo, diag2)
            take_a(JOB_FF, PAIR_FF + PAIRS)
            with v.Fori(0, CHUNKS - 1) as c:
                p0 = c * FF_PAIRS + PAIR_FF
                run_b(p0 + PAIRS, c)
                take_b(c * FF_JOBS + (JOB_FF + 1), p0 + 2 * PAIRS, c)
                run(p0 + 2 * PAIRS)
                take_a(c * FF_JOBS + (JOB_FF + 2), p0 + 3 * PAIRS)
                for k in outs(p0 + 3 * PAIRS, c * FF_JOBS + (JOB_FF + 3)):
                    lows(p0 + 3 * PAIRS, k)
            last = JOB_FF + (CHUNKS - 1) * FF_JOBS
            run_b(PAIR_END - 2 * PAIRS, CHUNKS - 1)

            def last_los(ks):
                for k in ks:
                    v.wait_ge(hi_ready, PAIR_END - PAIRS + k + 1)
                    V.tensor_tensor(last_w(1, k), raw[k % RAW][:, :, :], last_w(0, k).bitcast(F32), ALU.subtract).then_inc(lo_ready, 1)

            last_los(range(4))
            take_b(last + 1, PAIR_END - PAIRS, CHUNKS - 1)
            last_los(range(4, PAIRS))

            v.wait_ge(fg_landed, 16)
            squares = 2 * NT * NT
            for i in range(NT):
                def weigh(n):
                    v.wait_ge(sq_ready, squares + NT * i + n + 1)
                    r = res[:, i, n * COLS:(n + 1) * COLS]
                    V.tensor_tensor(r, r, fg[:, n * COLS:(n + 1) * COLS], ALU.mult).then_inc(weighted, 1)

                for n in range(NT):
                    v.wait_ge(tail_done, NT * i + n + 1)
                    r = res[:, i, n * COLS:(n + 1) * COLS]
                    V.tensor_tensor(r, acc[n][:, :], r, ALU.add).then_inc(acc_free[n], 1)
                    if n > 0:
                        weigh(n - 1)
                v.wait_ge(sq_ready, squares + NT * (i + 1))
                link(V.tensor_reduce(ss[:, i:i + 1], ssp[:, i, :], AX.X, ALU.add))
                link(V.tensor_scalar(inv[:, i:i + 1], ss[:, i:i + 1], 1.0 / DM, EPS, ALU.mult, ALU.add))
                V.reciprocal(ms[:, i:i + 1], inv[:, i:i + 1]).then_inc(ms_ready, 1)
                weigh(3)
                v.wait_ge(rstd_ready, i + 3)
                v.wait_ge(weighted, NT * (i + 1))
                V.tensor_scalar(res[:, i, 0:DM // 2], res[:, i, 0:DM // 2], rstd[:, i:i + 1], None, ALU.mult).then_inc(fin_v_ready, 1)


def kernel(**inputs):
    import concourse.bacc as bacc
    from concourse.bass_utils import run_bass_kernel_spmd

    a = {k: np.ascontiguousarray(v) for k, v in inputs.items()}
    w = a["w_in"][0]
    widths = [1024, 256, 256, 256, 256, 256, 256, 24, 1024, 1024, 1024, 4096]
    q_n, kc, vc, ksl, vsl, kw, vw, g_n, q_d, k_d, v_d, g_m = np.split(w, np.cumsum(widths)[:-1], axis=1)
    arrays = {
        "x": a["x"][0],
        "w_proj": np.concatenate([q_n, kc, vc, ksl, kw, q_d, k_d, g_m, vsl, vw, v_d, g_n], axis=1),
        "vectors": np.concatenate([a[n].reshape(-1, P) for n in (
            "norm_mix_g", "norm_ff_g", "diff_head_g", "diff_lq1", "diff_lk1", "diff_lq2", "diff_lk2", "cmp_pe_k", "cmp_pe_v")]),
        "cw1": np.concatenate([a["cmp_w1_k"], a["cmp_w1_v"]], axis=0),
        "cw2": np.concatenate([a["cmp_w2_k"], a["cmp_w2_v"]], axis=0),
        "final_g": a["norm_final_g"],
        "w_up": np.concatenate([a["w_up_nsa"][0], a["w_up_diff"][0]], axis=0),
        "w_out": a["w_out"][0], "w_ff_in": a["w_ff_in"][0], "w_ff_out": a["w_ff_out"][0],
        "table": a["rel_bias_table"], "onehot": bucket_onehot(),
    }
    nc = bacc.Bacc("TRN2", target_bir_lowering=False, num_devices=1)
    args = {}
    feed = {}
    for name, v in arrays.items():
        v = np.ascontiguousarray(v)
        feed[f"in_{name}"] = v
        args[name] = nc.dram_tensor(f"in_{name}", v.shape, mybir.dt.from_np(v.dtype), kind="ExternalInput").ap()
    out = nc.dram_tensor("out_0", (S, DM), F32, kind="ExternalOutput").ap()
    build(nc, **args, out=out)
    r = run_bass_kernel_spmd(nc, [feed], core_ids=[0])
    return r.results[0]["out_0"].reshape(1, S, DM)
```
